# Optimizing a Trainium2 kernel written in Bass

```python
import jax, jax.numpy as jnp
from jax import lax
import numpy as np
import math

D_MODEL = 1024
BATCH = 1
SEQ = 256
DEPTH = 2

GRID_W = 64
CTX_LEN = 256
N_MIXERS = 3
Q_BLOCK = 128
ROPE_THETA = 10000.0
NORM_EPS = 1e-6
N_MOD = 6
MLA_HEADS = 8
MLA_Q_LORA = 512
MLA_KV_LORA = 256
MLA_NOPE = 128
MLA_ROPE = 64
MLA_V = 128
CONV_WIDTH = 3
CONV_DIM = D_MODEL
GQA_HEADS = 16
GQA_KV_HEADS = 8
GQA_HEAD_DIM = 128
MOE_GROUPS = 4
MOE_EXPERTS_PER_GROUP = 8
MOE_EXPERTS = MOE_GROUPS * MOE_EXPERTS_PER_GROUP
MOE_TOP_K = 2
MOE_FF = 512
MOE_BLOCK = 128


def _n_layers_of(kind):
    return len(range(kind, DEPTH, N_MIXERS))

def _rmsnorm(x, g):
    xf = x.astype(jnp.float32)
    y = xf * lax.rsqrt(jnp.mean(xf * xf, axis=-1, keepdims=True) + NORM_EPS)
    return (y * g.astype(jnp.float32)).astype(x.dtype)

def _modulate(x, g, shift, scale):
    return _rmsnorm(x, g) * (1 + scale) + shift

def _rope_1d(x, pos):
    half = x.shape[-1] // 2
    inv_freq = ROPE_THETA ** (-jnp.arange(half, dtype=jnp.float32) / half)
    ang = pos.astype(jnp.float32)[:, None] * inv_freq[None, :]
    cos, sin = jnp.cos(ang)[:, None, :], jnp.sin(ang)[:, None, :]
    xf = x.astype(jnp.float32)
    x1, x2 = xf[..., :half], xf[..., half:]
    return jnp.concatenate([x1 * cos - x2 * sin, x1 * sin + x2 * cos], axis=-1).astype(x.dtype)

def _axial_rope(x, rows, cols):
    half = x.shape[-1] // 2
    return jnp.concatenate([_rope_1d(x[..., :half], rows), _rope_1d(x[..., half:], cols)], axis=-1)

def _attend(q, k, v, scale):
    B, n, H, dk = q.shape
    Hk, dv = k.shape[2], v.shape[-1]
    G = H // Hk
    nb = n // Q_BLOCK
    qb = q.reshape(B, nb, Q_BLOCK, Hk, G, dk).transpose(1, 0, 2, 3, 4, 5)

    def block(qblk):
        s = jnp.einsum("bqhgd,bkhd->bhgqk", qblk, k).astype(jnp.float32) * scale
        p = jax.nn.softmax(s, axis=-1).astype(v.dtype)
        return jnp.einsum("bhgqk,bkhd->bqhgd", p, v)

    o = lax.map(block, qb)
    return o.transpose(1, 0, 2, 3, 4, 5).reshape(B, n, H * dv)

def _mla_project(a, w_dq, g_q, w_uq, w_dkv, g_kv, w_ukv, pos, want_q):
    B, n, _ = a.shape
    ckv = a @ w_dkv
    c_kv = _rmsnorm(ckv[..., :MLA_KV_LORA], g_kv)
    k_pe = ckv[..., MLA_KV_LORA:][:, :, None, :]
    kv = (c_kv @ w_ukv).reshape(B, n, MLA_HEADS, MLA_NOPE + MLA_V)
    k_nope, v = kv[..., :MLA_NOPE], kv[..., MLA_NOPE:]
    if pos is not None:
        k_pe = _axial_rope(k_pe, *pos)
    k = jnp.concatenate([k_nope, jnp.broadcast_to(k_pe, (B, n, MLA_HEADS, MLA_ROPE))], axis=-1)
    q = None
    if want_q:
        cq = _rmsnorm(a @ w_dq, g_q)
        q = (cq @ w_uq).reshape(B, n, MLA_HEADS, MLA_NOPE + MLA_ROPE)
        if pos is not None:
            q = jnp.concatenate([q[..., :MLA_NOPE], _axial_rope(q[..., MLA_NOPE:], *pos)], axis=-1)
    return q, k, v

def _mla(a_lat, a_ctx, pos, ctx_out, w_dq, g_q, w_uq, w_dkv, g_kv, w_ukv, w_o):
    scale = (MLA_NOPE + MLA_ROPE) ** -0.5
    q_l, k_l, v_l = _mla_project(a_lat, w_dq, g_q, w_uq, w_dkv, g_kv, w_ukv, pos, True)
    q_c, k_c, v_c = _mla_project(a_ctx, w_dq, g_q, w_uq, w_dkv, g_kv, w_ukv, None, ctx_out)
    k_all = jnp.concatenate([k_c, k_l], axis=1)
    v_all = jnp.concatenate([v_c, v_l], axis=1)
    y_lat = _attend(q_l, k_all, v_all, scale) @ w_o
    y_ctx = _attend(q_c, k_c, v_c, scale) @ w_o if ctx_out else None
    return y_lat, y_ctx

def _short_conv_seq(a, w_in, conv_w, w_out):
    bcu = a @ w_in
    b_gate, c_gate, u = jnp.split(bcu, 3, axis=-1)
    z = lax.conv_general_dilated(
        c_gate * u, conv_w[:, None, :], window_strides=(1,),
        padding=[((CONV_WIDTH - 1) // 2, (CONV_WIDTH - 1) // 2)],
        dimension_numbers=("NWC", "WIO", "NWC"), feature_group_count=CONV_DIM)
    return (b_gate * z) @ w_out

def _short_conv(a_lat, a_ctx, ctx_out, w_in, conv_w, w_out):
    y_lat = _short_conv_seq(a_lat, w_in, conv_w, w_out)
    y_ctx = _short_conv_seq(a_ctx, w_in, conv_w, w_out) if ctx_out else None
    return y_lat, y_ctx

def _gqa_project(a, w_qkv, q_g, k_g, pos, want_q):
    B, n, _ = a.shape
    dq = GQA_HEADS * GQA_HEAD_DIM
    dkv = GQA_KV_HEADS * GQA_HEAD_DIM
    kv = a @ w_qkv[:, dq:]
    k = _rmsnorm(kv[..., :dkv].reshape(B, n, GQA_KV_HEADS, GQA_HEAD_DIM), k_g)
    v = kv[..., dkv:].reshape(B, n, GQA_KV_HEADS, GQA_HEAD_DIM)
    if pos is not None:
        k = _axial_rope(k, *pos)
    q = None
    if want_q:
        q = _rmsnorm((a @ w_qkv[:, :dq]).reshape(B, n, GQA_HEADS, GQA_HEAD_DIM), q_g)
        if pos is not None:
            q = _axial_rope(q, *pos)
    return q, k, v

def _gqa(a_lat, a_ctx, pos, ctx_out, w_qkv, q_g, k_g, w_o):
    scale = GQA_HEAD_DIM ** -0.5
    q_l, k_l, v_l = _gqa_project(a_lat, w_qkv, q_g, k_g, pos, True)
    q_c, k_c, v_c = _gqa_project(a_ctx, w_qkv, q_g, k_g, None, ctx_out)
    k_all = jnp.concatenate([k_c, k_l], axis=1)
    v_all = jnp.concatenate([v_c, v_l], axis=1)
    y_lat = _attend(q_l, k_all, v_all, scale) @ w_o
    y_ctx = _attend(q_c, k_c, v_c, scale) @ w_o if ctx_out else None
    return y_lat, y_ctx

def _hier_moe(h, w_group, b_group, w_expert, b_expert, w_gate, w_up, w_down):
    T, D = h.shape
    hf = h.astype(jnp.float32)
    g_prob = jax.nn.softmax(hf @ w_group.astype(jnp.float32), axis=-1)
    g_sel = jnp.argmax(g_prob + b_group.astype(jnp.float32), axis=-1)
    g_w = jnp.take_along_axis(g_prob, g_sel[:, None], axis=-1)
    e_logits = (hf @ w_expert.astype(jnp.float32)).reshape(T, MOE_GROUPS, MOE_EXPERTS_PER_GROUP)
    e_prob = jax.nn.softmax(jnp.take_along_axis(e_logits, g_sel[:, None, None], axis=1)[:, 0], axis=-1)
    e_bias = b_expert.astype(jnp.float32).reshape(MOE_GROUPS, MOE_EXPERTS_PER_GROUP)[g_sel]
    _, top_idx = lax.top_k(e_prob + e_bias, MOE_TOP_K)
    top_w = jnp.take_along_axis(e_prob, top_idx, axis=-1)
    top_w = top_w / jnp.sum(top_w, axis=-1, keepdims=True) * g_w
    expert_id = g_sel[:, None] * MOE_EXPERTS_PER_GROUP + top_idx

    A = T * MOE_TOP_K
    eid = expert_id.reshape(A)
    tok = jnp.arange(A, dtype=jnp.int32) // MOE_TOP_K
    wts = top_w.reshape(A)
    order = jnp.argsort(eid)
    e_s, tok_s, w_s = eid[order], tok[order], wts[order]
    counts = jnp.bincount(eid, length=MOE_EXPERTS)
    starts = jnp.cumsum(counts) - counts
    padded = (counts + MOE_BLOCK - 1) // MOE_BLOCK * MOE_BLOCK
    pends = jnp.cumsum(padded)
    pstarts = pends - padded
    dest = pstarts[e_s] + (jnp.arange(A, dtype=jnp.int32) - starts[e_s])
    nb = -(-A // MOE_BLOCK) + MOE_EXPERTS
    xp = jnp.zeros((nb * MOE_BLOCK, D), h.dtype).at[dest].set(h[tok_s])
    blk_e = jnp.clip(jnp.searchsorted(pends, jnp.arange(nb, dtype=jnp.int32) * MOE_BLOCK, side="right"),
                     0, MOE_EXPERTS - 1)

    def expert_block(args):
        xb, e = args
        return (jax.nn.silu(xb @ w_gate[e]) * (xb @ w_up[e])) @ w_down[e]

    yp = lax.map(expert_block, (xp.reshape(nb, MOE_BLOCK, D), blk_e)).reshape(nb * MOE_BLOCK, D)
    return jax.ops.segment_sum(yp[dest] * w_s[:, None].astype(h.dtype), tok_s, num_segments=T)

def _normal(k, shape, scale):
    return jax.random.normal(k, shape, jnp.float32) * scale

def first_inputs(seed: int = 0) -> dict:
    key = jax.random.key(seed)
    ks = iter(jax.random.split(key, 40))
    D = D_MODEL
    nA, nB, nC = _n_layers_of(0), _n_layers_of(1), _n_layers_of(2)
    dq = GQA_HEADS * GQA_HEAD_DIM
    dkv = GQA_KV_HEADS * GQA_HEAD_DIM
    return {
        "x": _normal(next(ks), (BATCH, SEQ, D), 1.0),
        "c": _normal(next(ks), (BATCH, D), 1.0),
        "ctx": _normal(next(ks), (BATCH, CTX_LEN, D), 1.0),
        "c_ctx": _normal(next(ks), (D,), 1.0),
        "w_mod": _normal(next(ks), (DEPTH, D, N_MOD * D), 0.5 * D ** -0.5),
        "b_mod": _normal(next(ks), (DEPTH, N_MOD * D), 0.02),
        "norm_mix_g": 1.0 + _normal(next(ks), (DEPTH, D), 0.05),
        "norm_ffn_g": 1.0 + _normal(next(ks), (DEPTH, D), 0.05),
        "mla_w_dq": _normal(next(ks), (nA, D, MLA_Q_LORA), D ** -0.5),
        "mla_g_q": 1.0 + _normal(next(ks), (nA, MLA_Q_LORA), 0.05),
        "mla_w_uq": _normal(next(ks), (nA, MLA_Q_LORA, MLA_HEADS * (MLA_NOPE + MLA_ROPE)), MLA_Q_LORA ** -0.5),
        "mla_w_dkv": _normal(next(ks), (nA, D, MLA_KV_LORA + MLA_ROPE), D ** -0.5),
        "mla_g_kv": 1.0 + _normal(next(ks), (nA, MLA_KV_LORA), 0.05),
        "mla_w_ukv": _normal(next(ks), (nA, MLA_KV_LORA, MLA_HEADS * (MLA_NOPE + MLA_V)), MLA_KV_LORA ** -0.5),
        "mla_w_o": _normal(next(ks), (nA, MLA_HEADS * MLA_V, D), (MLA_HEADS * MLA_V) ** -0.5),
        "conv_w_in": _normal(next(ks), (nB, D, 3 * CONV_DIM), D ** -0.5),
        "conv_w": _normal(next(ks), (nB, CONV_WIDTH, CONV_DIM), CONV_WIDTH ** -0.5),
        "conv_w_out": _normal(next(ks), (nB, CONV_DIM, D), CONV_DIM ** -0.5),
        "gqa_w_qkv": _normal(next(ks), (nC, D, dq + 2 * dkv), D ** -0.5),
        "gqa_q_norm_g": 1.0 + _normal(next(ks), (nC, GQA_HEAD_DIM), 0.05),
        "gqa_k_norm_g": 1.0 + _normal(next(ks), (nC, GQA_HEAD_DIM), 0.05),
        "gqa_w_o": _normal(next(ks), (nC, dq, D), dq ** -0.5),
        "moe_w_group": _normal(next(ks), (DEPTH, D, MOE_GROUPS), D ** -0.5),
        "moe_b_group": _normal(next(ks), (DEPTH, MOE_GROUPS), 0.01),
        "moe_w_expert": _normal(next(ks), (DEPTH, D, MOE_EXPERTS), D ** -0.5),
        "moe_b_expert": _normal(next(ks), (DEPTH, MOE_EXPERTS), 0.01),
        "moe_w_gate": _normal(next(ks), (DEPTH, MOE_EXPERTS, D, MOE_FF), D ** -0.5),
        "moe_w_up": _normal(next(ks), (DEPTH, MOE_EXPERTS, D, MOE_FF), D ** -0.5),
        "moe_w_down": _normal(next(ks), (DEPTH, MOE_EXPERTS, MOE_FF, D), MOE_FF ** -0.5),
        "final_norm_g": 1.0 + _normal(next(ks), (D,), 0.05),
    }

def first_block(x, c, ctx, c_ctx, w_mod, b_mod, norm_mix_g, norm_ffn_g,
              mla_w_dq, mla_g_q, mla_w_uq, mla_w_dkv, mla_g_kv, mla_w_ukv, mla_w_o,
              conv_w_in, conv_w, conv_w_out,
              gqa_w_qkv, gqa_q_norm_g, gqa_k_norm_g, gqa_w_o,
              moe_w_group, moe_b_group, moe_w_expert, moe_b_expert, moe_w_gate, moe_w_up, moe_w_down,
              final_norm_g):
    B, S, D = x.shape
    L = ctx.shape[1]
    ROWS = S // GRID_W
    rows = jnp.repeat(jnp.arange(ROWS, dtype=jnp.int32), GRID_W)
    cols = jnp.tile(jnp.arange(GRID_W, dtype=jnp.int32), ROWS)
    pos = (rows, cols)
    cond_lat = jax.nn.silu(c)
    cond_ctx = jax.nn.silu(c_ctx)[None]
    h = ctx
    for i in range(DEPTH):
        kind, j = i % N_MIXERS, i // N_MIXERS
        ctx_out = i < DEPTH - 1
        mod_l = (cond_lat @ w_mod[i] + b_mod[i])[:, None, :]
        mod_c = (cond_ctx @ w_mod[i] + b_mod[i])[:, None, :]
        sh1, sc1, g1, sh2, sc2, g2 = jnp.split(mod_l, N_MOD, axis=-1)
        csh1, csc1, cg1, csh2, csc2, cg2 = jnp.split(mod_c, N_MOD, axis=-1)
        a_lat = _modulate(x, norm_mix_g[i], sh1, sc1)
        a_ctx = _modulate(h, norm_mix_g[i], csh1, csc1)
        if kind == 0:
            y_lat, y_ctx = _mla(a_lat, a_ctx, pos, ctx_out, mla_w_dq[j], mla_g_q[j], mla_w_uq[j],
                                mla_w_dkv[j], mla_g_kv[j], mla_w_ukv[j], mla_w_o[j])
        elif kind == 1:
            y_lat, y_ctx = _short_conv(a_lat, a_ctx, ctx_out, conv_w_in[j], conv_w[j], conv_w_out[j])
        else:
            y_lat, y_ctx = _gqa(a_lat, a_ctx, pos, ctx_out, gqa_w_qkv[j], gqa_q_norm_g[j],
                                gqa_k_norm_g[j], gqa_w_o[j])
        x = x + g1 * y_lat
        f_lat = _modulate(x, norm_ffn_g[i], sh2, sc2)
        moe_args = (moe_w_group[i], moe_b_group[i], moe_w_expert[i], moe_b_expert[i],
                    moe_w_gate[i], moe_w_up[i], moe_w_down[i])
        if ctx_out:
            h = h + cg1 * y_ctx
            f_ctx = _modulate(h, norm_ffn_g[i], csh2, csc2)
            tokens = jnp.concatenate([f_lat.reshape(B * S, D), f_ctx.reshape(B * L, D)], axis=0)
            y = _hier_moe(tokens, *moe_args)
            x = x + g2 * y[:B * S].reshape(B, S, D)
            h = h + cg2 * y[B * S:].reshape(B, L, D)
        else:
            y = _hier_moe(f_lat.reshape(B * S, D), *moe_args)
            x = x + g2 * y.reshape(B, S, D)
    return _rmsnorm(x, final_norm_g)


HEAD_DIM = 64
ATTN_Q_HEADS = D_MODEL // (2 * HEAD_DIM)
ATTN_KV_HEADS = max(1, ATTN_Q_HEADS // 4)
RET_HEADS = D_MODEL // (2 * HEAD_DIM)
ATTN_WIDTH = ATTN_Q_HEADS * HEAD_DIM
KV_WIDTH = ATTN_KV_HEADS * HEAD_DIM
RET_WIDTH = RET_HEADS * HEAD_DIM
MIX_WIDTH = ATTN_WIDTH + RET_WIDTH
IN_SPLITS = (ATTN_WIDTH,
             ATTN_WIDTH + KV_WIDTH,
             ATTN_WIDTH + 2 * KV_WIDTH,
             ATTN_WIDTH + 2 * KV_WIDTH + RET_WIDTH,
             ATTN_WIDTH + 2 * KV_WIDTH + 2 * RET_WIDTH,
             ATTN_WIDTH + 2 * KV_WIDTH + 3 * RET_WIDTH)
IN_WIDTH = ATTN_WIDTH + 2 * KV_WIDTH + 4 * RET_WIDTH
WINDOW = 128
ATTN_BLOCK = 128
RET_CHUNK = 128
RET_THETA = 10000.0
D_FF = ((8 * D_MODEL // 3 + 127) // 128) * 128
LN_EPS = 1e-5
GN_EPS = 1e-6
DEEPNORM_ALPHA = (2 * DEPTH) ** 0.25
DEEPNORM_BETA = (8 * DEPTH) ** -0.25


def layer_norm(x, g, b):
    xf = x.astype(jnp.float32)
    mu = jnp.mean(xf, axis=-1, keepdims=True)
    var = jnp.mean(jnp.square(xf - mu), axis=-1, keepdims=True)
    return ((xf - mu) * lax.rsqrt(var + LN_EPS)).astype(x.dtype) * g + b

def swiglu_ffn(x, w_gu, w_down):
    a, u = jnp.split(x @ w_gu, 2, axis=-1)
    return (jax.nn.silu(a) * u) @ w_down

def rope_tables(seq):
    pos = jnp.arange(seq, dtype=jnp.float32)
    inv_freq = ROPE_THETA ** (-jnp.arange(0, HEAD_DIM, 2, dtype=jnp.float32) / HEAD_DIM)
    ang = pos[:, None] * inv_freq[None, :]
    return jnp.cos(ang), jnp.sin(ang)

def retention_rotation_tables(seq):
    pos = jnp.arange(seq, dtype=jnp.float32)
    ang_freq = 1.0 / (RET_THETA ** jnp.linspace(0.0, 1.0, HEAD_DIM // 2, dtype=jnp.float32))
    ang = pos[:, None] * ang_freq[None, :]
    return jnp.cos(ang), jnp.sin(ang)

def apply_rope(x, cos, sin):
    c = cos[:, None, :].astype(x.dtype)
    s = sin[:, None, :].astype(x.dtype)
    x1, x2 = jnp.split(x, 2, axis=-1)
    return jnp.concatenate([x1 * c - x2 * s, x2 * c + x1 * s], axis=-1)

def apply_pair_rotation(x, cos, sin):
    c = cos[:, None, :].astype(x.dtype)
    s = sin[:, None, :].astype(x.dtype)
    xe = x[..., 0::2]
    xo = x[..., 1::2]
    return jnp.stack([xe * c - xo * s, xo * c + xe * s], axis=-1).reshape(x.shape)

def sliding_window_sink_attention(q, k, v, sinks):
    B, S, Hq, D = q.shape
    Hkv = k.shape[2]
    G = Hq // Hkv
    C = ATTN_BLOCK
    N = S // C
    qb = (q * (HEAD_DIM ** -0.5)).reshape(B, N, C, Hkv, G, D)

    def with_prev_block(t):
        tb = t.reshape(B, N, C, Hkv, D)
        prev = jnp.pad(tb, ((0, 0), (1, 0), (0, 0), (0, 0), (0, 0)))[:, :-1]
        return jnp.concatenate([prev, tb], axis=2)

    kk = with_prev_block(k)
    vv = with_prev_block(v)
    s = jnp.einsum('bnqhgd,bnkhd->bnhgqk', qb, kk).astype(jnp.float32)
    q_idx = jnp.arange(C)[:, None]
    k_rel = jnp.arange(2 * C)[None, :] - C
    rel = q_idx - k_rel
    band = (rel >= 0) & (rel < WINDOW)
    valid = (jnp.arange(N)[:, None] * C + k_rel) >= 0
    mask = band[None, :, :] & valid[:, None, :]
    s = jnp.where(mask[None, :, None, None, :, :], s, -jnp.inf)
    sink = sinks.astype(jnp.float32).reshape(Hkv, G)[None, None, :, :, None, None]
    m = jnp.maximum(jnp.max(s, axis=-1, keepdims=True), sink)
    p = jnp.exp(s - m)
    denom = jnp.sum(p, axis=-1, keepdims=True) + jnp.exp(sink - m)
    o = jnp.einsum('bnhgqk,bnkhd->bnqhgd', (p / denom).astype(v.dtype), vv)
    return o.reshape(B, S, Hq * D)

def multiscale_retention(q, k, v, gate):
    B, S, H, D = q.shape
    C = RET_CHUNK
    N = S // C
    log_gamma = jnp.log1p(-jnp.exp2(-5.0 - jnp.arange(H, dtype=jnp.float32)))
    idx = jnp.arange(C, dtype=jnp.float32)
    diff = idx[:, None] - idx[None, :]
    decay = jnp.where(diff[None] >= 0,
                      jnp.exp(jnp.maximum(diff, 0.0)[None] * log_gamma[:, None, None]), 0.0)
    w_k = jnp.exp((C - 1.0 - idx)[None, :] * log_gamma[:, None])
    w_q = jnp.exp((idx + 1.0)[None, :] * log_gamma[:, None])
    g_chunk = jnp.exp(C * log_gamma)
    qc = q.reshape(B, N, C, H, D)
    kc = k.reshape(B, N, C, H, D)
    vc = v.reshape(B, N, C, H, D)
    scores = jnp.einsum('bnihd,bnjhd->bnhij', qc, kc) * decay
    intra = jnp.einsum('bnhij,bnjhe->bnihe', scores, vc)
    kv = jnp.einsum('bnjhd,hj,bnjhe->bnhde', kc, w_k, vc)

    def step(state, kv_n):
        return state * g_chunk[None, :, None, None] + kv_n, state

    init = jnp.zeros((B, H, D, D), dtype=kv.dtype)
    _, states = lax.scan(step, init, jnp.moveaxis(kv, 1, 0))
    states = jnp.moveaxis(states, 0, 1)
    cross = jnp.einsum('bnihd,hi,bnhde->bnihe', qc, w_q, states)
    o = (intra + cross).reshape(B, S, H, D).astype(jnp.float32)
    mu = jnp.mean(o, axis=-1, keepdims=True)
    var = jnp.mean(jnp.square(o - mu), axis=-1, keepdims=True)
    o = ((o - mu) * lax.rsqrt(var + GN_EPS)).reshape(B, S, H * D).astype(gate.dtype)
    return jax.nn.silu(gate) * o

def hybrid_mixer(x, w_in, w_out, sinks, rope_cos, rope_sin, ret_cos, ret_sin):
    B, S, _ = x.shape
    h = x @ w_in
    qa, ka, va, qr, kr, vr, gr = jnp.split(h, IN_SPLITS, axis=-1)
    qa = apply_rope(qa.reshape(B, S, ATTN_Q_HEADS, HEAD_DIM), rope_cos, rope_sin)
    ka = apply_rope(ka.reshape(B, S, ATTN_KV_HEADS, HEAD_DIM), rope_cos, rope_sin)
    va = va.reshape(B, S, ATTN_KV_HEADS, HEAD_DIM)
    y_attn = sliding_window_sink_attention(qa, ka, va, sinks)
    qr = apply_pair_rotation(qr.reshape(B, S, RET_HEADS, HEAD_DIM), ret_cos, ret_sin)
    kr = apply_pair_rotation(kr.reshape(B, S, RET_HEADS, HEAD_DIM), ret_cos, ret_sin) * (HEAD_DIM ** -0.5)
    y_ret = multiscale_retention(qr, kr, vr.reshape(B, S, RET_HEADS, HEAD_DIM), gr)
    return jnp.concatenate([y_attn, y_ret], axis=-1) @ w_out

def second_inputs(seed: int = 0) -> dict:
    key = jax.random.key(seed)
    ks = jax.random.split(key, 16)
    f32 = jnp.float32
    x = jax.random.normal(ks[0], (BATCH, SEQ, D_MODEL), f32)
    col_scale = jnp.concatenate([
        jnp.ones((ATTN_WIDTH + KV_WIDTH,), f32),
        jnp.full((KV_WIDTH,), DEEPNORM_BETA, f32),
        jnp.ones((2 * RET_WIDTH,), f32),
        jnp.full((RET_WIDTH,), DEEPNORM_BETA, f32),
        jnp.ones((RET_WIDTH,), f32)])
    w_in = jax.random.normal(ks[1], (DEPTH, D_MODEL, IN_WIDTH), f32) * (D_MODEL ** -0.5) * col_scale
    w_out = jax.random.normal(ks[2], (DEPTH, MIX_WIDTH, D_MODEL), f32) * (MIX_WIDTH ** -0.5) * DEEPNORM_BETA
    attn_sinks = 0.5 * jax.random.normal(ks[3], (DEPTH, ATTN_Q_HEADS), f32)
    ffn1_w_gu = jax.random.normal(ks[4], (DEPTH, D_MODEL, 2 * D_FF), f32) * (D_MODEL ** -0.5) * DEEPNORM_BETA
    ffn1_w_down = jax.random.normal(ks[5], (DEPTH, D_FF, D_MODEL), f32) * (D_FF ** -0.5) * DEEPNORM_BETA
    ffn2_w_gu = jax.random.normal(ks[6], (DEPTH, D_MODEL, 2 * D_FF), f32) * (D_MODEL ** -0.5) * DEEPNORM_BETA
    ffn2_w_down = jax.random.normal(ks[7], (DEPTH, D_FF, D_MODEL), f32) * (D_FF ** -0.5) * DEEPNORM_BETA
    ln1_g = 1.0 + 0.02 * jax.random.normal(ks[8], (DEPTH, D_MODEL), f32)
    ln1_b = 0.02 * jax.random.normal(ks[9], (DEPTH, D_MODEL), f32)
    ln2_g = 1.0 + 0.02 * jax.random.normal(ks[10], (DEPTH, D_MODEL), f32)
    ln2_b = 0.02 * jax.random.normal(ks[11], (DEPTH, D_MODEL), f32)
    ln3_g = 1.0 + 0.02 * jax.random.normal(ks[12], (DEPTH, D_MODEL), f32)
    ln3_b = 0.02 * jax.random.normal(ks[13], (DEPTH, D_MODEL), f32)
    return {"x": x, "w_in": w_in, "w_out": w_out, "attn_sinks": attn_sinks,
            "ffn1_w_gu": ffn1_w_gu, "ffn1_w_down": ffn1_w_down,
            "ffn2_w_gu": ffn2_w_gu, "ffn2_w_down": ffn2_w_down,
            "ln1_g": ln1_g, "ln1_b": ln1_b, "ln2_g": ln2_g, "ln2_b": ln2_b,
            "ln3_g": ln3_g, "ln3_b": ln3_b}

def second_block(x, w_in, w_out, attn_sinks, ffn1_w_gu, ffn1_w_down, ffn2_w_gu, ffn2_w_down,
              ln1_g, ln1_b, ln2_g, ln2_b, ln3_g, ln3_b):
    S = x.shape[1]
    rope_cos, rope_sin = rope_tables(S)
    ret_cos, ret_sin = retention_rotation_tables(S)
    for l in range(DEPTH):
        x = layer_norm(DEEPNORM_ALPHA * x + 0.5 * swiglu_ffn(x, ffn1_w_gu[l], ffn1_w_down[l]),
                       ln1_g[l], ln1_b[l])
        x = layer_norm(DEEPNORM_ALPHA * x + hybrid_mixer(x, w_in[l], w_out[l], attn_sinks[l],
                                                         rope_cos, rope_sin, ret_cos, ret_sin),
                       ln2_g[l], ln2_b[l])
        x = layer_norm(DEEPNORM_ALPHA * x + 0.5 * swiglu_ffn(x, ffn2_w_gu[l], ffn2_w_down[l]),
                       ln3_g[l], ln3_b[l])
    return x


def setup_inputs(seed=0):
    out = dict(first_inputs(seed))
    for name, value in second_inputs(seed + 1).items():
        if name != "x":
            out[name + "_2"] = value
    return out


def reference(
    x, c, ctx, c_ctx, w_mod, b_mod, norm_mix_g, norm_ffn_g, mla_w_dq, mla_g_q, mla_w_uq,
    mla_w_dkv, mla_g_kv, mla_w_ukv, mla_w_o, conv_w_in, conv_w, conv_w_out, gqa_w_qkv,
    gqa_q_norm_g, gqa_k_norm_g, gqa_w_o, moe_w_group, moe_b_group, moe_w_expert, moe_b_expert,
    moe_w_gate, moe_w_up, moe_w_down, final_norm_g, w_in_2, w_out_2, attn_sinks_2, ffn1_w_gu_2,
    ffn1_w_down_2, ffn2_w_gu_2, ffn2_w_down_2, ln1_g_2, ln1_b_2, ln2_g_2, ln2_b_2, ln3_g_2,
    ln3_b_2,
):
    x = first_block(
        x, c, ctx, c_ctx, w_mod, b_mod, norm_mix_g, norm_ffn_g, mla_w_dq, mla_g_q, mla_w_uq,
        mla_w_dkv, mla_g_kv, mla_w_ukv, mla_w_o, conv_w_in, conv_w, conv_w_out, gqa_w_qkv,
        gqa_q_norm_g, gqa_k_norm_g, gqa_w_o, moe_w_group, moe_b_group, moe_w_expert,
        moe_b_expert, moe_w_gate, moe_w_up, moe_w_down, final_norm_g,
    )
    return second_block(
        x, w_in_2, w_out_2, attn_sinks_2, ffn1_w_gu_2, ffn1_w_down_2, ffn2_w_gu_2,
        ffn2_w_down_2, ln1_g_2, ln1_b_2, ln2_g_2, ln2_b_2, ln3_g_2, ln3_b_2,
    )


_drawn_inputs = setup_inputs


def setup_inputs(seed=0):
    import zlib

    import numpy as np

    out = dict(_drawn_inputs(seed))
    spreads = {}
    factors = {'mla_g_q': 8.0,
     'mla_g_kv': 6.688,
     'moe_b_group': 12.473,
     'attn_sinks_2': 37.618,
     'norm_ffn_g': 3.768,
     'moe_b_expert': 6.032}
    for name, (base, spread) in spreads.items():
        noise = np.random.default_rng([zlib.crc32(name.encode()), seed]).standard_normal(out[name].shape)
        drawn = base * np.exp(spread * noise) if base else spread * noise
        out[name] = __import__('jax').numpy.asarray(drawn.astype(out[name].dtype))
    for name, factor in factors.items():
        out[name] = (out[name] * factor).astype(out[name].dtype)
    return out
```

```python
from contextlib import ExitStack

import concourse.bass as bass
import numpy as np
from concourse import mybir

F32 = mybir.dt.float32
F32R = mybir.dt.float32r
I32 = mybir.dt.int32
ACT = mybir.ActivationFunctionType
ALU = mybir.AluOpType
X = mybir.AxisListType.X

P = 128
D = 1024
KD = D // P
TL = 256
TA = 512
NORM_EPS = 1e-6

HEADS = 8
Q_LORA, KV_LORA = 512, 256
NOPE, ROPE, DV = 128, 64, 128
QW = NOPE + ROPE
MLA_SCALE = float(QW) ** -0.5
GRID_W = 64

GROUPS, PER_GROUP = 4, 8
EXPERTS = GROUPS * PER_GROUP
FF = 512
FT = FF // P
CAP = P
OUT_OF_BOUNDS = 4096.0

LAYERS = 2
D_FF = 2816
FFT = D_FF // P
HD = 64
AH, AKV, RH = 8, 2, 8
ALPHA = (2 * LAYERS) ** 0.25
LN_EPS, GN_EPS = 1e-5, 1e-6
MASKED = -1e30

RING = 6
SLOT = 4096
RING_2 = 4

UNIT = 1024
UNITS = (RING - RING_2) * SLOT // (2 * UNIT)
FFN_UNITS = 2 * FFT + KD * 3
FIRST_BYTE = 16640


def blocks_of(tokens):
    return EXPERTS + 2 * tokens // (CAP + 1) + 2


def shape_constants():
    f = np.float32
    ident = np.eye(P, dtype=f)
    ones = np.ones((P, P), f)
    before = np.triu(np.ones((P, P), f), 1)
    iota = np.tile(np.arange(P, dtype=f), (P, 1))
    lane = np.arange(P)[:, None] + P * np.arange(4)[None, :]
    place = np.concatenate([2 * lane + 1, 2 * lane + 2, lane + 1], axis=1).astype(f)
    base = np.concatenate([ident, ones, before, iota, place], axis=1)

    def angles(pos, half, theta):
        freq = theta ** (-np.arange(half, dtype=f) / f(half))
        return (pos.astype(f)[:, None] * freq[None, :].astype(f)).astype(f)

    rows, cols = np.repeat(np.arange(TL // GRID_W), GRID_W), np.tile(np.arange(GRID_W), TL // GRID_W)
    quarter = ROPE // 4
    ang = np.concatenate([angles(p, quarter, f(10000.0)).T for p in (rows, rows, cols, cols)], axis=0)
    cos, sin = np.zeros((P, TA), f), np.zeros((P, TA), f)
    cos[:ROPE, :TL], sin[:ROPE, :TL] = np.cos(ang), np.sin(ang)
    cos[:ROPE, TL:] = 1.0
    turn = np.zeros((P, ROPE), f)
    for b in range(0, ROPE, 2 * quarter):
        for i in range(quarter):
            turn[b + quarter + i, b + i] = -1.0
            turn[b + i, b + quarter + i] = 1.0
    mla = np.concatenate([cos, sin, turn], axis=1)

    pos = np.arange(TL, dtype=f)
    half = HD // 2
    inv = (f(10000.0) ** (-np.arange(0, HD, 2, dtype=f) / f(HD))).astype(f)
    a = (pos[:, None] * inv[None, :]).astype(f).T
    a = np.concatenate([a, a, a, a], axis=0)
    inv = (f(1.0) / (f(10000.0) ** np.linspace(0.0, 1.0, half, dtype=f))).astype(f)
    r = (pos[:, None] * inv[None, :]).astype(f).T
    r = np.repeat(r, 2, axis=0)
    r = np.concatenate([r, r], axis=0)
    turn_a, turn_r = np.zeros((P, P), f), np.zeros((P, P), f)
    for b in range(0, P, HD):
        for i in range(half):
            turn_a[b + half + i, b + i] = -1.0
            turn_a[b + i, b + half + i] = 1.0
            turn_r[b + 2 * i + 1, b + 2 * i] = -1.0
            turn_r[b + 2 * i, b + 2 * i + 1] = 1.0
    head_mean = np.kron(np.eye(2, dtype=f), np.full((HD, HD), 1.0 / HD, f))
    q, k = np.arange(P)[:, None], np.arange(P)[None, :]
    own = np.where(q >= k, 0.0, MASKED).astype(f)
    prev = np.where(q - k + P < P, 0.0, MASKED).astype(f)
    mask = np.concatenate([own, prev, own], axis=1)
    log_gamma = np.log1p(-np.exp2(-5.0 - np.arange(RH, dtype=f))).astype(f)
    diff = np.arange(TL, dtype=f)[None, :] - np.arange(P, dtype=f)[:, None]
    decay = [np.where(diff >= 0, np.exp(np.maximum(diff, 0.0) * g), 0.0).astype(f) for g in log_gamma]
    mix = np.concatenate([np.cos(a), np.sin(a), np.cos(r), np.sin(r), turn_a, turn_r, head_mean, mask,
                          ones / f(D)] + decay, axis=1).astype(f)
    return base, mla, mix


VEC = {}
VEC_WIDTH = 0
for _name, _width in (("cond", 2 * KD), ("b_mod", 2 * 48), ("norm_mix", 2 * KD), ("norm_ffn", 2 * KD),
                      ("final", KD), ("g_q", 4), ("g_kv", 2), ("conv", 3 * KD), ("ln", LAYERS * 6 * KD),
                      ("router", 2 * KD * 36), ("router_bias", 2 * 36), ("sinks", LAYERS * AH)):
    VEC[_name] = VEC_WIDTH
    VEC_WIDTH += _width


ACT_PER_LAYER = 0
DVE_PER_LAYER = 108
SPLITS_PER_LAYER = 2 * FFN_UNITS


class Signal:

    def __init__(self, sem, base=0, per_turn=0):
        self.sem, self.base, self.n, self.per_turn = sem, base, base, per_turn


class Lane:

    def __init__(self, eng, line, spare):
        self.eng, self.line, self.spare, self.turn, self.last = eng, line, spare, None, None

    def wait(self, signal, value):
        value += signal.base
        if self.turn is not None and signal.per_turn:
            value = self.turn * signal.per_turn + value
        self.eng.wait_ge(signal.sem, value)

    def inc(self, ins, signal=None):
        signal = signal or self.line
        ins.then_inc(signal.sem, 1)
        signal.n += 1
        self.last = (signal, signal.n - signal.base)

    def join(self):
        self.wait(*self.last)

    def settle(self):
        self.eng.sem_inc(self.spare.sem, 1)


def program(nc, xT, vec, base_c, mla_c, mix_c, w, out):
    ctx = ExitStack()
    with ctx:
        used_bytes = [FIRST_BYTE]

        def place(name, shape, dt, at):
            return nc.alloc_sbuf_tensor_at(name, shape, dt, offset=at)

        def sb(name, shape, dt=F32):
            at = used_bytes[0]
            used_bytes[0] += (4 * int(np.prod(shape[1:])) + 31) // 32 * 32
            return place(name, shape, dt, at)

        def sig(name, per_turn=0):
            return Signal(ctx.enter_context(nc.semaphore(name)), 0, per_turn)

        reused = {}

        def shared(name, count, turns=0):
            if name not in reused:
                reused[name] = [ctx.enter_context(nc.semaphore(name)), 0]
            sem, base = reused[name]
            reused[name][1] += count
            return Signal(sem, base, count * turns)

        ring_at = used_bytes[0]
        ring = sb("ring", [P, RING, SLOT])
        XT = sb("XT", [P, KD, TA])
        A_at = used_bytes[0]
        A = sb("A", [P, KD, TA])
        VECS = sb("VECS", [P, VEC_WIDTH])
        BASE = sb("BASE", [P, 4 * P + 12])
        RS = sb("RS", [P, 2, TA])
        COND = sb("COND", [P, KD, 2])
        MOD = [sb(f"MOD{l}", [P, 48, 2]) for l in range(2)]
        GAIN = [sb(f"GAIN{l}", [P, 2, KD, 2]) for l in range(2)]
        ARENA_W = 17568
        arena_at = used_bytes[0]
        arena = sb("arena", [P, ARENA_W])
        ps = ctx.enter_context(nc.psum_tensor("ps", [P, 8, 512], F32))

        IDENT, ONES, BEFORE, IOTA = (BASE[:, i * P:(i + 1) * P] for i in range(4))
        PLACE = BASE[:, 4 * P:4 * P + 12].rearrange("p (c t) -> p c t", c=3)

        def vcol(name, width, shift=0):
            return VECS[:, VEC[name] + shift:VEC[name] + shift + width]

        def carver():
            used = [0]

            def take(width):
                at = used[0]
                used[0] += width
                assert used[0] <= ARENA_W, (used[0], ARENA_W)
                return arena[:, at:at + width]
            return take

        f_rows = nc.dram_tensor("f_rows", [TA, D], F32, kind="Internal").ap()
        y_rows = nc.dram_tensor("y_rows", [2 * TA, D], F32, kind="Internal").ap()

        const_in = sig("const_in")
        x_in = sig("x_in")
        mla_in = sig("mla_in")
        mix_in = sig("mix_in")
        stages_done = sig("stages_done")
        slot_in = [sig(f"slot_in{i}") for i in range(RING)]
        spare = sig("spare")
        line = {e: sig(f"line_{e}") for e in ("pe", "act", "dve", "pool")}
        loop_line = {"act": sig("loop_line_act", ACT_PER_LAYER), "dve": sig("loop_line_dve", DVE_PER_LAYER)}

        loads, frees, arrivals, place_of, before = [], [], [], [], []
        second_stack = []

        def slot(n):
            return ring[:, place_of[n], :]

        def plan(src, shape, freed_by):
            n = len(loads)
            at = (n - second_stack[0]) % RING_2 if second_stack else n % RING
            before.append(max((i for i in range(n) if place_of[i] == at), default=None))
            place_of.append(at)
            width = int(np.prod(shape))
            dst = slot(n)[:, 0:width]
            if len(shape) == 2:
                dst = dst.rearrange("p (k n) -> p k n", k=shape[0])
            elif len(shape) == 3:
                dst = dst.rearrange("p (k a n) -> p k a n", k=shape[0], a=shape[1])
            parts = [(dst, src)] if len(shape) == 2 else [(dst[:, :, a, :], src[:, :, a, :]) for a in range(shape[1])]
            loads.append(parts)
            slot_in[at].n += 16 * len(parts)
            arrivals.append(slot_in[at].n)
            signal, value, turn = (*freed_by, 0)[:3]
            frees.append((signal.sem, signal.base + signal.per_turn * turn + value))
            return n

        def columns(weight, c0, c1):
            return weight[:, c0:c1].rearrange("(k p) n -> p k n", p=P)

        def slot_ready(L, n):
            L.wait(slot_in[place_of[n]], arrivals[n])

        PER_LAYER_STAGES = 6
        counters = {"pe": 0, "act": 0, "dve": 0}

        def begin(L, name):
            s = counters[name]
            if s:
                value = 3 * s
                if L.turn is not None:
                    value = L.turn * (3 * PER_LAYER_STAGES) + value
                L.eng.wait_ge(stages_done.sem, value)
                if L.turn is not None:
                    L.settle()

        def end(L, name):
            if L.last:
                L.join()
            L.eng.sem_inc(stages_done.sem, 1)
            counters[name] += 1

        class Mod:

            def __init__(self, l):
                self.l = l
                self.rows = sig(f"mod{l}_rows", 6)
                self.rows_kept = sig(f"mod{l}_rows_kept", 6)
                self.turned = sig(f"mod{l}_turned", 6)
                self.kept = sig(f"mod{l}_kept", 1)
                self.first = len(loads)
                for s in range(12):
                    plan(columns(w["w_mod"][l], 512 * s, 512 * (s + 1)), (KD, 512), (self.rows, s + 1))

            def pe(self, L):
                begin(L, "pe")
                L.eng.wait_ge(const_in.sem, 32)
                with L.eng.Fori(0, 2) as turn:
                    def turn_rows(s):
                        if s == 0:
                            L.eng.wait_ge(self.kept.sem, turn + 1)
                        L.eng.wait_ge(self.rows_kept.sem, turn * 6 + s + 1)
                        L.settle()
                        for t in range(4):
                            c = 4 * s + t
                            mm = L.eng.transpose(ps[:, 0, 2 * c:2 * c + 2], RS[0:2, s % 2, t * P:(t + 1) * P], IDENT[0:2, 0:2])
                        L.inc(mm, self.turned)

                    for s in range(6):
                        n = self.first + s
                        L.eng.wait_ge(slot_in[n % RING].sem, turn * 16 + arrivals[n])
                        wv = slot(n).rearrange("p (k n) -> p k n", k=KD)
                        for k in range(KD):
                            mm = L.eng.matmul(ps[0:2, 1 + s % 2, :], COND[:, k, :], wv[:, k, :], start=k == 0, stop=k == KD - 1)
                        L.inc(mm, self.rows)
                        if s:
                            turn_rows(s - 1)
                    turn_rows(5)
                L.last = (self.turned, 12)
                end(L, "pe")

            def act(self, L):
                begin(L, "act")
                with L.eng.Fori(0, 2) as turn:
                    for s in range(6):
                        L.eng.wait_ge(self.rows.sem, turn * 6 + s + 1)
                        if s >= 2:
                            L.eng.wait_ge(self.turned.sem, turn * 6 + s - 1)
                        L.inc(L.eng.copy(RS[0:2, s % 2, :], ps[0:2, 1 + s % 2, :]), self.rows_kept)
                L.last = (self.rows_kept, 12)
                end(L, "act")

            def dve(self, L):
                begin(L, "dve")
                L.eng.wait_ge(const_in.sem, 32)
                L.eng.sem_inc(self.kept.sem, 1)
                b = vcol("b_mod", 48, 48 * self.l)
                mod, gain = MOD[self.l], GAIN[self.l]
                with L.eng.Fori(0, 2) as turn:
                    L.eng.wait_ge(self.turned.sem, turn * 6 + 6)
                    half = bass.ds(turn * 24, 24)
                    L.eng.tensor_tensor(mod[:, half, :], ps[:, 0, 0:48].rearrange("p (c a) -> p c a", a=2),
                                        b[:, half].unsqueeze(2).to_broadcast([P, 24, 2]),
                                        ALU.add).then_inc(self.kept.sem, 1)
                L.last = (self.kept, 3)
                L.join()
                for which, name in enumerate(("norm_mix", "norm_ffn")):
                    g = vcol(name, KD, KD * self.l).unsqueeze(2).to_broadcast([P, KD, 2])
                    at = KD * (3 * which + 1)
                    L.inc(L.eng.scalar_tensor_tensor(out=gain[:, which], in0=mod[:, at:at + KD, :], scalar=1.0,
                                                     in1=g, op0=ALU.add, op1=ALU.mult))
                end(L, "dve")

        class Norm:
            def __init__(self, name, l, which, tokens):
                self.l, self.which, self.T = l, which, tokens
                plain = which == 2
                self.sq_act = shared("norm_sq_act", KD // 2)
                self.sq_dve = shared("norm_sq_dve", KD // 2)
                self.sums = shared("norm_sums", 1)
                self.var = shared("norm_var", 1)
                self.std = shared("norm_std", 1)
                self.scaled = shared("norm_scaled", 0 if plain else KD)
                self.done = shared("norm_done", 0 if plain else KD * tokens // TL)

            def pe(self, L):
                begin(L, "pe")
                for k in range(KD):
                    L.wait(self.sq_dve if k % 2 else self.sq_act, k // 2 + 1)
                    mm = L.eng.matmul(ps[:, 6, 0:self.T], ONES, A[:, k, 0:self.T], start=k == 0, stop=k == KD - 1)
                L.inc(mm, self.sums)
                end(L, "pe")

            def act(self, L):
                begin(L, "act")
                if self.l == 0 and self.which == 0:
                    L.eng.wait_ge(x_in.sem, 16)
                T = self.T
                for k in range(0, KD, 2):
                    L.inc(L.eng.activation(A[:, k, 0:T], XT[:, k, 0:T], ACT.Square), self.sq_act)
                L.wait(self.var, 1)
                L.inc(L.eng.activation(RS[:, 0, 0:T], RS[:, 0, 0:T], ACT.Sqrt), self.std)
                if self.which < 2:
                    gain, mod = GAIN[self.l], MOD[self.l]
                    for k in range(KD):
                        L.wait(self.scaled, k + 1)
                        for c in range(T // TL):
                            a = A[:, k, c * TL:(c + 1) * TL]
                            L.inc(L.eng.activation(a, a, ACT.Identity, bias=mod[:, 3 * KD * self.which + k, c:c + 1],
                                                   scale=gain[:, self.which, k, c:c + 1]), self.done)
                end(L, "act")

            def dve(self, L):
                begin(L, "dve")
                if self.l == 0 and self.which == 0:
                    L.eng.wait_ge(x_in.sem, 16)
                T = self.T
                for k in range(1, KD, 2):
                    L.inc(L.eng.tensor_tensor(A[:, k, 0:T], XT[:, k, 0:T], XT[:, k, 0:T], ALU.mult), self.sq_dve)
                L.wait(self.sums, 1)
                L.inc(L.eng.tensor_scalar(RS[:, 0, 0:T], ps[:, 6, 0:T], 1.0 / D, NORM_EPS, ALU.mult, ALU.add), self.var)
                L.wait(self.std, 1)
                L.inc(L.eng.reciprocal(RS[:, 0, 0:T], RS[:, 0, 0:T]))
                L.join()
                for k in range(KD):
                    if self.which < 2:
                        L.inc(L.eng.tensor_tensor(A[:, k, 0:T], XT[:, k, 0:T], RS[:, 0, 0:T], ALU.mult), self.scaled)
                    else:
                        L.inc(L.eng.scalar_tensor_tensor(out=XT[:, k, 0:T], in0=XT[:, k, 0:T],
                                                         scalar=vcol("final", KD)[:, k:k + 1], in1=RS[:, 0, 0:T],
                                                         op0=ALU.mult, op1=ALU.mult))
                end(L, "dve")

        class LayerNorm:
            def __init__(self, i):
                self.i = i
                self.mean = shared("ln_mean", 1, 3)
                self.centred = shared("ln_centred", KD, 3)
                self.squares = shared("norm_sq_act", KD, 3)
                self.sums = shared("norm_sums", 1, 3)
                self.var = shared("norm_var", 1, 3)
                self.std = shared("norm_std", 1, 3)
                self.scaled = shared("norm_scaled", KD, 3)
                self.done = shared("norm_done", KD, 3)

            def pe(self, L):
                begin(L, "pe")
                for k in range(KD):
                    mm = L.eng.matmul(ps[:, 5, 0:TL], MEAN, XT[:, k, 0:TL], start=k == 0, stop=k == KD - 1)
                L.inc(mm, self.mean)
                for k in range(KD):
                    L.wait(self.squares, k + 1)
                    mm = L.eng.matmul(ps[:, 6, 0:TL], MEAN, A[:, k, TL:TA], start=k == 0, stop=k == KD - 1)
                L.inc(mm, self.sums)
                end(L, "pe")

            def act(self, L):
                begin(L, "act")
                for k in range(KD):
                    L.wait(self.centred, k + 1)
                    L.inc(L.eng.activation(A[:, k, TL:TA], A[:, k, 0:TL], ACT.Square), self.squares)
                L.wait(self.var, 1)
                L.inc(L.eng.activation(RS[:, 0, 0:TL], RS[:, 0, 0:TL], ACT.Sqrt), self.std)
                for k in range(KD):
                    L.wait(self.scaled, k + 1)
                    L.inc(L.eng.activation(XT[:, k, 0:TL], XT[:, k, 0:TL], ACT.Identity,
                                           bias=LNP[:, (2 * self.i + 1) * KD + k:(2 * self.i + 1) * KD + k + 1]), self.done)
                end(L, "act")

            def dve(self, L):
                begin(L, "dve")
                L.wait(self.mean, 1)
                for k in range(KD):
                    L.inc(L.eng.tensor_tensor(A[:, k, 0:TL], XT[:, k, 0:TL], ps[:, 5, 0:TL], ALU.subtract), self.centred)
                L.wait(self.sums, 1)
                L.inc(L.eng.tensor_scalar(RS[:, 0, 0:TL], ps[:, 6, 0:TL], LN_EPS / ALPHA ** 2, None, ALU.add), self.var)
                L.wait(self.std, 1)
                L.inc(L.eng.reciprocal(RS[:, 0, 0:TL], RS[:, 0, 0:TL]))
                L.join()
                for k in range(KD):
                    L.inc(L.eng.scalar_tensor_tensor(out=XT[:, k, 0:TL], in0=A[:, k, 0:TL],
                                                     scalar=LNP[:, 2 * self.i * KD + k:2 * self.i * KD + k + 1],
                                                     in1=RS[:, 0, 0:TL], op0=ALU.mult, op1=ALU.mult), self.scaled)
                end(L, "dve")

        take = carver()
        KT = take(HEADS * TA).rearrange("p (h t) -> p h t", h=HEADS)
        V = take(4 * D).rearrange("p (t c) -> p t c", t=4)
        CKV = take(2 * TA).rearrange("p (c t) -> p c t", c=2)
        CQ = take(4 * TA).rearrange("p (c t) -> p c t", c=4)
        KPE, QN, QR, QRAW, T1 = (take(TA) for _ in range(5))
        PC = take(2 * TL).rearrange("p (q t) -> p q t", q=2)
        PTL = take(4 * TL).rearrange("p (k t) -> p k t", k=4)
        PTC = take(2 * TL).rearrange("p (k t) -> p k t", k=2)
        MLAC = take(2 * TA + ROPE)
        SMALL = take(16)
        PL = CKV
        SQ = [PTL[:, 0:2].rearrange("p a b -> p (a b)"), PTL[:, 2:4].rearrange("p a b -> p (a b)"),
              PTC.rearrange("p a b -> p (a b)"), PC.rearrange("p a b -> p (a b)"), QN, QR]
        OT = A
        COS, SIN, TURN = MLAC[0:ROPE, 0:TA], MLAC[0:ROPE, TA:2 * TA], MLAC[0:ROPE, 2 * TA:2 * TA + ROPE]
        MAXS, NEG, DEN, RDEN = (SMALL[:, 4 * i:4 * i + 4] for i in range(4))

        class Mla:
            def __init__(self):
                self.tiles = sig("mla_tiles")
                self.copied = sig("mla_copied")
                self.squares = sig("mla_squares")
                self.kpe_turned = sig("mla_kpe_turned")
                self.sums = sig("mla_sums")
                self.var = sig("mla_var")
                self.std = sig("mla_std")
                self.latents = sig("mla_latents")
                self.q_tiles = sig("mla_q_tiles")
                self.q_copied = sig("mla_q_copied")
                self.q_turned = sig("mla_q_turned")
                self.q_ready = sig("mla_q_ready")
                self.scores = sig("mla_scores")
                self.neg = sig("mla_neg")
                self.exps = sig("mla_exps")
                self.probs = sig("mla_probs")
                self.turned = sig("mla_turned")
                self.turned_copied = sig("mla_turned_copied")
                self.outs = sig("mla_outs")
                self.outs_copied = sig("mla_outs_copied")
                self.y_tiles = sig("mla_y_tiles")
                self.y_added = sig("mla_y_added")
                self.dkv = plan(columns(w["mla_w_dkv"][0], 0, 320), (KD, 320), (self.tiles, 3))
                self.dq = plan(columns(w["mla_w_dq"][0], 0, Q_LORA), (KD, Q_LORA), (self.tiles, 7))
                self.ukv = plan(columns(w["mla_w_ukv"][0], 0, 2048), (2, 2048), (self.tiles, 23))
                self.uq = [plan(columns(w["mla_w_uq"][0], 0, 5 * QW), (4, 5 * QW), (self.q_tiles, 10)),
                           plan(columns(w["mla_w_uq"][0], 5 * QW, 8 * QW), (4, 3 * QW), (self.q_tiles, 16))]
                self.wo = [plan(columns(w["mla_w_o"][0], 512 * i, 512 * (i + 1)), (HEADS, 512), (self.y_tiles, 4 * i + 4))
                           for i in range(2)]

            def q_weights(self, h, c0, c1):
                n = self.uq[0 if h < 5 else 1]
                heads = 5 if h < 5 else 3
                at = (h if h < 5 else h - 5) * QW
                return slot(n)[:, 0:4 * heads * QW].rearrange("p (k n) -> p k n", k=4)[:, :, at + c0:at + c1]

            def pe(self, L):
                begin(L, "pe")
                pe = L.eng
                pe.wait_ge(mla_in.sem, 16)
                i = 0
                for n, width, outs in ((self.dkv, 320, ((0, 128), (128, 256), (256, 320))),
                                       (self.dq, 512, tuple((c, c + 128) for c in range(0, 512, 128)))):
                    slot_ready(L, n)
                    wv = slot(n)[:, 0:KD * width].rearrange("p (k n) -> p k n", k=KD)
                    for c0, c1 in outs:
                        if i >= 4:
                            L.wait(self.copied, i - 3)
                        for k in range(KD):
                            mm = pe.matmul(ps[0:c1 - c0, i % 4, :], wv[:, k, c0:c1], A[:, k, :], start=k == 0, stop=k == KD - 1)
                        L.inc(mm, self.tiles)
                        i += 1
                L.wait(self.copied, 3)
                L.inc(pe.matmul(ps[0:ROPE, 4, :], TURN, QRAW[0:ROPE, :], start=True, stop=True), self.kpe_turned)
                for first, count, bank in ((0, 2, 5), (2, 4, 6)):
                    for c in range(count):
                        L.wait(self.squares, first + c + 1)
                        mm = pe.matmul(ps[:, bank, :], ONES, SQ[first + c], start=c == 0, stop=c == count - 1)
                    L.inc(mm, self.sums)
                slot_ready(L, self.ukv)
                wv = slot(self.ukv).rearrange("p (k h a n) -> p k h a n", k=2, h=HEADS, a=2)
                L.wait(self.latents, 2)
                for h in range(HEADS):
                    L.wait(self.copied, i - 3)
                    for k in range(2):
                        mm = pe.matmul(ps[:, i % 4, :], wv[:, k, h, 0, :], CKV[:, k, :], start=k == 0, stop=k == 1)
                    L.inc(mm, self.tiles)
                    i += 1
                for t in range(4):
                    for half in range(2):
                        L.wait(self.copied, i - 3)
                        for k in range(2):
                            mm = pe.matmul(ps[:, i % 4, :], CKV[:, k, t * P:(t + 1) * P],
                                           wv[:, k, 4 * half:4 * half + 4, 1, :], start=k == 0, stop=k == 1)
                        L.inc(mm, self.tiles)
                        i += 1
                L.wait(self.latents, 6)

                def queries(h):
                    if h in (0, 5):
                        slot_ready(L, self.uq[0 if h < 5 else 1])
                    for k in range(4):
                        mm = pe.matmul(ps[:, 7, :], self.q_weights(h, 0, NOPE)[:, k, :], CQ[:, k, :], start=k == 0, stop=k == 3)
                    L.inc(mm, self.q_tiles)
                    if h == 0:
                        L.wait(self.var, 2)
                    if h >= 2:
                        L.wait(self.outs_copied, h - 1)
                    for k in range(4):
                        mm = pe.matmul(ps[0:ROPE, 6, :], self.q_weights(h, NOPE, QW)[:, k, :], CQ[:, k, :],
                                       start=k == 0, stop=k == 3)
                    L.inc(mm, self.q_tiles)

                def turn_query(h):
                    L.wait(self.q_copied, 2 * h + 2)
                    L.inc(pe.matmul(ps[0:ROPE, 7, :], TURN, QRAW[0:ROPE, :], start=True, stop=True), self.q_turned)

                queries(0)
                turn_query(0)
                L.wait(self.copied, 23)
                for h in range(HEADS):
                    L.wait(self.q_ready, h + 1)
                    if h:
                        L.wait(self.exps, 4 * h)
                    for q in range(2):
                        rows = slice(q * P, (q + 1) * P)
                        pe.matmul(ps[:, q, :], QN[:, rows], KT[:, h, :], start=True, stop=False)
                        L.inc(pe.matmul(ps[:, q, :], QR[0:ROPE, rows], KPE[0:ROPE, :], start=False, stop=True), self.scores)
                    for q in range(2):
                        rows = slice(TL + q * P, TL + (q + 1) * P)
                        o = ps[:, 2, q * TL:(q + 1) * TL]
                        pe.matmul(o, QN[:, rows], KT[:, h, TL:TA], start=True, stop=False)
                        mm = pe.matmul(o, QR[0:ROPE, rows], KPE[0:ROPE, TL:TA], start=False, stop=True)
                    L.inc(mm, self.scores)
                    if h + 1 < HEADS:
                        queries(h + 1)
                    L.wait(self.probs, 4 * h + 4)
                    if h:
                        L.wait(self.turned_copied, 3 * h)
                    for bank in range(2):
                        for kk in range(2):
                            for q in range(2):
                                k = 2 * bank + kk
                                mm = pe.transpose(ps[:, 3 + bank, kk * TL + q * P:kk * TL + (q + 1) * P],
                                                  PL[:, q, k * P:(k + 1) * P], IDENT)
                        L.inc(mm, self.turned)
                    for kk in range(2):
                        for q in range(2):
                            mm = pe.transpose(ps[:, 5, kk * TL + q * P:kk * TL + (q + 1) * P],
                                              PC[:, q, kk * P:(kk + 1) * P], IDENT)
                    L.inc(mm, self.turned)
                    if h + 1 < HEADS:
                        turn_query(h + 1)
                    L.wait(self.turned_copied, 3 * h + 3)
                    if h:
                        L.wait(self.outs_copied, h)
                    for k in range(4):
                        pe.matmul(ps[:, 6, 0:TL], V[:, k, h * DV:(h + 1) * DV], PTL[:, k, :], start=k == 0, stop=k == 3)
                    for k in range(2):
                        mm = pe.matmul(ps[:, 6, TL:TA], V[:, 2 + k, h * DV:(h + 1) * DV], PTC[:, k, :], start=k == 0, stop=k == 1)
                    L.inc(mm, self.outs)
                L.wait(self.outs_copied, HEADS)
                for m in range(KD):
                    n = self.wo[m // 4]
                    if m % 4 == 0:
                        slot_ready(L, n)
                    if m >= 4:
                        L.wait(self.y_added, 2 * (m - 3))
                    wv = slot(n).rearrange("p (k n) -> p k n", k=HEADS)
                    for h in range(HEADS):
                        mm = pe.matmul(ps[:, m % 4, :], wv[:, h, m % 4 * P:(m % 4 + 1) * P], OT[:, h, :],
                                       start=h == 0, stop=h == HEADS - 1)
                    L.inc(mm, self.y_tiles)
                end(L, "pe")

            def act(self, L):
                begin(L, "act")
                act = L.eng
                for i in range(7):
                    L.wait(self.tiles, i + 1)
                    o = (CKV[:, 0, :], CKV[:, 1, :], QRAW[0:ROPE, :])[i] if i < 3 else CQ[:, i - 3, :]
                    L.inc(act.copy(o, ps[0:ROPE if i == 2 else P, i % 4, :]), self.copied)
                for i in range(2):
                    L.wait(self.var, i + 1)
                    L.inc(act.activation(RS[:, i, :], RS[:, i, :], ACT.Sqrt), self.std)
                for i in range(7, 23):
                    L.wait(self.tiles, i + 1)
                    j = i - 7
                    o = KT[:, j, :] if j < 8 else V[:, (j - 8) // 2, (j - 8) % 2 * 512:((j - 8) % 2 + 1) * 512]
                    L.inc(act.copy(o, ps[:, i % 4, :]), self.copied)

                def copy_query(h):
                    L.wait(self.q_tiles, 2 * h + 1)
                    if h == 0:
                        L.wait(self.latents, 6)
                    L.inc(act.copy(QN, ps[:, 7, :]), self.q_copied)
                    L.wait(self.q_tiles, 2 * h + 2)
                    L.inc(act.copy(QRAW[0:ROPE, :], ps[0:ROPE, 6, :]), self.q_copied)

                L.wait(self.latents, 7)
                copy_query(0)
                for h in range(HEADS):
                    L.wait(self.neg, h + 1)
                    for q in range(2):
                        L.inc(act.activation(PL[:, q, :], ps[:, q, :], ACT.Exp, bias=NEG[:, q:q + 1], scale=MLA_SCALE,
                                             accum_out=DEN[:, q:q + 1]), self.exps)
                    for q in range(2):
                        L.inc(act.activation(PC[:, q, :], ps[:, 2, q * TL:(q + 1) * TL], ACT.Exp, bias=NEG[:, 2 + q:3 + q],
                                             scale=MLA_SCALE, accum_out=DEN[:, 2 + q:3 + q]), self.exps)
                    if h + 1 < HEADS:
                        copy_query(h + 1)
                    L.wait(self.outs, h + 1)
                    L.inc(act.copy(OT[:, h, :], ps[:, 6, :]), self.outs_copied)
                end(L, "act")

            def dve(self, L):
                begin(L, "dve")
                dve = L.eng
                dve.wait_ge(mla_in.sem, 16)
                for c in range(6):
                    L.wait(self.copied, c + 1 if c < 2 else c + 2)
                    src = CKV[:, c, :] if c < 2 else CQ[:, c - 2, :]
                    L.inc(dve.tensor_tensor(SQ[c], src, src, ALU.mult), self.squares)
                for i, width in enumerate((KV_LORA, Q_LORA)):
                    L.wait(self.sums, i + 1)
                    L.inc(dve.tensor_scalar(RS[:, i, :], ps[:, 5 + i, :], 1.0 / width, NORM_EPS, ALU.mult, ALU.add), self.var)
                for i in range(2):
                    L.wait(self.std, i + 1)
                    L.inc(dve.reciprocal(RS[:, i, :], RS[:, i, :]))
                    L.join()
                    for c in range(2 + 2 * i):
                        o = CQ[:, c, :] if i else CKV[:, c, :]
                        L.inc(dve.scalar_tensor_tensor(out=o, in0=o, scalar=vcol("g_q" if i else "g_kv", 4 if i else 2)[:, c:c + 1],
                                                       in1=RS[:, i, :], op0=ALU.mult, op1=ALU.mult), self.latents)

                def rotate(out_ap, bank, signal):
                    L.inc(dve.tensor_tensor(T1[0:ROPE, :], QRAW[0:ROPE, :], COS, ALU.mult))
                    L.inc(dve.tensor_tensor(out_ap[0:ROPE, :], ps[0:ROPE, bank, :], SIN, ALU.mult))
                    L.join()
                    L.inc(dve.tensor_tensor(out_ap[0:ROPE, :], out_ap[0:ROPE, :], T1[0:ROPE, :], ALU.add), signal)

                L.wait(self.kpe_turned, 1)
                rotate(KPE, 4, self.latents)

                L.wait(self.q_turned, 1)
                rotate(QR, 7, self.q_ready)
                for h in range(HEADS):
                    for q in range(2):
                        L.wait(self.scores, 3 * h + q + 1)
                        L.inc(dve.tensor_reduce(MAXS[:, q:q + 1], ps[:, q, :], X, ALU.max))
                    L.wait(self.scores, 3 * h + 3)
                    L.inc(dve.tensor_reduce(MAXS[:, 2:4], ps[:, 2, :].rearrange("p (q t) -> p q t", q=2), X, ALU.max))
                    L.join()
                    L.inc(dve.tensor_scalar(NEG, MAXS, -MLA_SCALE, None, ALU.mult), self.neg)
                    L.wait(self.exps, 4 * h + 4)
                    L.inc(dve.reciprocal(RDEN, DEN))
                    L.join()
                    for q in range(4):
                        p = PL[:, q, :] if q < 2 else PC[:, q - 2, :]
                        L.inc(dve.tensor_scalar(p, p, RDEN[:, q:q + 1], None, ALU.mult), self.probs)
                    for bank in range(3):
                        L.wait(self.turned, 3 * h + bank + 1)
                        o = PTL[:, 2 * bank:2 * bank + 2, :] if bank < 2 else PTC
                        L.inc(dve.tensor_copy(o.rearrange("p k t -> p (k t)"), ps[:, 3 + bank, :]), self.turned_copied)
                    if h + 1 < HEADS:
                        L.wait(self.q_turned, h + 2)
                        rotate(QR, 7, self.q_ready)
                gated_add(L, 0, 0, TA, self.y_tiles, self.y_added)
                end(L, "dve")

        def gated_add(L, l, which, tokens, tiles, added):
            for m in range(KD):
                L.wait(tiles, m + 1)
                for c in range(tokens // TL):
                    xs = XT[:, m, c * TL:(c + 1) * TL]
                    L.inc(L.eng.scalar_tensor_tensor(out=xs, in0=ps[:, m % 4, c * TL:(c + 1) * TL],
                                                     scalar=MOD[l][:, 3 * KD * which + 2 * KD + m, c:c + 1], in1=xs,
                                                     op0=ALU.mult, op1=ALU.add), added)

        class Moe:

            def __init__(self, l, tokens):
                self.l, self.T, self.NT = l, tokens, tokens // P
                self.NB = blocks_of(tokens)
                NT = self.NT
                self.logits = shared("moe_logits", 1)
                self.logits_kept = shared("moe_logits_kept", 1)
                self.rows_turned = shared("moe_rows_turned", NT)
                self.rows_kept = shared("moe_rows_kept", NT)
                self.less_max = shared("moe_less_max", 2)
                self.exps = shared("moe_exps", 2)
                self.chosen = shared("moe_chosen", 1)
                self.ranks = shared("moe_ranks", 1)
                self.counts = shared("moe_counts", 1)
                self.counts_kept = shared("moe_counts_kept", 1)
                self.firsts = shared("moe_firsts", 1)
                self.places = shared("moe_places", 2 * NT)
                self.table = shared("moe_table", 1)
                self.table_kept = shared("moe_table_kept", 1)
                self.sum_turned = shared("moe_sum_turned", NT)
                self.sum_made = shared("moe_sum_made", NT)
                self.sum_added = shared("moe_sum_added", NT)
                self.expert_done = shared("moe_expert_done", EXPERTS)
                self.scattered_all = shared("moe_scattered_all", 1)
                self.rows_out = [shared(f"moe_rows_out{i}", 16 * NT // 2) for i in range(2)]
                self.pairs_in = [shared(f"moe_pairs_in{i}", 16 * NT // 2) for i in range(2)]
                self.block_turned = sig(f"moe{l}_block_turned")
                self.block_kept = sig(f"moe{l}_block_kept")
                self.gate_made = sig(f"moe{l}_gate_made")
                self.up_made = sig(f"moe{l}_up_made")
                self.hidden_turned = sig(f"moe{l}_hidden_turned")
                self.hidden_kept = sig(f"moe{l}_hidden_kept")
                self.gated = sig(f"moe{l}_gated")
                self.multiplied = sig(f"moe{l}_multiplied")
                self.y_done = sig(f"moe{l}_y_done")
                self.y_kept = sig(f"moe{l}_y_kept")
                self.index_g = sig(f"moe{l}_index_g")
                self.index_s = sig(f"moe{l}_index_s")
                self.gathered = sig(f"moe{l}_gathered")
                self.scattered = sig(f"moe{l}_scattered")
                self.stored = sig(f"moe{l}_stored")
                self.first = len(loads)
                for e in range(EXPERTS):
                    done = (self.expert_done, e + 1)
                    plan(columns(w["moe_w_gate"][l][e], 0, FF), (KD, FF), done)
                    plan(columns(w["moe_w_up"][l][e], 0, FF), (KD, FF), done)
                    plan(columns(w["moe_w_down"][l][e], 0, D), (FT, D), done)
                NT, NB = self.NT, self.NB
                take = carver()

                def tiles(n):
                    return take(NT * n).rearrange("p (t n) -> p t n", t=NT)
                self.ROWS = [take(D) for _ in range(2)]
                self.PAIRS = [take(2 * D).rearrange("p (c d) -> p c d", c=2) for _ in range(2)]
                self.SUM = take(D)
                self.LOG = tiles(36)
                self.M1, self.M2 = tiles(1), tiles(1)
                self.GP, self.GB, self.CG, self.OG = (tiles(GROUPS) for _ in range(4))
                self.GW, self.GS = tiles(1), tiles(1)
                self.TMP = tiles(EXPERTS)
                self.EL, self.EB, self.ES, self.CE = (tiles(PER_GROUP) for _ in range(4))
                self.OE = [tiles(PER_GROUP) for _ in range(2)]
                self.WT = [tiles(1) for _ in range(2)]
                self.WS = tiles(1)
                self.O32 = [tiles(EXPERTS) for _ in range(2)]
                self.BOTH = tiles(EXPERTS)
                self.RANK = [tiles(1) for _ in range(2)]
                self.QUOT = [tiles(1) for _ in range(2)]
                self.BLK = [tiles(1) for _ in range(2)]
                self.CNT, self.NBLK = take(P), take(P)
                self.FIRST = take(EXPERTS + 1)
                self.FIRSTI = take(EXPERTS + 1).bitcast(I32)
                self.AT_PLACE = [[take(CAP) for _ in range(2)] for _ in range(NT)]
                self.AT_BLOCK = [[take(2 * NB).rearrange("p (c b) -> p c b", c=2) for _ in range(2)] for _ in range(NT)]
                self.TAB, self.EMPTY = (take(2 * NB).rearrange("p (c b) -> p c b", c=2) for _ in range(2))
                self.TABI = take(2 * NB).bitcast(I32).rearrange("p (c b) -> p c b", c=2)
                self.IDXG, self.IDXS = take(1).bitcast(I32), take(1).bitcast(I32)
                self.XG = take(D)
                self.XGT = take(KD * CAP).rearrange("p (k t) -> p k t", k=KD)
                self.SG, self.H = take(FF), take(FF)
                self.HT = take(FT * CAP).rearrange("p (k t) -> p k t", k=FT)
                self.YS = take(D)

            def pe(self, L):
                pe, NT, NB = L.eng, self.NT, self.NB
                begin(L, "pe")
                router = vcol("router", KD * 36, self.l * KD * 36).rearrange("p (k n) -> p k n", k=KD)
                for t in range(NT):
                    for k in range(KD):
                        mm = pe.matmul(ps[:, 0, 36 * t:36 * t + 36], A[:, k, t * P:(t + 1) * P], router[:, k, :],
                                       start=k == 0, stop=k == KD - 1)
                L.inc(mm, self.logits)
                for t in range(NT):
                    if t >= 2:
                        L.wait(self.rows_kept, t - 1)
                    for k in range(KD):
                        mm = pe.transpose(ps[:, 1 + 2 * (t % 2) + k // 4, k % 4 * P:(k % 4 + 1) * P],
                                          A[:, k, t * P:(t + 1) * P], IDENT)
                    L.inc(mm, self.rows_turned)
                L.wait(self.chosen, 1)
                for t in range(NT):
                    for u in range(t + 1):
                        mm = pe.matmul(ps[:, 5, 32 * t:32 * t + 32], BEFORE if u == t else ONES, self.BOTH[:, u, :],
                                       start=u == 0, stop=u == t)
                L.inc(mm, self.ranks)
                for t in range(NT):
                    mm = pe.matmul(ps[0:EXPERTS, 6, 0:P], self.BOTH[:, t, :], ONES, start=t == 0, stop=t == NT - 1)
                L.inc(mm, self.counts)
                L.wait(self.counts_kept, 1)
                L.inc(pe.matmul(ps[:, 0, 0:EXPERTS + 1], self.NBLK[0:EXPERTS, :], BEFORE[0:EXPERTS, 0:EXPERTS + 1],
                                start=True, stop=True), self.firsts)
                for t in range(NT):
                    for c in range(2):
                        L.wait(self.places, 2 * t + c + 1)
                        mm = pe.matmul(ps[0:CAP, 6, 0:2 * NB], self.AT_PLACE[t][c],
                                       self.AT_BLOCK[t][c].rearrange("p c b -> p (c b)"),
                                       start=t + c == 0, stop=2 * t + c == 2 * NT - 1)
                L.inc(mm, self.table)

                def turn_block():
                    for k in range(KD):
                        mm = pe.transpose(ps[:, 3 + k // 4, k % 4 * CAP:(k % 4 + 1) * CAP], self.XG[0:CAP, k * P:(k + 1) * P],
                                          IDENT[0:CAP, 0:CAP])
                    mm.then_inc(self.block_turned.sem, 1)

                L.wait(self.rows_kept, NT)
                pe.wait_ge(self.gathered.sem, 16)
                turn_block()
                with pe.Fori(0, EXPERTS // 2) as pair:
                    for a in range(2):
                        lo, hi = self.range_of(pe, pair, a)
                        views = []
                        for j in range(3):
                            n = self.first + 3 * a + j
                            views.append(slot(n).rearrange("p (k n) -> p k n", k=KD if j < 2 else FT))
                            pe.wait_ge(slot_in[n % RING].sem, pair * 16 + arrivals[n])
                        gate, up, down = views
                        pe.sem_inc(spare.sem, 1)
                        with pe.Fori(lo, hi) as b:
                            pe.wait_ge(self.block_kept.sem, b + 1)
                            for bank, wv, made in ((0, gate, self.gate_made), (1, up, self.up_made)):
                                for k in range(KD):
                                    mm = pe.matmul(ps[0:CAP, bank, :], self.XGT[:, k, :], wv[:, k, :],
                                                   start=k == 0, stop=k == KD - 1)
                                mm.then_inc(made.sem, 1)
                            pe.wait_ge(self.gathered.sem, b * 16 + 32)
                            pe.sem_inc(spare.sem, 1)
                            turn_block()
                            pe.wait_ge(self.multiplied.sem, b + 1)
                            pe.sem_inc(spare.sem, 1)
                            for k in range(FT):
                                mm = pe.transpose(ps[:, 2 if k < 2 else 7, k % 2 * CAP:(k % 2 + 1) * CAP],
                                                  self.H[0:CAP, k * P:(k + 1) * P], IDENT[0:CAP, 0:CAP])
                                if k % 2:
                                    mm.then_inc(self.hidden_turned.sem, 1)
                            pe.wait_ge(self.y_kept.sem, b * 2 + 2)
                            pe.wait_ge(self.hidden_kept.sem, b * 2 + 2)
                            for half in range(2):
                                for k in range(FT):
                                    mm = pe.matmul(ps[0:CAP, 5 + half, :], self.HT[:, k, :], down[:, k, 512 * half:512 * (half + 1)],
                                                   start=k == 0, stop=k == FT - 1)
                                mm.then_inc(self.y_done.sem, 1)
                        pe.matmul(ps[0:1, 7, 0:1], ONES[:, 0:1], ONES[:, 0:1], start=True, stop=True).then_inc(self.expert_done.sem, 1)
                for t in range(NT):
                    L.wait(self.sum_made, t + 1)
                    if t >= 1:
                        L.wait(self.sum_added, t)
                    for k in range(KD):
                        mm = pe.transpose(ps[:, 5 + k // 4, k % 4 * P:(k % 4 + 1) * P], self.SUM[:, k * P:(k + 1) * P], IDENT)
                    L.inc(mm, self.sum_turned)
                end(L, "pe")

            def range_of(self, eng, pair, a):
                return tuple(eng.value_load(self.FIRSTI[0:1, bass.ds(pair * 2 + (a + i), 1)], min_val=i, max_val=self.NB - 2)
                             for i in range(2))

            def act(self, L):
                act, NT = L.eng, self.NT
                begin(L, "act")
                for t in range(NT):
                    L.wait(self.rows_turned, t + 1)
                    if t >= 2:
                        L.wait(self.rows_out[t % 2], 16)
                    L.inc(act.copy(self.ROWS[t % 2], ps[:, 1 + 2 * (t % 2):3 + 2 * (t % 2), :].rearrange("p b n -> p (b n)")),
                          self.rows_kept)
                    L.join()
                    act.dma_start(f_rows[t * P:(t + 1) * P, :], self.ROWS[t % 2]).then_inc(self.rows_out[t % 2].sem, 16)
                for s in (self.GP, self.ES):
                    L.wait(self.less_max, 1 if s is self.GP else 2)
                    L.inc(act.activation(s, s, ACT.Exp), self.exps)
                L.wait(self.table_kept, 1)
                with act.Fori(0, EXPERTS // 2) as pair:
                    for a in range(2):
                        lo, hi = self.range_of(act, pair, a)
                        with act.Fori(lo, hi) as b:
                            act.wait_ge(self.gate_made.sem, b + 1)
                            act.activation(self.SG[0:CAP], ps[0:CAP, 0, :], ACT.Silu).then_inc(self.gated.sem, 1)
                            act.wait_ge(self.hidden_turned.sem, b * 2 + 1)
                            act.copy(self.HT[:, 0:2, :].rearrange("p k t -> p (k t)"), ps[:, 2, 0:2 * CAP])\
                               .then_inc(self.hidden_kept.sem, 1)
                            act.wait_ge(self.y_done.sem, b * 2 + 1)
                            act.wait_ge(self.stored.sem, b + 1)
                            act.copy(self.YS[0:CAP, 0:512], ps[0:CAP, 5, :]).then_inc(self.y_kept.sem, 1)
                L.last = None
                L.wait(self.scattered_all, 1)
                for t in range(NT):
                    if t >= 2:
                        L.wait(self.sum_made, t - 1)
                    act.dma_start(self.PAIRS[t % 2], y_rows[2 * P * t:2 * P * (t + 1), :].rearrange("(p c) d -> p c d", c=2))\
                       .then_inc(self.pairs_in[t % 2].sem, 16)
                end(L, "act")

            def dve(self, L):
                v, NT, NB = L.eng, self.NT, self.NB
                begin(L, "dve")

                def lanes(ap, n):
                    return ap.to_broadcast([P, NT, n])

                def row(ap, n):
                    return ap.unsqueeze(1).to_broadcast([P, NT, n])

                def step(ins, signal=None):
                    L.inc(ins, signal)
                    L.join()

                def first_of_largest(values, n, cand, one_hot):
                    step(v.tensor_reduce(self.M1[:, :, 0], values, X, ALU.max))
                    step(v.tensor_tensor(cand, values, lanes(self.M1, n), ALU.is_ge))
                    step(v.scalar_tensor_tensor(out=cand, in0=cand, scalar=-64.0, in1=row(IOTA[:, 0:n], n),
                                                op0=ALU.mult, op1=ALU.add))
                    step(v.tensor_reduce(self.M1[:, :, 0], cand, X, ALU.min))
                    step(v.tensor_tensor(one_hot, cand, lanes(self.M1, n), ALU.is_equal))

                def softmax(values, out_ap, n, turn):
                    step(v.tensor_reduce(self.M1[:, :, 0], values, X, ALU.max))
                    step(v.tensor_tensor(out_ap, values, lanes(self.M1, n), ALU.subtract), self.less_max)
                    L.wait(self.exps, turn)
                    step(v.tensor_reduce(self.M1[:, :, 0], out_ap, X, ALU.add))
                    step(v.reciprocal(self.M2[:, :, 0], self.M1[:, :, 0]))
                    step(v.tensor_tensor(out_ap, out_ap, lanes(self.M2, n), ALU.mult))

                def pick(out_ap, values, weights, n):
                    t = self.TMP[:, :, 0:n]
                    step(v.tensor_tensor(t, values, weights, ALU.mult))
                    step(v.tensor_reduce(out_ap[:, :, 0], t, X, ALU.add))

                bias = vcol("router_bias", 36, 36 * self.l)
                L.wait(self.logits, 1)
                step(v.tensor_copy(self.LOG.rearrange("p t n -> p (t n)"), ps[:, 0, 0:36 * NT]), self.logits_kept)
                softmax(self.LOG[:, :, 0:GROUPS], self.GP, GROUPS, 1)
                step(v.tensor_tensor(self.GB, self.GP, row(bias[:, 0:GROUPS], GROUPS), ALU.add))
                first_of_largest(self.GB, GROUPS, self.CG, self.OG)
                pick(self.GW, self.GP, self.OG, GROUPS)
                by_group = self.TMP.rearrange("p t (g j) -> p t g j", g=GROUPS)
                by_expert = self.TMP.rearrange("p t (g j) -> p t j g", g=GROUPS)
                group4 = self.OG.unsqueeze(3).to_broadcast([P, NT, GROUPS, PER_GROUP])
                for o, values in ((self.EL, self.LOG[:, :, GROUPS:36].rearrange("p t (g j) -> p t g j", g=GROUPS)),
                                  (self.EB, bias[:, GROUPS:36].rearrange("p (g j) -> p g j", g=GROUPS).unsqueeze(1)
                                   .to_broadcast([P, NT, GROUPS, PER_GROUP]))):
                    step(v.tensor_tensor(by_group, values, group4, ALU.mult))
                    step(v.tensor_reduce(o, by_expert, X, ALU.add))
                softmax(self.EL, self.ES, PER_GROUP, 2)
                step(v.tensor_tensor(self.EB, self.ES, self.EB, ALU.add))
                for c in range(2):
                    first_of_largest(self.EB, PER_GROUP, self.CE, self.OE[c])
                    pick(self.WT[c], self.ES, self.OE[c], PER_GROUP)
                    step(v.scalar_tensor_tensor(out=self.EB, in0=self.OE[c], scalar=MASKED, in1=self.EB, op0=ALU.mult, op1=ALU.add))
                    step(v.tensor_tensor(self.O32[c].rearrange("p t (g j) -> p t g j", g=GROUPS),
                                         self.OE[c].unsqueeze(2).to_broadcast([P, NT, GROUPS, PER_GROUP]), group4, ALU.mult))
                step(v.tensor_tensor(self.BOTH, self.O32[0], self.O32[1], ALU.add), self.chosen)
                step(v.tensor_tensor(self.WS, self.WT[0], self.WT[1], ALU.add))
                step(v.reciprocal(self.WS, self.WS))
                step(v.tensor_tensor(self.WS, self.WS, self.GW, ALU.mult))
                for c in range(2):
                    step(v.tensor_tensor(self.WT[c], self.WT[c], self.WS, ALU.mult))
                L.wait(self.counts, 1)
                step(v.tensor_copy(self.CNT[0:EXPERTS, :], ps[0:EXPERTS, 6, 0:P]))
                step(v.tensor_scalar(self.NBLK[0:EXPERTS, :], self.CNT[0:EXPERTS, :], float(CAP), 1.0, ALU.is_gt, ALU.add))
                for r in range(2, self.T // CAP):
                    step(v.scalar_tensor_tensor(out=self.NBLK[0:EXPERTS, :], in0=self.CNT[0:EXPERTS, :], scalar=float(r * CAP),
                                                in1=self.NBLK[0:EXPERTS, :], op0=ALU.is_gt, op1=ALU.add))
                v.sem_inc(self.counts_kept.sem, 1)
                L.wait(self.firsts, 1)
                step(v.tensor_copy(self.FIRST, ps[:, 0, 0:EXPERTS + 1]))
                step(v.tensor_copy(self.FIRSTI, self.FIRST))
                for c in range(2):
                    step(v.tensor_tensor(self.TMP, ps[:, 5, 0:32 * NT].rearrange("p (t e) -> p t e", t=NT), self.O32[c], ALU.mult))
                    step(v.tensor_reduce(self.RANK[c][:, :, 0], self.TMP, X, ALU.add))
                    pick(self.BLK[c], row(self.FIRST[:, 0:EXPERTS], EXPERTS), self.O32[c], EXPERTS)
                    step(v.tensor_scalar(self.QUOT[c], self.RANK[c], float(CAP), None, ALU.is_ge))
                    for r in range(2, self.T // CAP):
                        step(v.scalar_tensor_tensor(out=self.QUOT[c], in0=self.RANK[c], scalar=float(r * CAP), in1=self.QUOT[c],
                                                    op0=ALU.is_ge, op1=ALU.add))
                    step(v.tensor_tensor(self.BLK[c], self.BLK[c], self.QUOT[c], ALU.add))
                    step(v.scalar_tensor_tensor(out=self.RANK[c], in0=self.QUOT[c], scalar=-float(CAP), in1=self.RANK[c],
                                                op0=ALU.mult, op1=ALU.add))
                for t in range(NT):
                    for c in range(2):
                        L.inc(v.tensor_scalar(self.AT_PLACE[t][c], IOTA[:, 0:CAP], self.RANK[c][:, t, :], None, ALU.is_equal))
                        L.inc(v.tensor_scalar(self.AT_BLOCK[t][c][:, 0, :], IOTA[:, 0:NB], self.BLK[c][:, t, :],
                                              PLACE[:, c, t:t + 1], ALU.is_equal, ALU.mult))
                        L.inc(v.tensor_scalar(self.AT_BLOCK[t][c][:, 1, :], IOTA[:, 0:NB], self.BLK[c][:, t, :],
                                              PLACE[:, 2, t:t + 1], ALU.is_equal, ALU.mult), self.places)
                L.wait(self.table, 1)
                tab = ps[0:CAP, 6, 0:2 * NB].rearrange("p (c b) -> p c b", c=2)
                step(v.tensor_scalar(self.EMPTY[0:CAP], tab, 0.5, OUT_OF_BOUNDS, ALU.is_lt, ALU.mult))
                step(v.scalar_tensor_tensor(out=self.TAB[0:CAP], in0=tab, scalar=-1.0, in1=self.EMPTY[0:CAP], op0=ALU.add, op1=ALU.add))
                step(v.tensor_copy(self.TABI[0:CAP], self.TAB[0:CAP]), self.table_kept)

                def keep_block():
                    v.tensor_copy(self.XGT.rearrange("p (b k) t -> p b (k t)", b=2), ps[:, 3:5, 0:4 * CAP]).then_inc(self.block_kept.sem, 1)

                v.wait_ge(self.block_turned.sem, 1)
                keep_block()
                with v.Fori(0, EXPERTS // 2) as pair:
                    for a in range(2):
                        lo, hi = self.range_of(v, pair, a)
                        with v.Fori(lo, hi) as b:
                            v.wait_ge(self.gated.sem, b + 1)
                            v.wait_ge(self.up_made.sem, b + 1)
                            v.tensor_tensor(self.H[0:CAP], self.SG[0:CAP], ps[0:CAP, 1, :], ALU.mult)\
                             .then_inc(self.multiplied.sem, 1)
                            v.wait_ge(self.hidden_turned.sem, b * 2 + 2)
                            v.sem_inc(spare.sem, 1)
                            v.tensor_copy(self.HT[:, 2:4, :].rearrange("p k t -> p (k t)"), ps[:, 7, 0:2 * CAP])\
                             .then_inc(self.hidden_kept.sem, 1)
                            v.wait_ge(self.block_turned.sem, b + 2)
                            v.sem_inc(spare.sem, 1)
                            keep_block()
                            v.wait_ge(self.y_done.sem, b * 2 + 2)
                            v.wait_ge(self.stored.sem, b + 1)
                            v.sem_inc(spare.sem, 1)
                            v.tensor_copy(self.YS[0:CAP, 512:D], ps[0:CAP, 6, :]).then_inc(self.y_kept.sem, 1)
                for t in range(NT):
                    L.wait(self.pairs_in[t % 2], 16 * (t // 2 + 1))
                    if t >= 1:
                        L.wait(self.sum_turned, t)
                    step(v.tensor_scalar(self.SUM, self.PAIRS[t % 2][:, 0, :], self.WT[0][:, t, :], None, ALU.mult))
                    step(v.scalar_tensor_tensor(out=self.SUM, in0=self.PAIRS[t % 2][:, 1, :], scalar=self.WT[1][:, t, :],
                                                in1=self.SUM, op0=ALU.mult, op1=ALU.add), self.sum_made)
                    L.wait(self.sum_turned, t + 1)
                    for k in range(KD):
                        xs = XT[:, k, t * P:(t + 1) * P]
                        ins = v.scalar_tensor_tensor(out=xs, in0=ps[:, 5 + k // 4, k % 4 * P:(k % 4 + 1) * P],
                                                     scalar=MOD[self.l][:, 5 * KD + k, t * P // TL:t * P // TL + 1], in1=xs,
                                                     op0=ALU.mult, op1=ALU.add)
                        L.inc(ins, self.sum_added if k == KD - 1 else None)
                end(L, "dve")

            def pool(self, L):
                g, NT = L.eng, self.NT
                g.sem_inc(self.y_kept.sem, 2)
                g.sem_inc(self.stored.sem, 1)
                L.wait(self.table_kept, 1)
                g.memset(self.XG[0:CAP], 0.0).then_inc(self.index_g.sem, 1)
                for i in range(2):
                    L.wait(self.rows_out[i], 16 * (NT // 2))
                blocks = g.value_load(self.FIRSTI[0:1, EXPERTS:EXPERTS + 1], min_val=EXPERTS, max_val=self.NB - 2)

                def gather(block, indices):
                    g.tensor_copy(self.IDXG[0:CAP], self.TABI[0:CAP, 1, block]).then_inc(self.index_g.sem, 1)
                    g.wait_ge(self.index_g.sem, indices + 1)
                    g.sem_inc(spare.sem, 1)
                    g.indirect_dma_start(out=self.XG[0:CAP], out_offset=None, in_=f_rows[:, :],
                                         in_offset=bass.IndirectOffsetOnAxis(ap=self.IDXG[0:CAP], axis=0),
                                         bounds_check=self.T - 1, oob_is_err=False).then_inc(self.gathered.sem, 16)

                gather(slice(0, 1), 1)
                g.wait_ge(self.gathered.sem, 16)
                g.wait_ge(self.block_turned.sem, 1)
                gather(slice(1, 2), 2)
                with g.Fori(0, blocks) as b:
                    g.wait_ge(self.gathered.sem, b * 16 + 32)
                    g.wait_ge(self.block_turned.sem, b + 2)
                    g.sem_inc(spare.sem, 1)
                    gather(bass.ds(b + 2, 1), b + 3)
                    g.tensor_copy(self.IDXS[0:CAP], self.TABI[0:CAP, 0, bass.ds(b, 1)]).then_inc(self.index_s.sem, 1)
                    g.wait_ge(self.index_s.sem, b + 1)
                    g.wait_ge(self.y_kept.sem, b * 2 + 4)
                    g.sem_inc(spare.sem, 1)
                    g.indirect_dma_start(out=y_rows[:, :], out_offset=bass.IndirectOffsetOnAxis(ap=self.IDXS[0:CAP], axis=0),
                                         in_=self.YS[0:CAP], in_offset=None, bounds_check=2 * self.T - 1,
                                         oob_is_err=False).then_inc(self.scattered.sem, 16)
                    g.wait_ge(self.scattered.sem, b * 16 + 16)
                    g.sem_inc(self.stored.sem, 1)
                g.wait_ge(self.gathered.sem, blocks * 16 + 32)
                g.sem_inc(self.scattered_all.sem, 1)

        take = carver()
        CG = take(4 * TL).rearrange("p (m t) -> p m t", m=4)
        CU = take(4 * (TL + 2)).rearrange("p (m t) -> p m t", m=4)
        CZ = take(4 * TL).rearrange("p (m t) -> p m t", m=4)
        BZ = take(KD * TL).rearrange("p (m t) -> p m t", m=KD)

        class Conv:
            def __init__(self):
                self.tiles = sig("conv_tiles")
                self.kept = sig("conv_kept")
                self.gate_in = sig("conv_gate_in")
                self.y_tiles = sig("conv_y_tiles")
                self.y_added = sig("conv_y_added")
                win = w["conv_w_in"][0]
                self.slots = []
                for half in range(2):
                    for part in (1, 2, 0):
                        c0 = part * D + half * 512
                        self.slots.append(plan(columns(win, c0, c0 + 512), (KD, 512), (self.tiles, 4 * len(self.slots) + 4)))
                self.wo = [plan(columns(w["conv_w_out"][0], 512 * i, 512 * (i + 1)), (KD, 512), (self.y_tiles, 4 * i + 4))
                           for i in range(2)]

            def pe(self, L):
                pe = L.eng
                begin(L, "pe")
                for s, n in enumerate(self.slots):
                    slot_ready(L, n)
                    wv = slot(n).rearrange("p (k n) -> p k n", k=KD)
                    for t in range(4):
                        i = 4 * s + t
                        if i >= 4:
                            if (s - 1) % 3 == 0:
                                L.wait(self.gate_in, 4 * ((s - 1) // 3) + t + 1)
                            else:
                                L.wait(self.kept, 4 * (2 * ((s - 1) // 3) + (s - 1) % 3 - 1) + t + 1)
                        for k in range(KD):
                            mm = pe.matmul(ps[:, t, 0:TL], wv[:, k, t * P:(t + 1) * P], A[:, k, 0:TL], start=k == 0, stop=k == KD - 1)
                        L.inc(mm, self.tiles)
                for m in range(KD):
                    if m % 4 == 0:
                        slot_ready(L, self.wo[m // 4])
                    if m == 0:
                        L.wait(self.kept, 16)
                    if m >= 4:
                        L.wait(self.y_added, m - 3)
                    wv = slot(self.wo[m // 4]).rearrange("p (k n) -> p k n", k=KD)
                    for k in range(KD):
                        mm = pe.matmul(ps[:, m % 4, 0:TL], wv[:, k, m % 4 * P:(m % 4 + 1) * P], BZ[:, k, :],
                                       start=k == 0, stop=k == KD - 1)
                    L.inc(mm, self.y_tiles)
                end(L, "pe")

            def act(self, L):
                begin(L, "act")
                for half in range(2):
                    for t in range(4):
                        L.wait(self.tiles, 12 * half + t + 1)
                        if half:
                            L.wait(self.kept, 8)
                        L.inc(L.eng.copy(CG[:, t, :], ps[:, t, 0:TL]), self.gate_in)
                end(L, "act")

            def dve(self, L):
                v = L.eng
                begin(L, "dve")
                taps = vcol("conv", 3 * KD).rearrange("p (j m) -> p j m", j=3)
                L.inc(v.memset(CU[:, :, 0:1], 0.0))
                L.inc(v.memset(CU[:, :, TL + 1:TL + 2], 0.0))
                L.join()
                for half in range(2):
                    for t in range(4):
                        L.wait(self.gate_in, 4 * half + t + 1)
                        L.wait(self.tiles, 12 * half + 4 + t + 1)
                        L.inc(v.tensor_tensor(CU[:, t, 1:TL + 1], CG[:, t, :], ps[:, t, 0:TL], ALU.mult), self.kept)
                    for t in range(4):
                        m = 4 * half + t
                        L.join()
                        L.inc(v.tensor_scalar(CZ[:, t, :], CU[:, t, 0:TL], taps[:, 0, m:m + 1], None, ALU.mult))
                        for j in (1, 2):
                            L.join()
                            L.inc(v.scalar_tensor_tensor(out=CZ[:, t, :], in0=CU[:, t, j:j + TL], scalar=taps[:, j, m:m + 1],
                                                         in1=CZ[:, t, :], op0=ALU.mult, op1=ALU.add))
                        L.wait(self.tiles, 12 * half + 8 + t + 1)
                        L.join()
                        L.inc(v.tensor_tensor(BZ[:, m, :], CZ[:, t, :], ps[:, t, 0:TL], ALU.mult), self.kept)
                gated_add(L, 1, 0, TL, self.y_tiles, self.y_added)
                end(L, "dve")

        take = carver()
        heads_at = arena_at
        H0 = take((AH + AKV + RH) * TL)

        def inside(at, heads):
            return H0[0:HD, at:at + heads * TL].rearrange("p (h t) -> p h t", h=heads)
        QA, KA, QT = inside(0, AH), inside(AH * TL, AKV), inside((AH + AKV) * TL, RH)
        KR = take(RH * TL)[0:HD].rearrange("p (h t) -> p h t", h=RH)
        VA = take(2 * P).rearrange("p (t c) -> p t c", t=2)
        VR = take(2 * 512).rearrange("p (t c) -> p t c", t=2)
        GR = take(4 * TL).rearrange("p (m t) -> p m t", m=4)
        RAW = [take(TL) for _ in range(2)]
        R1, R2 = take(TL), take(TL)
        SC = [take(3 * P) for _ in range(2)]
        PT = [take(3 * P) for _ in range(2)]
        SM = take(16)
        HS = place("HS", [P, 2, FFT, TL], F32R, heads_at)
        XS = place("XS", [P, 2, KD, TL], F32R, A_at)
        WS = place("WS", [P, 2, UNITS, UNIT], F32R, ring_at + 4 * RING_2 * SLOT)
        SA = [take(TL) for _ in range(2)]
        HF = [take(TL) for _ in range(2)]
        MIXC = take(4 * TL + 3 * P + 3 * P + P + RH * TL)
        Y = A[:, 0:4, :].rearrange("p k t -> p (k t)").rearrange("p (m t) -> p m t", m=KD)
        O4 = A[:, 4:6, :].rearrange("p k t -> p (k t)").rearrange("p (m t) -> p m t", m=4)
        O2 = A[:, 6:8, :].rearrange("p k t -> p (k t)").rearrange("p (m t) -> p m t", m=4)
        COS_A, SIN_A, COS_R, SIN_R = (MIXC[:, i * TL:(i + 1) * TL] for i in range(4))
        TURN_A, TURN_R, HEAD_MEAN = (MIXC[:, 4 * TL + i * P:4 * TL + (i + 1) * P] for i in range(3))
        MASK = MIXC[:, 4 * TL + 3 * P:4 * TL + 6 * P]
        MEAN = MIXC[:, 4 * TL + 6 * P:4 * TL + 7 * P]
        DECAY = MIXC[:, 4 * TL + 7 * P:].rearrange("p (h t) -> p h t", h=RH)
        LNP = sb("LNP", [P, 6 * KD + AH])
        SINK = LNP[:, 6 * KD:]

        def high(ap):
            return ap.bitcast(F32)

        class Ffn:

            def __init__(self, i, gu, dn):
                self.i, self.gu, self.dn = i, gu, dn
                self.w_high = shared("split_high", FFN_UNITS, 2)
                self.w_split = shared("split_ready", FFN_UNITS, 2)
                self.w_used = shared("split_used", FFN_UNITS, 2)
                self.x_high = shared("ffn_x_high", KD, 2)
                self.x_split = shared("ffn_x_split", KD, 2)
                self.silu = shared("ffn_silu", FFT, 2)
                self.hidden = shared("ffn_hidden", FFT, 2)
                self.h_high = shared("ffn_h_high", FFT, 2)
                self.h_split = shared("ffn_h_split", FFT, 2)
                self.y_added = shared("ffn_y_added", KD, 2)

            def plan(self, l):
                gu = w[self.gu][l].rearrange("(k p) (a n) -> p k a n", p=P, a=2)
                first = len(loads)
                for s in range(FFT // 2):
                    plan(gu[:, :, :, 2 * P * s:2 * P * (s + 1)], (KD, 2, 2 * P), (self.w_split, 4 * s + 4, l))
                for m in range(KD):
                    plan(columns(w[self.dn][l], P * m, P * (m + 1)), (FFT, P), (self.w_split, 2 * FFT + 3 * m + 3, l))
                if l == 0:
                    self.first = first

            def unit(self, u):
                if u < 2 * FFT:
                    f, a = u // 2, u % 2
                    n = self.first + f // 2
                    wv = slot(n).rearrange("p (k a n) -> p k a n", k=KD, a=2)
                    return n, wv[:, :, a, f % 2 * P:(f % 2 + 1) * P], range(KD)
                m, third = (u - 2 * FFT) // 3, (u - 2 * FFT) % 3
                n = self.first + FFT // 2 + m
                tiles = range(KD * third, min(KD * (third + 1), FFT))
                wv = slot(n)[:, 0:FFT * P].rearrange("p (k n) -> p k n", k=FFT)
                return n, wv[:, tiles.start:tiles.stop, :], tiles

            def parts(self, u):
                count = len(self.unit(u)[2])
                return [WS[:, j, u % UNITS, 0:count * P].rearrange("p (k n) -> p k n", k=count) for j in range(2)]

            def units_used(self, L, count):
                L.wait(self.w_used, count + UNITS)

            def pe(self, L):
                begin(L, "pe")

                def products(u, out_ap, moving):
                    L.wait(self.w_split, u + 1)
                    wh, wl = self.parts(u)
                    tiles = self.unit(u)[2]
                    total = KD if u < 2 * FFT else FFT
                    for i, k in enumerate(tiles):
                        if u < 2:
                            L.wait(self.x_split, k + 1)
                        elif 2 * FFT <= u < 2 * FFT + 3:
                            L.wait(self.h_split, k + 1)
                        for weights, j in ((wh, 0), (wh, 1), (wl, 0)):
                            mm = L.eng.matmul(out_ap, weights[:, i, :], moving[:, j, k, :], start=k == 0 and weights is wh and j == 0,
                                              stop=k == total - 1 and weights is wl)
                    L.inc(mm, self.w_used)

                for f in range(FFT):
                    if f >= 2:
                        L.wait(self.hidden, f - 1)
                    for a in range(2):
                        products(2 * f + a, ps[:, 2 * (f % 2) + a, 0:TL], XS)
                for m in range(KD):
                    if m >= 4:
                        L.wait(self.y_added, m - 3)
                    for third in range(3):
                        products(2 * FFT + 3 * m + third, ps[:, 4 + m % 4, 0:TL], HS)
                end(L, "pe")

            def act(self, L):
                act = L.eng

                def round_weights(u):
                    if u < FFN_UNITS:
                        n, source, _ = self.unit(u)
                        slot_ready(L, n)
                        self.units_used(L, u + 1 - UNITS)
                        L.inc(act.copy(self.parts(u)[0], source), self.w_high)

                for u in range(UNITS):
                    round_weights(u)
                begin(L, "act")
                for k in range(KD):
                    L.inc(act.copy(XS[:, 0, k, :], XT[:, k, 0:TL]), self.x_high)
                for f in range(FFT):
                    round_weights(UNITS + 2 * f)
                    self.units_used(L, 2 * f + 1)
                    if f >= 2:
                        L.wait(self.hidden, f - 1)
                    L.inc(act.activation(SA[f % 2], ps[:, 2 * (f % 2), 0:TL], ACT.Silu), self.silu)
                    round_weights(UNITS + 2 * f + 1)
                    L.wait(self.hidden, f + 1)
                    L.inc(act.copy(HS[:, 0, f, :], HF[f % 2]), self.h_high)
                for u in range(UNITS + 2 * FFT, FFN_UNITS):
                    round_weights(u)
                end(L, "act")

            def dve(self, L):
                v = L.eng

                def split_weights(u):
                    if u < FFN_UNITS:
                        wh, wl = self.parts(u)
                        L.wait(self.w_high, u + 1)
                        L.inc(v.tensor_tensor(wl, self.unit(u)[1], high(wh), ALU.subtract), self.w_split)

                for u in range(UNITS):
                    split_weights(u)
                begin(L, "dve")
                for k in range(KD):
                    L.wait(self.x_high, k + 1)
                    L.inc(v.tensor_tensor(XS[:, 1, k, :], XT[:, k, 0:TL], high(XS[:, 0, k, :]), ALU.subtract), self.x_split)
                for f in range(FFT):
                    split_weights(UNITS + 2 * f)
                    L.wait(self.silu, f + 1)
                    self.units_used(L, 2 * f + 2)
                    if f >= 2:
                        L.wait(self.h_split, f - 1)
                    L.inc(v.tensor_tensor(HF[f % 2], SA[f % 2], ps[:, 2 * (f % 2) + 1, 0:TL], ALU.mult), self.hidden)
                    split_weights(UNITS + 2 * f + 1)
                    L.wait(self.h_high, f + 1)
                    L.inc(v.tensor_tensor(HS[:, 1, f, :], HF[f % 2], high(HS[:, 0, f, :]), ALU.subtract), self.h_split)
                for m in range(KD):
                    for third in range(3):
                        split_weights(2 * FFT + UNITS + 3 * m + third)
                    self.units_used(L, 2 * FFT + 3 * m + 3)
                    L.inc(v.scalar_tensor_tensor(out=XT[:, m, 0:TL], in0=ps[:, 4 + m % 4, 0:TL], scalar=0.5 / ALPHA,
                                                 in1=XT[:, m, 0:TL], op0=ALU.mult, op1=ALU.add), self.y_added)
                end(L, "dve")

        def residual(L, tiles, added, scale):
            for m in range(KD):
                L.wait(tiles, m + 1)
                L.inc(L.eng.scalar_tensor_tensor(out=XT[:, m, 0:TL], in0=ps[:, m % 4, 0:TL], scalar=scale,
                                                 in1=XT[:, m, 0:TL], op0=ALU.mult, op1=ALU.add), added)

        class Mixer:

            ROTATED = ([("qa", t) for t in range(4)] + [("ka", 0)] + [("qr", t) for t in range(4)] + [("kr", t) for t in range(4)])

            def __init__(self):
                self.tiles = sig("mix_tiles", 13)
                self.raw = sig("mix_raw", 13)
                self.turned = sig("mix_turned", 13)
                self.rotated = sig("mix_rotated", 13)
                self.values = sig("mix_values", 4)
                self.values_kept = sig("mix_values_kept", 4)
                self.gates = sig("mix_gates", 4)
                self.gates_kept = sig("mix_gates_kept", 4)
                self.scores = sig("mix_scores", AH)
                self.neg = sig("mix_neg", AH)
                self.exps = sig("mix_exps", 3 * AH)
                self.probs = sig("mix_probs", AH)
                self.p_turned = sig("mix_p_turned", AH)
                self.p_kept = sig("mix_p_kept", AH)
                self.outs = sig("mix_outs", AH)
                self.outs_kept = sig("mix_outs_kept", AH)
                self.r_scores = sig("mix_r_scores", RH)
                self.decayed = sig("mix_decayed", RH)
                self.r_outs = sig("mix_r_outs", RH)
                self.r_outs_kept = sig("mix_r_outs_kept", RH)
                self.means = sig("mix_means", 4)
                self.centred = sig("mix_centred", 4)
                self.squares = sig("mix_squares", 4)
                self.vars = sig("mix_vars", 4)
                self.var = sig("mix_var", 4)
                self.std = sig("mix_std", 4)
                self.y_ready = sig("mix_y_ready", 4)
                self.y_tiles = sig("mix_y_tiles", KD)
                self.y_added = sig("mix_y_added", KD)

            def plan(self, l):
                first = len(loads)
                win = w["w_in_2"][l]
                for c0, c1, freed in ((0, 512, (self.tiles, 4, l)), (512, 768, (self.values, 2, l)),
                                      (768, 1280, (self.tiles, 9, l)), (1280, 1792, (self.tiles, 13, l)),
                                      (1792, 2304, (self.values, 4, l)), (2304, 2816, (self.gates, 4, l))):
                    plan(columns(win, c0, c1), (KD, c1 - c0), freed)
                for i in range(4):
                    plan(columns(w["w_out_2"][l], 256 * i, 256 * (i + 1)), (KD, 256), (self.y_tiles, 2 * i + 2, l))
                if l == 0:
                    self.first = first

            def weights(self, j, width):
                return slot(self.first + j)[:, 0:KD * width].rearrange("p (k n) -> p k n", k=KD)

            def pe(self, L):
                pe = L.eng
                begin(L, "pe")

                def turn(i):
                    L.wait(self.raw, i + 1)
                    if i >= 2:
                        L.wait(self.rotated, i - 1)
                    L.inc(pe.matmul(ps[:, 2 + i % 2, 0:TL], TURN_A if i < 5 else TURN_R, RAW[i % 2], start=True, stop=True), self.turned)

                def values(count, wv, width):
                    for t in range(2):
                        for k in range(KD):
                            mm = pe.matmul(ps[:, 4 + t, 0:width], XT[:, k, t * P:(t + 1) * P], wv[:, k, :], start=k == 0, stop=k == KD - 1)
                        L.inc(mm, self.values)

                for i, (part, t) in enumerate(self.ROTATED):
                    j = {"qa": 0, "ka": 1, "qr": 2, "kr": 3}[part]
                    if t == 0:
                        slot_ready(L, self.first + j)
                    wv = self.weights(j, 256 if j == 1 else 512)
                    if i >= 2:
                        L.wait(self.raw, i - 1)
                    for k in range(KD):
                        mm = pe.matmul(ps[:, i % 2, 0:TL], wv[:, k, t * P:(t + 1) * P], XT[:, k, 0:TL], start=k == 0, stop=k == KD - 1)
                    L.inc(mm, self.tiles)
                    if i:
                        turn(i - 1)
                    if part == "ka":
                        values(0, wv[:, :, P:2 * P], P)
                turn(12)
                slot_ready(L, self.first + 4)
                L.wait(self.values_kept, 2)
                values(2, self.weights(4, 512), 512)
                slot_ready(L, self.first + 5)
                wv = self.weights(5, 512)
                L.wait(self.raw, 13)
                for t in range(4):
                    if t >= 2:
                        L.wait(self.gates_kept, t - 1)
                    for k in range(KD):
                        mm = pe.matmul(ps[:, t % 2, 0:TL], wv[:, k, t * P:(t + 1) * P], XT[:, k, 0:TL], start=k == 0, stop=k == KD - 1)
                    L.inc(mm, self.gates)

                def scores(h):
                    b = h % 2
                    if h >= 2:
                        L.wait(self.probs, h - 1)
                    pe.matmul(ps[:, b, 0:P], QA[:, h, 0:P], KA[:, h // 4, 0:P], start=True, stop=True)
                    L.inc(pe.matmul(ps[:, b, P:3 * P], QA[:, h, P:TL], KA[:, h // 4, :], start=True, stop=True), self.scores)

                def finish(h):
                    b = h % 2
                    L.wait(self.probs, h + 1)
                    if h >= 2:
                        L.wait(self.p_kept, h - 1)
                    for c in range(3):
                        mm = pe.transpose(ps[:, 2 + b, c * P:(c + 1) * P], SC[b][:, c * P:(c + 1) * P], IDENT)
                    L.inc(mm, self.p_turned)
                    L.wait(self.p_kept, h + 1)
                    if h >= 2:
                        L.wait(self.outs_kept, h - 1)
                    kv = slice(h // 4 * HD, (h // 4 + 1) * HD)
                    pe.matmul(ps[0:HD, 4 + b, 0:P], VA[:, 0, kv], PT[b][:, 0:P], start=True, stop=True)
                    for c in range(2):
                        mm = pe.matmul(ps[0:HD, 4 + b, P:TL], VA[:, c, kv], PT[b][:, (1 + c) * P:(2 + c) * P], start=c == 0, stop=c == 1)
                    L.inc(mm, self.outs)

                L.wait(self.rotated, 13)
                L.wait(self.values_kept, 4)
                L.wait(self.gates_kept, 4)
                scores(0)
                for h in range(1, AH):
                    scores(h)
                    finish(h - 1)
                finish(AH - 1)

                def r_scores(h):
                    b = h % 2
                    if h >= 2:
                        L.wait(self.decayed, h - 1)
                    pe.matmul(ps[:, b, 0:TL], KR[:, h, 0:P], QT[:, h, :], start=True, stop=True)
                    L.inc(pe.matmul(ps[:, b, TL:3 * P], KR[:, h, P:TL], QT[:, h, P:TL], start=True, stop=True), self.r_scores)

                def r_finish(h):
                    b = h % 2
                    L.wait(self.decayed, h + 1)
                    if h >= 2:
                        L.wait(self.r_outs_kept, h - 1)
                    e = slice(h * HD, (h + 1) * HD)
                    pe.matmul(ps[0:HD, 2 + b, 0:P], VR[:, 0, e], SC[b][:, 0:P], start=True, stop=True)
                    pe.matmul(ps[0:HD, 2 + b, P:TL], VR[:, 0, e], SC[b][:, P:TL], start=True, stop=False)
                    L.inc(pe.matmul(ps[0:HD, 2 + b, P:TL], VR[:, 1, e], SC[b][:, TL:3 * P], start=False, stop=True), self.r_outs)

                L.wait(self.outs_kept, AH)
                r_scores(0)
                for h in range(1, RH):
                    r_scores(h)
                    r_finish(h - 1)
                r_finish(RH - 1)
                for m in range(4):
                    L.wait(self.r_outs_kept, 2 * m + 2)
                    if m >= 2:
                        L.wait(self.centred, m - 1)
                    L.inc(pe.matmul(ps[:, 4 + m % 2, (m // 2) * TL:(m // 2 + 1) * TL], HEAD_MEAN, O4[:, m, :], start=True, stop=True), self.means)
                L.wait(self.decayed, RH)
                for m in range(4):
                    L.wait(self.squares, m + 1)
                    if m >= 2:
                        L.wait(self.var, m - 1)
                    L.inc(pe.matmul(ps[:, m % 2, (m // 2) * TL:(m // 2 + 1) * TL], HEAD_MEAN, O2[:, m, :], start=True, stop=True), self.vars)
                L.wait(self.y_ready, 4)
                for m in range(KD):
                    if m % 2 == 0:
                        slot_ready(L, self.first + 6 + m // 2)
                    if m >= 4:
                        L.wait(self.y_added, m - 3)
                    wv = self.weights(6 + m // 2, 256)
                    for k in range(KD):
                        mm = pe.matmul(ps[:, m % 4, 0:TL], wv[:, k, m % 2 * P:(m % 2 + 1) * P], Y[:, k, :], start=k == 0, stop=k == KD - 1)
                    L.inc(mm, self.y_tiles)
                end(L, "pe")

            def act(self, L):
                act = L.eng
                begin(L, "act")
                for i, (part, t) in enumerate(self.ROTATED):
                    L.wait(self.tiles, i + 1)
                    if i >= 2:
                        L.wait(self.rotated, i - 1)
                    scale = HD ** -0.5 if part in ("qa", "kr") else 1.0
                    L.inc(act.activation(RAW[i % 2], ps[:, i % 2, 0:TL], ACT.Copy, scale=scale), self.raw)
                    if part == "qr" and t == 0:
                        for t2 in range(2):
                            L.wait(self.values, t2 + 1)
                            L.inc(act.copy(VA[:, t2, :], ps[:, 4 + t2, 0:P]), self.values_kept)
                for t in range(2):
                    L.wait(self.values, 3 + t)
                    L.inc(act.copy(VR[:, t, :], ps[:, 4 + t, :]), self.values_kept)
                for t in range(4):
                    L.wait(self.gates, t + 1)
                    L.inc(act.activation(GR[:, t, :], ps[:, t % 2, 0:TL], ACT.Silu), self.gates_kept)

                def keep_out(h, source, tile, signal):
                    half = slice(h % 2 * HD, (h % 2 + 1) * HD)
                    L.inc(act.copy(tile[half, h // 2, :], source), signal)

                for h in range(AH):
                    b = h % 2
                    L.wait(self.neg, h + 1)
                    for c, cols in enumerate((slice(0, P), slice(P, 3 * P))):
                        L.inc(act.activation(SC[b][:, cols], SC[b][:, cols], ACT.Exp, bias=SM[:, 4 + c:5 + c],
                                             accum_out=SM[:, 6 + c:7 + c]), self.exps)
                    L.inc(act.activation(SM[:, 8:10], SM[:, 4:6], ACT.Exp, bias=SINK[:, h:h + 1]), self.exps)
                    if h:
                        L.wait(self.outs, h)
                        keep_out(h - 1, ps[0:HD, 4 + (h - 1) % 2, 0:TL], Y, self.outs_kept)
                L.wait(self.outs, AH)
                keep_out(AH - 1, ps[0:HD, 4 + (AH - 1) % 2, 0:TL], Y, self.outs_kept)
                for h in range(RH):
                    L.wait(self.r_outs, h + 1)
                    keep_out(h, ps[0:HD, 2 + h % 2, 0:TL], O4, self.r_outs_kept)
                for m in range(4):
                    L.wait(self.centred, m + 1)
                    L.inc(act.activation(O2[:, m, :], O4[:, m, :], ACT.Square), self.squares)
                for m in range(4):
                    L.wait(self.var, m + 1)
                    L.inc(act.activation(O2[:, m, :], O2[:, m, :], ACT.Sqrt), self.std)
                end(L, "act")

            def dve(self, L):
                v = L.eng
                begin(L, "dve")
                for i, (part, t) in enumerate(self.ROTATED):
                    cos, sin = (COS_A, SIN_A) if i < 5 else (COS_R, SIN_R)
                    L.wait(self.raw, i + 1)
                    L.inc(v.tensor_tensor(R1, RAW[i % 2], cos, ALU.mult))
                    L.wait(self.turned, i + 1)
                    L.inc(v.tensor_tensor(R2, ps[:, 2 + i % 2, 0:TL], sin, ALU.mult))
                    L.join()
                    to = {"qa": QA, "ka": KA, "qr": QT, "kr": KR}[part]
                    L.inc(v.tensor_tensor(to[:, 2 * t, :], R1[0:HD], R2[0:HD], ALU.add))
                    L.inc(v.tensor_tensor(to[:, 2 * t + 1, :], R1[HD:P], R2[HD:P], ALU.add), self.rotated)
                    L.join()
                for h in range(AH):
                    b = h % 2
                    L.wait(self.scores, h + 1)
                    if h >= 2:
                        L.wait(self.p_turned, h - 1)
                    L.inc(v.tensor_tensor(SC[b], ps[:, b, 0:3 * P], MASK, ALU.add))
                    L.join()
                    L.inc(v.tensor_reduce(SM[:, 0:1], SC[b][:, 0:P], X, ALU.max))
                    L.inc(v.tensor_reduce(SM[:, 1:2], SC[b][:, P:3 * P], X, ALU.max))
                    L.join()
                    L.inc(v.tensor_scalar(SM[:, 4:6], SM[:, 0:2], SINK[:, h:h + 1], -1.0, ALU.max, ALU.mult), self.neg)
                    L.wait(self.exps, 3 * h + 3)
                    L.inc(v.tensor_tensor(SM[:, 10:12], SM[:, 6:8], SM[:, 8:10], ALU.add))
                    L.join()
                    L.inc(v.reciprocal(SM[:, 12:14], SM[:, 10:12]))
                    L.join()
                    L.inc(v.tensor_scalar(SC[b][:, 0:P], SC[b][:, 0:P], SM[:, 12:13], None, ALU.mult))
                    L.inc(v.tensor_scalar(SC[b][:, P:3 * P], SC[b][:, P:3 * P], SM[:, 13:14], None, ALU.mult), self.probs)
                    L.wait(self.p_turned, h + 1)
                    L.inc(v.tensor_copy(PT[b], ps[:, 2 + b, 0:3 * P]), self.p_kept)
                for h in range(RH):
                    b = h % 2
                    L.wait(self.r_scores, h + 1)
                    if h >= 2:
                        L.wait(self.r_outs, h - 1)
                    L.inc(v.tensor_tensor(SC[b][:, 0:TL], ps[:, b, 0:TL], DECAY[:, h, :], ALU.mult))
                    L.inc(v.tensor_tensor(SC[b][:, TL:3 * P], ps[:, b, TL:3 * P], DECAY[:, h, 0:P], ALU.mult), self.decayed)

                def half_bank(m, bank):
                    return ps[:, bank + m % 2, (m // 2) * TL:(m // 2 + 1) * TL]
                for m in range(4):
                    L.wait(self.means, m + 1)
                    L.inc(v.tensor_tensor(O4[:, m, :], O4[:, m, :], half_bank(m, 4), ALU.subtract), self.centred)
                for m in range(4):
                    L.wait(self.vars, m + 1)
                    L.inc(v.tensor_scalar(O2[:, m, :], half_bank(m, 0), GN_EPS, None, ALU.add), self.var)
                for m in range(4):
                    L.wait(self.std, m + 1)
                    L.inc(v.reciprocal(O2[:, m, :], O2[:, m, :]))
                    L.inc(v.tensor_tensor(O4[:, m, :], O4[:, m, :], GR[:, m, :], ALU.mult))
                    L.join()
                    L.inc(v.tensor_tensor(Y[:, 4 + m, :], O4[:, m, :], O2[:, m, :], ALU.mult), self.y_ready)
                residual(L, self.y_tiles, self.y_added, 1.0 / ALPHA)
                end(L, "dve")

        mods = [None, None]
        mods[0] = Mod(0)
        norms = [Norm("norm0", 0, 0, TA), Norm("norm1", 0, 1, TA), Norm("norm2", 1, 0, TL), Norm("norm3", 1, 1, TL),
                 Norm("norm4", 1, 2, TL)]
        mla = Mla()
        moes = [None, None]
        moes[0] = Moe(0, TA)
        mods[1] = Mod(1)
        conv = Conv()
        moes[1] = Moe(1, TL)
        layer_first = len(loads)
        second_stack.append(layer_first)
        ffns = [Ffn(0, "ffn1_w_gu_2", "ffn1_w_down_2"), Ffn(1, "ffn2_w_gu_2", "ffn2_w_down_2")]
        mixer = Mixer()
        for l in range(LAYERS):
            before_layer = [s.n for s in slot_in]
            ffns[0].plan(l)
            mixer.plan(l)
            ffns[1].plan(l)
            for s, count in zip(slot_in, before_layer):
                s.per_turn = s.n - count
        assert (len(loads) - layer_first) % (RING_2 * LAYERS) == 0
        lns = [LayerNorm(i) for i in range(3)]
        first_stack = [mods[0], norms[0], mla, norms[1], moes[0], mods[1], norms[2], conv, norms[3], moes[1], norms[4]]
        layer = [ffns[0], lns[0], mixer, lns[1], ffns[1], lns[2]]
        assert len(layer) == PER_LAYER_STAGES

        block = ctx.enter_context(nc.Block())

        @block.sync
        def _(sp):
            sp.dma_start(VECS[:, :], vec).then_inc(const_in.sem, 16)
            sp.dma_start(BASE[:, :], base_c).then_inc(const_in.sem, 16)

            def load(n):
                if before[n] is not None:
                    sp.wait_ge(*frees[before[n]])
                for dst, src in loads[n]:
                    sp.dma_start(dst, src).then_inc(slot_in[place_of[n]].sem, 16)

            n = 0
            while n < len(loads):
                moe = next((m for m in moes if m.first == n - RING), None)
                if moe is None:
                    load(n)
                    n += 1
                    if n == RING:
                        sp.dma_start(XT[:, :, :], xT).then_inc(x_in.sem, 16)
                        sp.dma_start(MLAC, mla_c).then_inc(mla_in.sem, 16)
                    continue
                with sp.Fori(0, EXPERTS // 2 - 1) as pair:
                    for a in range(2):
                        e = pair * 2 + (2 + a)
                        sp.wait_ge(moe.expert_done.sem, pair * 2 + (moe.expert_done.base + a + 1))
                        for j, name in enumerate(("moe_w_gate", "moe_w_up", "moe_w_down")):
                            dst = loads[n + 3 * a + j][0][0]
                            src = w[name][moe.l][bass.ds(e, 1)].rearrange("o (k p) n -> p (o k) n", p=P)
                            sp.dma_start(dst, src).then_inc(slot_in[(n + 3 * a + j) % RING].sem, 16)
                n += 3 * EXPERTS - RING
            sp.wait_ge(stages_done.sem, 3 * (len(first_stack) + 1 + LAYERS * len(layer)))
            sp.dma_start(out, XT[:, :, 0:TL]).then_inc(const_in.sem, 16)
            sp.wait_ge(const_in.sem, 48)

        @block.gpsimd
        def _(pool):
            L = Lane(pool, line["pool"], spare)
            for m in moes:
                m.pool(L)

        @block.scalar
        def _(act):
            L = Lane(act, line["act"], spare)
            act.wait_ge(const_in.sem, 32)
            L.inc(act.activation(COND.rearrange("p k a -> p (k a)") if False else COND[:, :, :],
                                 vcol("cond", 2 * KD).rearrange("p (k a) -> p k a", a=2), ACT.Silu))
            end(L, "act")
            for s in first_stack:
                s.act(L)
            L.eng.wait_ge(stages_done.sem, 3 * counters["act"])
            act.dma_start(MIXC, mix_c).then_inc(mix_in.sem, 16)
            L.line, L.last = loop_line["act"], None
            with act.Fori(0, LAYERS) as l:
                L.turn = l
                for s in layer:
                    s.act(L)
            assert loop_line["act"].n == ACT_PER_LAYER, loop_line["act"].n

        @block.tensor
        def _(pe):
            L = Lane(pe, line["pe"], spare)
            end(L, "pe")
            for s in first_stack:
                s.pe(L)
            pe.wait_ge(mix_in.sem, 16)
            pe.sem_inc(ffns[0].w_used.sem, UNITS)
            with pe.Fori(0, LAYERS) as l:
                L.turn = l
                for s in layer:
                    s.pe(L)

        @block.vector
        def _(dve):
            L = Lane(dve, line["dve"], spare)
            end(L, "dve")
            for s in first_stack:
                s.dve(L)
            dve.wait_ge(mix_in.sem, 16)
            L.line, L.last = loop_line["dve"], None
            with dve.Fori(0, LAYERS) as l:
                L.turn = l
                dve.wait_ge(stages_done.sem, l * (3 * PER_LAYER_STAGES) + 3 * counters["dve"])
                L.settle()
                L.inc(dve.tensor_copy(LNP[:, 0:6 * KD], VECS[:, bass.ds(l * (6 * KD) + VEC["ln"], 6 * KD)]))
                L.inc(dve.tensor_copy(SINK, VECS[:, bass.ds(l * AH + VEC["sinks"], AH)]))
                L.join()
                for s in layer:
                    s.dve(L)
            assert loop_line["dve"].n == DVE_PER_LAYER, loop_line["dve"].n


WEIGHTS = ["w_mod", "mla_w_dq", "mla_w_uq", "mla_w_dkv", "mla_w_ukv", "mla_w_o", "conv_w_in", "conv_w_out",
           "moe_w_gate", "moe_w_up", "moe_w_down", "w_in_2", "w_out_2",
           "ffn1_w_gu_2", "ffn1_w_down_2", "ffn2_w_gu_2", "ffn2_w_down_2"]


def lay_out(inputs):
    def features(a):
        a = np.asarray(a)
        a = a.reshape(-1, a.shape[-1] // P, P)
        return a.transpose(2, 0, 1).reshape(P, -1)

    def everywhere(a):
        return np.broadcast_to(np.asarray(a).reshape(1, -1), (P, np.asarray(a).size))

    a = {k: np.asarray(v) for k, v in inputs.items()}
    tokens = np.concatenate([a["x"][0], a["ctx"][0]], axis=0)
    xT = np.ascontiguousarray(tokens.T.reshape(KD, P, TA).transpose(1, 0, 2))
    cond = np.stack([a["c"][0], a["c_ctx"]], axis=1).reshape(KD, P, 2).transpose(1, 0, 2).reshape(P, -1)
    ln = np.stack([a[f"ln{i}_{s}_2"] for i in (1, 2, 3) for s in "gb"], axis=1)
    router = np.concatenate([a["moe_w_group"], a["moe_w_expert"]], axis=2).reshape(2, KD, P, 36)
    parts = {
        "cond": cond, "b_mod": features(a["b_mod"]), "norm_mix": features(a["norm_mix_g"]),
        "norm_ffn": features(a["norm_ffn_g"]), "final": features(a["final_norm_g"]), "g_q": features(a["mla_g_q"]),
        "g_kv": features(a["mla_g_kv"]), "conv": features(a["conv_w"][0]), "ln": features(ln),
        "router": router.transpose(2, 0, 1, 3).reshape(P, -1),
        "router_bias": everywhere(np.concatenate([a["moe_b_group"], a["moe_b_expert"]], axis=1)),
        "sinks": everywhere(a["attn_sinks_2"]),
    }
    return xT, np.ascontiguousarray(np.concatenate([parts[name] for name in VEC], axis=1))


def kernel(**inputs):
    import concourse.bacc as bacc
    from concourse.bass_utils import run_bass_kernel_spmd as run

    nc = bacc.Bacc("TRN2", target_bir_lowering=False, num_devices=1)
    arrays = {}

    def given(name, a):
        arrays[name] = np.ascontiguousarray(a)
        return nc.dram_tensor(name, arrays[name].shape, mybir.dt.from_np(arrays[name].dtype), kind="ExternalInput").ap()

    xT, vec = lay_out(inputs)
    base_c, mla_c, mix_c = shape_constants()
    args = [given("in_tokens", xT), given("in_vectors", vec), given("in_base", base_c), given("in_mla", mla_c),
            given("in_mix", mix_c)]
    weights = {name: given("in_" + name, inputs[name]) for name in WEIGHTS}
    out = nc.dram_tensor("out_features", (P, KD, TL), F32, kind="ExternalOutput").ap()
    program(nc, *args, weights, out)
    r = run(nc, [arrays], core_ids=[0])
    got = np.asarray(r.results[0]["out_features"])
    return np.ascontiguousarray(got.transpose(2, 1, 0).reshape(1, TL, D))
```

```python
from contextlib import ExitStack

import concourse.bass as bass
import numpy as np
from concourse import mybir

F32 = mybir.dt.float32
F32R = mybir.dt.float32r
I32 = mybir.dt.int32
ACT = mybir.ActivationFunctionType
ALU = mybir.AluOpType
X = mybir.AxisListType.X

P = 128
D = 1024
KD = D // P
TL = 256
TA = 512
NORM_EPS = 1e-6

HEADS = 8
Q_LORA, KV_LORA = 512, 256
NOPE, ROPE, DV = 128, 64, 128
QW = NOPE + ROPE
MLA_SCALE = float(QW) ** -0.5
GRID_W = 64

GROUPS, PER_GROUP = 4, 8
EXPERTS = GROUPS * PER_GROUP
FF = 512
FT = FF // P
CAP = 3 * P // 4
OUT_OF_BOUNDS = 4096.0

LAYERS = 2
D_FF = 2816
FFT = D_FF // P
HD = 64
AH, AKV, RH = 8, 2, 8
ALPHA = (2 * LAYERS) ** 0.25
LN_EPS, GN_EPS = 1e-5, 1e-6
MASKED = -1e30

RING = 6
SLOT = 4096
RING_2 = 4

UNIT = 1024
UNITS = (RING - RING_2) * SLOT // (2 * UNIT)
FFN_UNITS = 2 * FFT + KD * 3
BLOCK_UNITS = 3 * SLOT // UNIT
FIRST_BYTE = 16640


def blocks_of(tokens):
    return EXPERTS + 2 * tokens // (CAP + 1) + 2


def shape_constants():
    f = np.float32
    ident = np.eye(P, dtype=f)
    ones = np.ones((P, P), f)
    before = np.triu(np.ones((P, P), f), 1)
    iota = np.tile(np.arange(P, dtype=f), (P, 1))
    lane = np.arange(P)[:, None] + P * np.arange(4)[None, :]
    place = np.concatenate([2 * lane + 1, 2 * lane + 2, lane + 1], axis=1).astype(f)
    base = np.concatenate([ident, ones, before, iota, place], axis=1)

    def angles(pos, half, theta):
        freq = theta ** (-np.arange(half, dtype=f) / f(half))
        return (pos.astype(f)[:, None] * freq[None, :].astype(f)).astype(f)

    rows, cols = np.repeat(np.arange(TL // GRID_W), GRID_W), np.tile(np.arange(GRID_W), TL // GRID_W)
    quarter = ROPE // 4
    ang = np.concatenate([angles(p, quarter, f(10000.0)).T for p in (rows, rows, cols, cols)], axis=0)
    cos, sin = np.zeros((P, TA), f), np.zeros((P, TA), f)
    cos[:ROPE, :TL], sin[:ROPE, :TL] = np.cos(ang), np.sin(ang)
    cos[:ROPE, TL:] = 1.0
    turn = np.zeros((P, ROPE), f)
    for b in range(0, ROPE, 2 * quarter):
        for i in range(quarter):
            turn[b + quarter + i, b + i] = -1.0
            turn[b + i, b + quarter + i] = 1.0
    mla = np.concatenate([cos, sin, turn], axis=1)

    pos = np.arange(TL, dtype=f)
    half = HD // 2
    inv = (f(10000.0) ** (-np.arange(0, HD, 2, dtype=f) / f(HD))).astype(f)
    a = (pos[:, None] * inv[None, :]).astype(f).T
    a = np.concatenate([a, a, a, a], axis=0)
    inv = (f(1.0) / (f(10000.0) ** np.linspace(0.0, 1.0, half, dtype=f))).astype(f)
    r = (pos[:, None] * inv[None, :]).astype(f).T
    r = np.repeat(r, 2, axis=0)
    r = np.concatenate([r, r], axis=0)
    turn_a, turn_r = np.zeros((P, P), f), np.zeros((P, P), f)
    for b in range(0, P, HD):
        for i in range(half):
            turn_a[b + half + i, b + i] = -1.0
            turn_a[b + i, b + half + i] = 1.0
            turn_r[b + 2 * i + 1, b + 2 * i] = -1.0
            turn_r[b + 2 * i, b + 2 * i + 1] = 1.0
    head_mean = np.kron(np.eye(2, dtype=f), np.full((HD, HD), 1.0 / HD, f))
    q, k = np.arange(P)[:, None], np.arange(P)[None, :]
    own = np.where(q >= k, 0.0, MASKED).astype(f)
    prev = np.where(q - k + P < P, 0.0, MASKED).astype(f)
    mask = np.concatenate([own, prev, own], axis=1)
    log_gamma = np.log1p(-np.exp2(-5.0 - np.arange(RH, dtype=f))).astype(f)
    diff = np.arange(TL, dtype=f)[None, :] - np.arange(P, dtype=f)[:, None]
    decay = [np.where(diff >= 0, np.exp(np.maximum(diff, 0.0) * g), 0.0).astype(f) for g in log_gamma]
    mix = np.concatenate([np.cos(a), np.sin(a), np.cos(r), np.sin(r), turn_a, turn_r, head_mean, mask,
                          ones / f(D)] + decay, axis=1).astype(f)
    return base, mla, mix


VEC = {}
VEC_WIDTH = 0
for _name, _width in (("cond", 2 * KD), ("b_mod", 2 * 48), ("norm_mix", 2 * KD), ("norm_ffn", 2 * KD),
                      ("final", KD), ("g_q", 4), ("g_kv", 2), ("conv", 3 * KD), ("ln", LAYERS * 6 * KD),
                      ("router", 2 * KD * 36), ("router_bias", 2 * 36), ("sinks", LAYERS * AH)):
    VEC[_name] = VEC_WIDTH
    VEC_WIDTH += _width


ACT_PER_LAYER = 0
DVE_PER_LAYER = 108
SPLITS_PER_LAYER = 2 * FFN_UNITS


class Signal:

    def __init__(self, sem, base=0, per_turn=0):
        self.sem, self.base, self.n, self.per_turn = sem, base, base, per_turn


class Lane:

    def __init__(self, eng, line, spare):
        self.eng, self.line, self.spare, self.turn, self.last = eng, line, spare, None, None

    def wait(self, signal, value):
        value += signal.base
        if self.turn is not None and signal.per_turn:
            value = self.turn * signal.per_turn + value
        self.eng.wait_ge(signal.sem, value)

    def inc(self, ins, signal=None):
        signal = signal or self.line
        ins.then_inc(signal.sem, 1)
        signal.n += 1
        self.last = (signal, signal.n - signal.base)

    def join(self):
        self.wait(*self.last)

    def settle(self):
        self.eng.sem_inc(self.spare.sem, 1)


def program(nc, xT, vec, base_c, mla_c, mix_c, w, out):
    ctx = ExitStack()
    with ctx:
        used_bytes = [FIRST_BYTE]

        def place(name, shape, dt, at):
            return nc.alloc_sbuf_tensor_at(name, shape, dt, offset=at)

        def sb(name, shape, dt=F32):
            at = used_bytes[0]
            used_bytes[0] += (4 * int(np.prod(shape[1:])) + 31) // 32 * 32
            return place(name, shape, dt, at)

        def sig(name, per_turn=0):
            return Signal(ctx.enter_context(nc.semaphore(name)), 0, per_turn)

        reused = {}

        def shared(name, count, turns=0):
            if name not in reused:
                reused[name] = [ctx.enter_context(nc.semaphore(name)), 0]
            sem, base = reused[name]
            reused[name][1] += count
            return Signal(sem, base, count * turns)

        ring_at = used_bytes[0]
        ring = sb("ring", [P, RING, SLOT])
        XT = sb("XT", [P, KD, TA])
        A_at = used_bytes[0]
        A = sb("A", [P, KD, TA])
        VECS = sb("VECS", [P, VEC_WIDTH])
        BASE = sb("BASE", [P, 4 * P + 12])
        RS = sb("RS", [P, 2, TA])
        COND = sb("COND", [P, KD, 2])
        MOD = [sb(f"MOD{l}", [P, 48, 2]) for l in range(2)]
        GAIN = [sb(f"GAIN{l}", [P, 2, KD, 2]) for l in range(2)]
        ARENA_W = 17496
        arena_at = used_bytes[0]
        arena = sb("arena", [P, ARENA_W])
        ps = ctx.enter_context(nc.psum_tensor("ps", [P, 8, 512], F32))

        IDENT, ONES, BEFORE, IOTA = (BASE[:, i * P:(i + 1) * P] for i in range(4))
        PLACE = BASE[:, 4 * P:4 * P + 12].rearrange("p (c t) -> p c t", c=3)

        def vcol(name, width, shift=0):
            return VECS[:, VEC[name] + shift:VEC[name] + shift + width]

        def carver():
            used = [0]

            def take(width):
                at = used[0]
                used[0] += width
                assert used[0] <= ARENA_W, (used[0], ARENA_W)
                return arena[:, at:at + width]
            return take

        f_rows = nc.dram_tensor("f_rows", [TA, D], F32, kind="Internal").ap()
        y_rows = nc.dram_tensor("y_rows", [2 * TA, D], F32, kind="Internal").ap()

        const_in = sig("const_in")
        x_in = sig("x_in")
        mla_in = sig("mla_in")
        mix_in = sig("mix_in")
        stages_done = sig("stages_done")
        slot_in = [sig(f"slot_in{i}") for i in range(RING)]
        spare = sig("spare")
        line = {e: sig(f"line_{e}") for e in ("pe", "act", "dve", "pool")}
        loop_line = {"act": sig("loop_line_act", ACT_PER_LAYER), "dve": sig("loop_line_dve", DVE_PER_LAYER)}

        loads, frees, arrivals, place_of, before = [], [], [], [], []
        second_stack = []

        def slot(n):
            return ring[:, place_of[n], :]

        def plan(src, shape, freed_by):
            n = len(loads)
            at = (n - second_stack[0]) % RING_2 if second_stack else n % RING
            before.append(max((i for i in range(n) if place_of[i] == at), default=None))
            place_of.append(at)
            width = int(np.prod(shape))
            dst = slot(n)[:, 0:width]
            if len(shape) == 2:
                dst = dst.rearrange("p (k n) -> p k n", k=shape[0])
            elif len(shape) == 3:
                dst = dst.rearrange("p (k a n) -> p k a n", k=shape[0], a=shape[1])
            parts = [(dst, src)] if len(shape) == 2 else [(dst[:, :, a, :], src[:, :, a, :]) for a in range(shape[1])]
            loads.append(parts)
            slot_in[at].n += 16 * len(parts)
            arrivals.append(slot_in[at].n)
            signal, value, turn = (*freed_by, 0)[:3]
            frees.append((signal.sem, signal.base + signal.per_turn * turn + value))
            return n

        def columns(weight, c0, c1):
            return weight[:, c0:c1].rearrange("(k p) n -> p k n", p=P)

        def slot_ready(L, n):
            L.wait(slot_in[place_of[n]], arrivals[n])

        PER_LAYER_STAGES = 6
        counters = {"pe": 0, "act": 0, "dve": 0}

        def begin(L, name):
            s = counters[name]
            if s:
                value = 3 * s
                if L.turn is not None:
                    value = L.turn * (3 * PER_LAYER_STAGES) + value
                L.eng.wait_ge(stages_done.sem, value)
                if L.turn is not None:
                    L.settle()

        def end(L, name):
            if L.last:
                L.join()
            L.eng.sem_inc(stages_done.sem, 1)
            counters[name] += 1

        def high(ap):
            return ap.bitcast(F32)

        FOLD = sb("FOLD", [4, 2])
        COND_SPLIT = place("COND_SPLIT", [P, KD, 4], F32R, used_bytes[0])
        used_bytes[0] += 4 * 4 * KD
        MOD_WS = place("MOD_WS", [P, 2, UNITS, UNIT], F32R, arena_at)

        class Mod:

            def __init__(self, l):
                self.l = l
                self.w_high = shared("split_high", 48)
                self.w_split = shared("split_ready", 48)
                self.w_used = shared("split_used", 48)
                self.rows_kept = sig(f"mod{l}_rows_kept", 6)
                self.turned = sig(f"mod{l}_turned", 6)
                self.kept = sig(f"mod{l}_kept", 1)
                self.first = len(loads)
                for s in range(12):
                    plan(columns(w["w_mod"][l], 512 * s, 512 * (s + 1)), (KD, 512), (self.w_split, 4 * (s + 1)))
                for signal in (self.w_high, self.w_split, self.w_used):
                    signal.per_turn = 24

            def unit(self, u):
                return slot(self.first + u // 4).rearrange("p (k n) -> p k n", k=KD)[:, 2 * (u % 4):2 * (u % 4) + 2, :]

            def parts(self, u):
                return [MOD_WS[:, j, u % UNITS, :].rearrange("p (k n) -> p k n", k=2) for j in range(2)]

            def units_used(self, L, count):
                L.wait(self.w_used, count + UNITS)

            def pe(self, L):
                begin(L, "pe")
                with L.eng.Fori(0, 2) as turn:
                    L.turn = turn

                    def turn_rows(s):
                        if s == 0:
                            L.eng.wait_ge(self.kept.sem, turn + 1)
                        L.wait(self.rows_kept, s + 1)
                        L.settle()
                        for t in range(4):
                            c = 4 * s + t
                            mm = L.eng.matmul(ps[:, 0, 2 * c:2 * c + 2], RS[0:4, s % 2, t * P:(t + 1) * P], FOLD[:, :],
                                              start=True, stop=True)
                        L.inc(mm, self.turned)

                    for s in range(6):
                        for q in range(4):
                            u = 4 * s + q
                            L.wait(self.w_split, u + 1)
                            for j, weights in enumerate(self.parts(u)):
                                for i in range(2):
                                    mm = L.eng.matmul(ps[0:4, 1 + s % 2, :], COND_SPLIT[:, 2 * q + i, :], weights[:, i, :],
                                                      start=q + i + j == 0, stop=q + i + j == 5)
                            L.inc(mm, self.w_used)
                        if s:
                            turn_rows(s - 1)
                    turn_rows(5)
                L.turn, L.last = None, (self.turned, 12)
                end(L, "pe")

            def act(self, L):
                begin(L, "act")
                with L.eng.Fori(0, 2) as turn:
                    L.turn = turn

                    def keep_rows(s):
                        self.units_used(L, 4 * s + 4)
                        if s >= 2:
                            L.wait(self.turned, s - 1)
                        L.inc(L.eng.copy(RS[0:4, s % 2, :], ps[0:4, 1 + s % 2, :]), self.rows_kept)

                    for s in range(6):
                        n = self.first + s
                        L.eng.wait_ge(slot_in[place_of[n]].sem, turn * 16 + arrivals[n])
                        for q in range(4):
                            u = 4 * s + q
                            self.units_used(L, u + 1 - UNITS)
                            L.inc(L.eng.copy(self.parts(u)[0], self.unit(u)), self.w_high)
                        if s:
                            keep_rows(s - 1)
                    keep_rows(5)
                L.turn, L.last = None, (self.rows_kept, 12)
                end(L, "act")

            def dve(self, L):
                begin(L, "dve")
                L.eng.sem_inc(self.kept.sem, 1)
                b = vcol("b_mod", 48, 48 * self.l)
                mod, gain = MOD[self.l], GAIN[self.l]
                with L.eng.Fori(0, 2) as turn:
                    L.turn = turn
                    for u in range(24):
                        wh, wl = self.parts(u)
                        L.wait(self.w_high, u + 1)
                        L.inc(L.eng.tensor_tensor(wl, self.unit(u), high(wh), ALU.subtract), self.w_split)
                    L.wait(self.turned, 6)
                    half = bass.ds(turn * 24, 24)
                    L.eng.tensor_tensor(mod[:, half, :], ps[:, 0, 0:48].rearrange("p (c a) -> p c a", a=2),
                                        b[:, half].unsqueeze(2).to_broadcast([P, 24, 2]),
                                        ALU.add).then_inc(self.kept.sem, 1)
                L.turn = None
                L.last = (self.kept, 3)
                L.join()
                for which, name in enumerate(("norm_mix", "norm_ffn")):
                    g = vcol(name, KD, KD * self.l).unsqueeze(2).to_broadcast([P, KD, 2])
                    at = KD * (3 * which + 1)
                    L.inc(L.eng.scalar_tensor_tensor(out=gain[:, which], in0=mod[:, at:at + KD, :], scalar=1.0,
                                                     in1=g, op0=ALU.add, op1=ALU.mult))
                end(L, "dve")

        x_high, x_split = sig("x_high"), sig("x_split")

        def stream_split(use, per_turn):
            return [Signal(s.sem, KD * use, 2 * KD * per_turn) for s in (x_high, x_split)]

        def stream_high(L, made, k, signals):
            L.wait(made, k + 1)
            L.inc(L.eng.copy(XS[:, 0, k, :], XT[:, k, 0:TL]), signals[0])

        def stream_low(L, k, signals):
            L.wait(signals[0], k + 1)
            L.inc(L.eng.tensor_tensor(XS[:, 1, k, :], XT[:, k, 0:TL], high(XS[:, 0, k, :]), ALU.subtract), signals[1])

        class Norm:
            def __init__(self, name, l, which, tokens):
                self.l, self.which, self.T = l, which, tokens
                plain = which == 2
                self.split = stream_split(0, 0)
                self.sq_act = shared("norm_sq_act", KD // 2)
                self.sq_dve = shared("norm_sq_dve", KD // 2)
                self.sums = shared("norm_sums", 1)
                self.var = shared("norm_var", 1)
                self.std = shared("norm_std", 1)
                self.scaled = shared("norm_scaled", KD)
                self.done = shared("norm_done", 0 if plain else KD * tokens // TL)

            def pe(self, L):
                begin(L, "pe")
                for k in range(KD):
                    L.wait(self.sq_dve if k % 2 else self.sq_act, k // 2 + 1)
                    mm = L.eng.matmul(ps[:, 6, 0:self.T], ONES, A[:, k, 0:self.T], start=k == 0, stop=k == KD - 1)
                L.inc(mm, self.sums)
                end(L, "pe")

            def act(self, L):
                begin(L, "act")
                if self.l == 0 and self.which == 0:
                    L.eng.wait_ge(x_in.sem, 16)
                T = self.T
                for k in range(0, KD, 2):
                    L.inc(L.eng.activation(A[:, k, 0:T], XT[:, k, 0:T], ACT.Square), self.sq_act)
                L.wait(self.var, 1)
                L.inc(L.eng.activation(RS[:, 0, 0:T], RS[:, 0, 0:T], ACT.Sqrt), self.std)
                if self.which < 2:
                    gain, mod = GAIN[self.l], MOD[self.l]
                    for k in range(KD):
                        L.wait(self.scaled, k + 1)
                        for c in range(T // TL):
                            a = A[:, k, c * TL:(c + 1) * TL]
                            L.inc(L.eng.activation(a, a, ACT.Identity, bias=mod[:, 3 * KD * self.which + k, c:c + 1],
                                                   scale=gain[:, self.which, k, c:c + 1]), self.done)
                else:
                    for k in range(KD):
                        stream_high(L, self.scaled, k, self.split)
                end(L, "act")

            def dve(self, L):
                begin(L, "dve")
                if self.l == 0 and self.which == 0:
                    L.eng.wait_ge(x_in.sem, 16)
                T = self.T
                for k in range(1, KD, 2):
                    L.inc(L.eng.tensor_tensor(A[:, k, 0:T], XT[:, k, 0:T], XT[:, k, 0:T], ALU.mult), self.sq_dve)
                L.wait(self.sums, 1)
                L.inc(L.eng.tensor_scalar(RS[:, 0, 0:T], ps[:, 6, 0:T], 1.0 / D, NORM_EPS, ALU.mult, ALU.add), self.var)
                L.wait(self.std, 1)
                L.inc(L.eng.reciprocal(RS[:, 0, 0:T], RS[:, 0, 0:T]))
                L.join()
                for k in range(KD):
                    if self.which < 2:
                        L.inc(L.eng.tensor_tensor(A[:, k, 0:T], XT[:, k, 0:T], RS[:, 0, 0:T], ALU.mult), self.scaled)
                    else:
                        L.inc(L.eng.scalar_tensor_tensor(out=XT[:, k, 0:T], in0=XT[:, k, 0:T],
                                                         scalar=vcol("final", KD)[:, k:k + 1], in1=RS[:, 0, 0:T],
                                                         op0=ALU.mult, op1=ALU.mult), self.scaled)
                        if k >= 2:
                            stream_low(L, k - 2, self.split)
                if self.which == 2:
                    for k in (KD - 2, KD - 1):
                        stream_low(L, k, self.split)
                end(L, "dve")

        class LayerNorm:
            def __init__(self, i):
                self.i = i
                self.split = stream_split(i, 1) if i else None
                self.mean = shared("ln_mean", 1, 3)
                self.centred = shared("ln_centred", KD, 3)
                self.squares = shared("norm_sq_act", KD, 3)
                self.sums = shared("norm_sums", 1, 3)
                self.var = shared("norm_var", 1, 3)
                self.std = shared("norm_std", 1, 3)
                self.scaled = shared("norm_scaled", KD, 3)
                self.done = shared("norm_done", KD, 3)

            def mean_tile(self, L, added, k):
                if k == 0:
                    L.eng.wait_ge(mix_in.sem, 16)
                L.wait(added, k + 1)
                mm = L.eng.matmul(ps[:, 6, 0:TL], MEAN, XT[:, k, 0:TL], start=k == 0, stop=k == KD - 1)
                if k == KD - 1:
                    L.inc(mm, self.mean)

            def pe(self, L):
                for k in range(KD):
                    L.wait(self.squares, k + 1)
                    mm = L.eng.matmul(ps[:, 7, 0:TL], MEAN, LN_TILES[:, k, TL:TA], start=k == 0, stop=k == KD - 1)
                L.inc(mm, self.sums)
                end(L, "pe")

            def act(self, L):
                for k in range(KD):
                    L.wait(self.centred, k + 1)
                    L.inc(L.eng.activation(LN_TILES[:, k, TL:TA], LN_TILES[:, k, 0:TL], ACT.Square), self.squares)
                L.wait(self.var, 1)
                L.inc(L.eng.activation(RS[:, 0, 0:TL], RS[:, 0, 0:TL], ACT.Sqrt), self.std)
                for k in range(KD):
                    L.wait(self.scaled, k + 1)
                    L.inc(L.eng.activation(XT[:, k, 0:TL], XT[:, k, 0:TL], ACT.Identity,
                                           bias=LNP[:, (2 * self.i + 1) * KD + k:(2 * self.i + 1) * KD + k + 1]), self.done)
                    if self.split and k:
                        stream_high(L, self.done, k - 1, self.split)
                if self.split:
                    stream_high(L, self.done, KD - 1, self.split)
                end(L, "act")

            def dve(self, L):
                L.wait(self.mean, 1)
                for k in range(KD):
                    L.inc(L.eng.tensor_tensor(LN_TILES[:, k, 0:TL], XT[:, k, 0:TL], ps[:, 6, 0:TL], ALU.subtract), self.centred)
                L.wait(self.sums, 1)
                L.inc(L.eng.tensor_scalar(RS[:, 0, 0:TL], ps[:, 7, 0:TL], LN_EPS / ALPHA ** 2, None, ALU.add), self.var)
                L.wait(self.std, 1)
                L.inc(L.eng.reciprocal(RS[:, 0, 0:TL], RS[:, 0, 0:TL]))
                L.join()
                for k in range(KD):
                    L.inc(L.eng.scalar_tensor_tensor(out=XT[:, k, 0:TL], in0=LN_TILES[:, k, 0:TL],
                                                     scalar=LNP[:, 2 * self.i * KD + k:2 * self.i * KD + k + 1],
                                                     in1=RS[:, 0, 0:TL], op0=ALU.mult, op1=ALU.mult), self.scaled)
                    if self.split and k >= 2:
                        stream_low(L, k - 2, self.split)
                if self.split:
                    for k in (KD - 2, KD - 1):
                        stream_low(L, k, self.split)
                end(L, "dve")

        take = carver()
        KT = take(HEADS * TA).rearrange("p (h t) -> p h t", h=HEADS)
        V = take(4 * D).rearrange("p (t c) -> p t c", t=4)
        CKV = take(2 * TA).rearrange("p (c t) -> p c t", c=2)
        CQ = take(4 * TA).rearrange("p (c t) -> p c t", c=4)
        KPE, QN, QR, QRAW, T1 = (take(TA) for _ in range(5))
        PC = take(2 * TL).rearrange("p (q t) -> p q t", q=2)
        PTL = take(4 * TL).rearrange("p (k t) -> p k t", k=4)
        PTC = take(2 * TL).rearrange("p (k t) -> p k t", k=2)
        MLAC = take(2 * TA + ROPE)
        SMALL = take(16)
        PL = CKV
        SQ = [PTL[:, 0:2].rearrange("p a b -> p (a b)"), PTL[:, 2:4].rearrange("p a b -> p (a b)"),
              PTC.rearrange("p a b -> p (a b)"), PC.rearrange("p a b -> p (a b)"), QN, QR]
        OT = A
        COS, SIN, TURN = MLAC[0:ROPE, 0:TA], MLAC[0:ROPE, TA:2 * TA], MLAC[0:ROPE, 2 * TA:2 * TA + ROPE]
        MAXS, NEG, DEN, RDEN = (SMALL[:, 4 * i:4 * i + 4] for i in range(4))

        class Mla:
            def __init__(self):
                self.tiles = sig("mla_tiles")
                self.copied = sig("mla_copied")
                self.squares = sig("mla_squares")
                self.kpe_turned = sig("mla_kpe_turned")
                self.sums = sig("mla_sums")
                self.var = sig("mla_var")
                self.std = sig("mla_std")
                self.latents = sig("mla_latents")
                self.q_tiles = sig("mla_q_tiles")
                self.q_copied = sig("mla_q_copied")
                self.q_turned = sig("mla_q_turned")
                self.q_ready = sig("mla_q_ready")
                self.scores = sig("mla_scores")
                self.neg = sig("mla_neg")
                self.exps = sig("mla_exps")
                self.probs = sig("mla_probs")
                self.turned = sig("mla_turned")
                self.turned_copied = sig("mla_turned_copied")
                self.outs = sig("mla_outs")
                self.outs_copied = sig("mla_outs_copied")
                self.y_tiles = sig("mla_y_tiles")
                self.y_added = sig("mla_y_added")
                self.dkv = plan(columns(w["mla_w_dkv"][0], 0, 320), (KD, 320), (self.tiles, 3))
                self.dq = plan(columns(w["mla_w_dq"][0], 0, Q_LORA), (KD, Q_LORA), (self.tiles, 7))
                self.ukv = plan(columns(w["mla_w_ukv"][0], 0, 2048), (2, 2048), (self.tiles, 23))
                self.uq = [plan(columns(w["mla_w_uq"][0], 0, 5 * QW), (4, 5 * QW), (self.q_tiles, 10)),
                           plan(columns(w["mla_w_uq"][0], 5 * QW, 8 * QW), (4, 3 * QW), (self.q_tiles, 16))]
                self.wo = [plan(columns(w["mla_w_o"][0], 512 * i, 512 * (i + 1)), (HEADS, 512), (self.y_tiles, 4 * i + 4))
                           for i in range(2)]

            def q_weights(self, h, c0, c1):
                n = self.uq[0 if h < 5 else 1]
                heads = 5 if h < 5 else 3
                at = (h if h < 5 else h - 5) * QW
                return slot(n)[:, 0:4 * heads * QW].rearrange("p (k n) -> p k n", k=4)[:, :, at + c0:at + c1]

            def pe(self, L):
                pe = L.eng
                pe.wait_ge(mla_in.sem, 16)
                i = 0
                for n, width, outs in ((self.dkv, 320, ((0, 128), (128, 256), (256, 320))),
                                       (self.dq, 512, tuple((c, c + 128) for c in range(0, 512, 128)))):
                    slot_ready(L, n)
                    wv = slot(n)[:, 0:KD * width].rearrange("p (k n) -> p k n", k=KD)
                    for c0, c1 in outs:
                        if i >= 4:
                            L.wait(self.copied, i - 3)
                        for k in range(KD):
                            if i == 0:
                                L.wait(norms[0].done, (k + 1) * TA // TL)
                            mm = pe.matmul(ps[0:c1 - c0, i % 4, :], wv[:, k, c0:c1], A[:, k, :], start=k == 0, stop=k == KD - 1)
                        L.inc(mm, self.tiles)
                        i += 1
                L.wait(self.copied, 3)
                L.inc(pe.matmul(ps[0:ROPE, 4, :], TURN, QRAW[0:ROPE, :], start=True, stop=True), self.kpe_turned)
                for first, count, bank in ((0, 2, 5), (2, 4, 6)):
                    for c in range(count):
                        L.wait(self.squares, first + c + 1)
                        mm = pe.matmul(ps[:, bank, :], ONES, SQ[first + c], start=c == 0, stop=c == count - 1)
                    L.inc(mm, self.sums)
                slot_ready(L, self.ukv)
                wv = slot(self.ukv).rearrange("p (k h a n) -> p k h a n", k=2, h=HEADS, a=2)
                L.wait(self.latents, 2)
                for h in range(HEADS):
                    L.wait(self.copied, i - 3)
                    for k in range(2):
                        mm = pe.matmul(ps[:, i % 4, :], wv[:, k, h, 0, :], CKV[:, k, :], start=k == 0, stop=k == 1)
                    L.inc(mm, self.tiles)
                    i += 1
                for t in range(4):
                    for half in range(2):
                        L.wait(self.copied, i - 3)
                        for k in range(2):
                            mm = pe.matmul(ps[:, i % 4, :], CKV[:, k, t * P:(t + 1) * P],
                                           wv[:, k, 4 * half:4 * half + 4, 1, :], start=k == 0, stop=k == 1)
                        L.inc(mm, self.tiles)
                        i += 1
                L.wait(self.latents, 6)

                def queries(h):
                    if h in (0, 5):
                        slot_ready(L, self.uq[0 if h < 5 else 1])
                    for k in range(4):
                        mm = pe.matmul(ps[:, 7, :], self.q_weights(h, 0, NOPE)[:, k, :], CQ[:, k, :], start=k == 0, stop=k == 3)
                    L.inc(mm, self.q_tiles)
                    if h == 0:
                        L.wait(self.var, 2)
                    if h >= 2:
                        L.wait(self.outs_copied, h - 1)
                    for k in range(4):
                        mm = pe.matmul(ps[0:ROPE, 6, :], self.q_weights(h, NOPE, QW)[:, k, :], CQ[:, k, :],
                                       start=k == 0, stop=k == 3)
                    L.inc(mm, self.q_tiles)

                def turn_query(h):
                    L.wait(self.q_copied, 2 * h + 2)
                    L.inc(pe.matmul(ps[0:ROPE, 7, :], TURN, QRAW[0:ROPE, :], start=True, stop=True), self.q_turned)

                queries(0)
                turn_query(0)
                L.wait(self.copied, 23)
                for h in range(HEADS):
                    L.wait(self.q_ready, h + 1)
                    if h:
                        L.wait(self.exps, 4 * h)
                    for q in range(2):
                        rows = slice(q * P, (q + 1) * P)
                        pe.matmul(ps[:, q, :], QN[:, rows], KT[:, h, :], start=True, stop=False)
                        L.inc(pe.matmul(ps[:, q, :], QR[0:ROPE, rows], KPE[0:ROPE, :], start=False, stop=True), self.scores)
                    for q in range(2):
                        rows = slice(TL + q * P, TL + (q + 1) * P)
                        o = ps[:, 2, q * TL:(q + 1) * TL]
                        pe.matmul(o, QN[:, rows], KT[:, h, TL:TA], start=True, stop=False)
                        mm = pe.matmul(o, QR[0:ROPE, rows], KPE[0:ROPE, TL:TA], start=False, stop=True)
                    L.inc(mm, self.scores)
                    if h + 1 < HEADS:
                        queries(h + 1)
                    L.wait(self.probs, 4 * h + 4)
                    if h:
                        L.wait(self.turned_copied, 3 * h)
                    for bank in range(2):
                        for kk in range(2):
                            for q in range(2):
                                k = 2 * bank + kk
                                mm = pe.transpose(ps[:, 3 + bank, kk * TL + q * P:kk * TL + (q + 1) * P],
                                                  PL[:, q, k * P:(k + 1) * P], IDENT)
                        L.inc(mm, self.turned)
                    for kk in range(2):
                        for q in range(2):
                            mm = pe.transpose(ps[:, 5, kk * TL + q * P:kk * TL + (q + 1) * P],
                                              PC[:, q, kk * P:(kk + 1) * P], IDENT)
                    L.inc(mm, self.turned)
                    if h + 1 < HEADS:
                        turn_query(h + 1)
                    L.wait(self.turned_copied, 3 * h + 3)
                    if h:
                        L.wait(self.outs_copied, h)
                    for k in range(4):
                        pe.matmul(ps[:, 6, 0:TL], V[:, k, h * DV:(h + 1) * DV], PTL[:, k, :], start=k == 0, stop=k == 3)
                    for k in range(2):
                        mm = pe.matmul(ps[:, 6, TL:TA], V[:, 2 + k, h * DV:(h + 1) * DV], PTC[:, k, :], start=k == 0, stop=k == 1)
                    L.inc(mm, self.outs)
                L.wait(self.outs_copied, HEADS)
                for m in range(KD):
                    n = self.wo[m // 4]
                    if m % 4 == 0:
                        slot_ready(L, n)
                    if m >= 4:
                        L.wait(self.y_added, 2 * (m - 3))
                    wv = slot(n).rearrange("p (k n) -> p k n", k=HEADS)
                    for h in range(HEADS):
                        mm = pe.matmul(ps[:, m % 4, :], wv[:, h, m % 4 * P:(m % 4 + 1) * P], OT[:, h, :],
                                       start=h == 0, stop=h == HEADS - 1)
                    L.inc(mm, self.y_tiles)
                end(L, "pe")

            def act(self, L):
                begin(L, "act")
                act = L.eng
                for i in range(7):
                    L.wait(self.tiles, i + 1)
                    o = (CKV[:, 0, :], CKV[:, 1, :], QRAW[0:ROPE, :])[i] if i < 3 else CQ[:, i - 3, :]
                    L.inc(act.copy(o, ps[0:ROPE if i == 2 else P, i % 4, :]), self.copied)
                for i in range(2):
                    L.wait(self.var, i + 1)
                    L.inc(act.activation(RS[:, i, :], RS[:, i, :], ACT.Sqrt), self.std)
                for i in range(7, 23):
                    L.wait(self.tiles, i + 1)
                    j = i - 7
                    o = KT[:, j, :] if j < 8 else V[:, (j - 8) // 2, (j - 8) % 2 * 512:((j - 8) % 2 + 1) * 512]
                    L.inc(act.copy(o, ps[:, i % 4, :]), self.copied)

                def copy_query(h):
                    L.wait(self.q_tiles, 2 * h + 1)
                    if h == 0:
                        L.wait(self.latents, 6)
                    L.inc(act.copy(QN, ps[:, 7, :]), self.q_copied)
                    L.wait(self.q_tiles, 2 * h + 2)
                    L.inc(act.copy(QRAW[0:ROPE, :], ps[0:ROPE, 6, :]), self.q_copied)

                L.wait(self.latents, 7)
                copy_query(0)
                for h in range(HEADS):
                    L.wait(self.neg, h + 1)
                    for q in range(2):
                        L.inc(act.activation(PL[:, q, :], ps[:, q, :], ACT.Exp, bias=NEG[:, q:q + 1], scale=MLA_SCALE,
                                             accum_out=DEN[:, q:q + 1]), self.exps)
                    for q in range(2):
                        L.inc(act.activation(PC[:, q, :], ps[:, 2, q * TL:(q + 1) * TL], ACT.Exp, bias=NEG[:, 2 + q:3 + q],
                                             scale=MLA_SCALE, accum_out=DEN[:, 2 + q:3 + q]), self.exps)
                    if h + 1 < HEADS:
                        copy_query(h + 1)
                    L.wait(self.outs, h + 1)
                    L.inc(act.copy(OT[:, h, :], ps[:, 6, :]), self.outs_copied)
                end(L, "act")

            def dve(self, L):
                begin(L, "dve")
                dve = L.eng
                dve.wait_ge(mla_in.sem, 16)
                for c in range(6):
                    L.wait(self.copied, c + 1 if c < 2 else c + 2)
                    src = CKV[:, c, :] if c < 2 else CQ[:, c - 2, :]
                    L.inc(dve.tensor_tensor(SQ[c], src, src, ALU.mult), self.squares)
                for i, width in enumerate((KV_LORA, Q_LORA)):
                    L.wait(self.sums, i + 1)
                    L.inc(dve.tensor_scalar(RS[:, i, :], ps[:, 5 + i, :], 1.0 / width, NORM_EPS, ALU.mult, ALU.add), self.var)
                for i in range(2):
                    L.wait(self.std, i + 1)
                    L.inc(dve.reciprocal(RS[:, i, :], RS[:, i, :]))
                    L.join()
                    for c in range(2 + 2 * i):
                        o = CQ[:, c, :] if i else CKV[:, c, :]
                        L.inc(dve.scalar_tensor_tensor(out=o, in0=o, scalar=vcol("g_q" if i else "g_kv", 4 if i else 2)[:, c:c + 1],
                                                       in1=RS[:, i, :], op0=ALU.mult, op1=ALU.mult), self.latents)

                def rotate(out_ap, bank, signal):
                    L.inc(dve.tensor_tensor(T1[0:ROPE, :], QRAW[0:ROPE, :], COS, ALU.mult))
                    L.inc(dve.tensor_tensor(out_ap[0:ROPE, :], ps[0:ROPE, bank, :], SIN, ALU.mult))
                    L.join()
                    L.inc(dve.tensor_tensor(out_ap[0:ROPE, :], out_ap[0:ROPE, :], T1[0:ROPE, :], ALU.add), signal)

                L.wait(self.kpe_turned, 1)
                rotate(KPE, 4, self.latents)

                L.wait(self.q_turned, 1)
                rotate(QR, 7, self.q_ready)
                for h in range(HEADS):
                    for q in range(2):
                        L.wait(self.scores, 3 * h + q + 1)
                        L.inc(dve.tensor_reduce(MAXS[:, q:q + 1], ps[:, q, :], X, ALU.max))
                    L.wait(self.scores, 3 * h + 3)
                    L.inc(dve.tensor_reduce(MAXS[:, 2:4], ps[:, 2, :].rearrange("p (q t) -> p q t", q=2), X, ALU.max))
                    L.join()
                    L.inc(dve.tensor_scalar(NEG, MAXS, -MLA_SCALE, None, ALU.mult), self.neg)
                    L.wait(self.exps, 4 * h + 4)
                    L.inc(dve.reciprocal(RDEN, DEN))
                    L.join()
                    for q in range(4):
                        p = PL[:, q, :] if q < 2 else PC[:, q - 2, :]
                        L.inc(dve.tensor_scalar(p, p, RDEN[:, q:q + 1], None, ALU.mult), self.probs)
                    for bank in range(3):
                        L.wait(self.turned, 3 * h + bank + 1)
                        o = PTL[:, 2 * bank:2 * bank + 2, :] if bank < 2 else PTC
                        L.inc(dve.tensor_copy(o.rearrange("p k t -> p (k t)"), ps[:, 3 + bank, :]), self.turned_copied)
                    if h + 1 < HEADS:
                        L.wait(self.q_turned, h + 2)
                        rotate(QR, 7, self.q_ready)
                gated_add(L, 0, 0, TA, self.y_tiles, self.y_added)
                end(L, "dve")

        def gated_add(L, l, which, tokens, tiles, added):
            for m in range(KD):
                L.wait(tiles, m + 1)
                for c in range(tokens // TL):
                    xs = XT[:, m, c * TL:(c + 1) * TL]
                    L.inc(L.eng.scalar_tensor_tensor(out=xs, in0=ps[:, m % 4, c * TL:(c + 1) * TL],
                                                     scalar=MOD[l][:, 3 * KD * which + 2 * KD + m, c:c + 1], in1=xs,
                                                     op0=ALU.mult, op1=ALU.add), added)

        class Moe:

            def __init__(self, l, tokens, norm):
                self.l, self.T, self.NT, self.norm = l, tokens, tokens // P, norm
                self.NB = blocks_of(tokens)
                NT = self.NT
                self.logits_made = shared("moe_logits_made", 1)
                self.logits_copied = shared("moe_logits_copied", 1)
                self.logits = shared("moe_logits", 1)
                self.logits_kept = shared("moe_logits_kept", 1)
                self.rows_turned = shared("moe_rows_turned", NT)
                self.rows_kept = shared("moe_rows_kept", NT)
                self.less_max = shared("moe_less_max", 2)
                self.exps = shared("moe_exps", 2)
                self.chosen = shared("moe_chosen", 1)
                self.ranks = shared("moe_ranks", 1)
                self.counts = shared("moe_counts", 1)
                self.counts_kept = shared("moe_counts_kept", 1)
                self.firsts = shared("moe_firsts", 1)
                self.places = shared("moe_places", 2 * NT)
                self.table = shared("moe_table", 1)
                self.table_kept = shared("moe_table_kept", 1)
                self.sum_turned = shared("moe_sum_turned", NT)
                self.sum_made = shared("moe_sum_made", NT)
                self.sum_added = shared("moe_sum_added", NT)
                self.scattered_all = shared("moe_scattered_all", 1)
                self.rows_out = [shared(f"moe_rows_out{i}", 16 * NT // 2) for i in range(2)]
                self.pairs_in = [shared(f"moe_pairs_in{i}", 16 * NT // 2) for i in range(2)]
                self.block_turned = sig(f"moe{l}_block_turned")
                self.x_high = sig(f"moe{l}_x_high")
                self.x_split = sig(f"moe{l}_x_split")
                self.w_high = sig(f"moe{l}_w_high")
                self.w_split = sig(f"moe{l}_w_split")
                self.w_used = sig(f"moe{l}_w_used")
                self.gated = sig(f"moe{l}_gated")
                self.multiplied = sig(f"moe{l}_multiplied")
                self.hidden_turned = sig(f"moe{l}_hidden_turned")
                self.h_high = sig(f"moe{l}_h_high")
                self.h_split = sig(f"moe{l}_h_split")
                self.y_kept = sig(f"moe{l}_y_kept")
                self.stored = sig(f"moe{l}_stored")
                self.index_g = sig(f"moe{l}_index_g")
                self.index_s = sig(f"moe{l}_index_s")
                self.gathered = sig(f"moe{l}_gathered")
                self.scattered = sig(f"moe{l}_scattered")
                self.first = len(loads)
                for e in range(EXPERTS):
                    done = (self.w_split, 0) if e < EXPERTS - 1 else (self.pairs_in[1], 16 * (NT // 2))
                    plan(columns(w["moe_w_gate"][l][e], 0, FF), (KD, FF), done)
                    plan(columns(w["moe_w_up"][l][e], 0, FF), (KD, FF), done)
                    plan(columns(w["moe_w_down"][l][e], 0, D), (FT, D), done)
                NT, NB = self.NT, self.NB
                take = carver()

                def tiles(n):
                    return take(NT * n).rearrange("p (t n) -> p t n", t=NT)
                self.ROWS = [take(D) for _ in range(2)]
                self.PAIRS = [take(2 * D).rearrange("p (c d) -> p c d", c=2) for _ in range(2)]
                self.SUM = take(D)
                self.LOG = tiles(36)
                self.M1, self.M2 = tiles(1), tiles(1)
                self.GP, self.GB, self.CG, self.OG = (tiles(GROUPS) for _ in range(4))
                self.GW, self.GS = tiles(1), tiles(1)
                self.TMP = tiles(EXPERTS)
                self.EL, self.EB, self.ES, self.CE = (tiles(PER_GROUP) for _ in range(4))
                self.OE = [tiles(PER_GROUP) for _ in range(2)]
                self.WT = [tiles(1) for _ in range(2)]
                self.WS = tiles(1)
                self.O32 = [tiles(EXPERTS) for _ in range(2)]
                self.BOTH = tiles(EXPERTS)
                self.RANK = [tiles(1) for _ in range(2)]
                self.QUOT = [tiles(1) for _ in range(2)]
                self.BLK = [tiles(1) for _ in range(2)]
                self.CNT, self.NBLK = take(P), take(P)
                self.FIRST = take(EXPERTS + 1)
                self.FIRSTI = take(EXPERTS + 1).bitcast(I32)
                self.UNITS_BEFORE = take(EXPERTS + 1)
                self.UNITS_BEFOREI = take(EXPERTS + 1).bitcast(I32)
                self.AT_PLACE = [[take(CAP) for _ in range(2)] for _ in range(NT)]
                self.AT_BLOCK = [[take(2 * NB).rearrange("p (c b) -> p c b", c=2) for _ in range(2)] for _ in range(NT)]
                self.TAB, self.EMPTY = (take(2 * NB).rearrange("p (c b) -> p c b", c=2) for _ in range(2))
                self.TABI = take(2 * NB).bitcast(I32).rearrange("p (c b) -> p c b", c=2)
                self.IDXG, self.IDXS = take(1).bitcast(I32), take(1).bitcast(I32)
                self.XG = take(D)
                self.SG, self.H = take(FF), take(FF)
                self.YS = take(D)
                self.WH = place(f"MOE_WH{l}", [P, UNITS, UNIT], F32R, A_at)
                self.WL = place(f"MOE_WL{l}", [P, UNITS, UNIT], F32R, arena_at + 4 * 2 * D)
                self.XS = place(f"MOE_XS{l}", [P, 2, KD, CAP], F32R, arena_at)
                self.HS = place(f"MOE_HS{l}", [P, 2, FT, CAP], F32R, arena_at + 4 * 6 * D)

            def unit(self, a, u):
                n = self.first + 3 * a + u // UNITS
                return slot(n)[:, u % UNITS * UNIT:(u % UNITS + 1) * UNIT]

            def pe(self, L):
                pe, NT, NB = L.eng, self.NT, self.NB
                router = vcol("router", KD * 36, self.l * KD * 36).rearrange("p (k n) -> p k n", k=KD)
                for k in range(KD):
                    L.wait(self.norm.done, (k + 1) * self.T // TL)
                    mm = pe.matmul(ps[0:36, 7, 0:self.T], router[:, k, :], A[:, k, 0:self.T], start=k == 0, stop=k == KD - 1)
                L.inc(mm, self.logits_made)
                L.wait(self.logits_copied, 1)
                for t in range(NT):
                    mm = pe.transpose(ps[:, 0, 36 * t:36 * t + 36], self.SUM[0:36, t * P:(t + 1) * P], IDENT[0:36, 0:36])
                L.inc(mm, self.logits)
                for t in range(NT):
                    if t >= 2:
                        L.wait(self.rows_kept, t - 1)
                    for k in range(KD):
                        mm = pe.transpose(ps[:, 1 + 2 * (t % 2) + k // 4, k % 4 * P:(k % 4 + 1) * P],
                                          A[:, k, t * P:(t + 1) * P], IDENT)
                    L.inc(mm, self.rows_turned)
                L.wait(self.chosen, 1)
                for t in range(NT):
                    for u in range(t + 1):
                        mm = pe.matmul(ps[:, 5, 32 * t:32 * t + 32], BEFORE if u == t else ONES, self.BOTH[:, u, :],
                                       start=u == 0, stop=u == t)
                L.inc(mm, self.ranks)
                for t in range(NT):
                    mm = pe.matmul(ps[0:EXPERTS, 6, 0:P], self.BOTH[:, t, :], ONES, start=t == 0, stop=t == NT - 1)
                L.inc(mm, self.counts)
                L.wait(self.counts_kept, 1)
                L.inc(pe.matmul(ps[:, 0, 0:EXPERTS + 1], self.NBLK[0:EXPERTS, :], BEFORE[0:EXPERTS, 0:EXPERTS + 1],
                                start=True, stop=True), self.firsts)
                for t in range(NT):
                    for c in range(2):
                        L.wait(self.places, 2 * t + c + 1)
                        mm = pe.matmul(ps[0:CAP, 6, 0:2 * NB], self.AT_PLACE[t][c],
                                       self.AT_BLOCK[t][c].rearrange("p c b -> p (c b)"),
                                       start=t + c == 0, stop=2 * t + c == 2 * NT - 1)
                L.inc(mm, self.table)

                def turn_block(half):
                    for k in range(4 * half, 4 * half + 4):
                        mm = pe.transpose(ps[:, 3 + k // 4, k % 4 * CAP:(k % 4 + 1) * CAP], self.XG[0:CAP, k * P:(k + 1) * P],
                                          IDENT[0:CAP, 0:CAP])
                    if half:
                        mm.then_inc(self.block_turned.sem, 1)

                L.wait(self.rows_kept, NT)
                pe.wait_ge(self.gathered.sem, 16)
                turn_block(0)
                turn_block(1)

                def products(b, u, outs, moving, tiles, first, last):
                    pe.wait_ge(self.w_split.sem, b * BLOCK_UNITS + (u + 1))
                    j = u % UNITS
                    for i, k in enumerate(tiles):
                        for c, out_ap in enumerate(outs):
                            at = slice((i + c) * 512, (i + c + 1) * 512)
                            for x, weights in ((0, self.WH), (1, self.WH), (0, self.WL)):
                                mm = pe.matmul(out_ap, moving[:, x, k, :], weights[:, j, at],
                                               start=first and i == 0 and x == 0 and weights is self.WH,
                                               stop=last and i == len(tiles) - 1 and weights is self.WL)
                    mm.then_inc(self.w_used.sem, 1)

                with pe.Fori(0, EXPERTS // 2) as pair:
                    for a in range(2):
                        lo, hi = self.range_of(pe, pair, a)
                        with pe.Fori(lo, hi) as b:
                            pe.wait_ge(self.x_split.sem, b * 2 + 2)
                            for u in range(2 * UNITS):
                                q = u % UNITS
                                products(b, u, [ps[0:CAP, u // UNITS, :]], self.XS, (2 * q, 2 * q + 1), q == 0, q == UNITS - 1)
                            pe.wait_ge(self.gathered.sem, b * 16 + 32)
                            pe.sem_inc(spare.sem, 1)
                            turn_block(0)
                            pe.wait_ge(self.multiplied.sem, b + 1)
                            pe.sem_inc(spare.sem, 1)
                            for k in range(FT):
                                mm = pe.transpose(ps[:, 2 if k < 2 else 7, k % 2 * CAP:(k % 2 + 1) * CAP],
                                                  self.H[0:CAP, k * P:(k + 1) * P], IDENT[0:CAP, 0:CAP])
                                if k % 2:
                                    mm.then_inc(self.hidden_turned.sem, 1)
                            turn_block(1)
                            pe.wait_ge(self.y_kept.sem, b * 2 + 2)
                            for k in range(FT):
                                if k % 2 == 0:
                                    pe.wait_ge(self.h_split.sem, b * 2 + (k // 2 + 1))
                                products(b, 2 * UNITS + k, [ps[0:CAP, 5, :], ps[0:CAP, 6, :]], self.HS, (k,), k == 0, k == FT - 1)
                for t in range(NT):
                    L.wait(self.sum_made, t + 1)
                    if t >= 1:
                        L.wait(self.sum_added, t)
                    for k in range(KD):
                        mm = pe.transpose(ps[:, 5 + k // 4, k % 4 * P:(k % 4 + 1) * P], self.SUM[:, k * P:(k + 1) * P], IDENT)
                    L.inc(mm, self.sum_turned)
                end(L, "pe")

            def range_of(self, eng, pair, a):
                return tuple(eng.value_load(self.FIRSTI[0:1, bass.ds(pair * 2 + (a + i), 1)], min_val=i, max_val=self.NB - 2)
                             for i in range(2))

            def count_of(self, eng):
                return eng.value_load(self.FIRSTI[0:1, EXPERTS:EXPERTS + 1], min_val=EXPERTS, max_val=self.NB - 2)

            def keep_rows(self, eng, half, copy, blocks):
                eng.wait_ge(self.w_used.sem, blocks * BLOCK_UNITS + UNITS)
                eng.wait_ge(self.stored.sem, blocks + 1)
                eng.sem_inc(spare.sem, 1)
                copy(self.YS[0:CAP, 512 * half:512 * (half + 1)], ps[0:CAP, 5 + half, :]).then_inc(self.y_kept.sem, 1)

            def act(self, L):
                act, NT = L.eng, self.NT
                begin(L, "act")
                def store_rows(t):
                    L.wait(self.rows_turned, t + 1)
                    if t >= 2:
                        L.wait(self.rows_out[t % 2], 16)
                    L.inc(act.copy(self.ROWS[t % 2], ps[:, 1 + 2 * (t % 2):3 + 2 * (t % 2), :].rearrange("p b n -> p (b n)")),
                          self.rows_kept)
                    L.join()
                    act.dma_start(f_rows[t * P:(t + 1) * P, :], self.ROWS[t % 2]).then_inc(self.rows_out[t % 2].sem, 16)

                L.wait(self.less_max, 1)
                L.inc(act.activation(self.GP, self.GP, ACT.Exp), self.exps)
                for t in range(2):
                    store_rows(t)
                L.wait(self.less_max, 2)
                L.inc(act.activation(self.ES, self.ES, ACT.Exp), self.exps)
                for t in range(2, NT):
                    store_rows(t)
                L.wait(self.table_kept, 1)

                keep_rows = self.keep_rows

                def round_tokens():
                    for c in range(2):
                        act.copy(self.XS[:, 0, 4 * c:4 * c + 4, :].rearrange("p k t -> p (k t)"), ps[:, 3 + c, 0:4 * CAP])\
                           .then_inc(self.x_high.sem, 1)

                act.wait_ge(self.block_turned.sem, 1)
                round_tokens()
                with act.Fori(0, EXPERTS // 2) as pair:
                    for a in range(2):
                        lo, hi = self.range_of(act, pair, a)
                        with act.Fori(lo, hi) as b:
                            def round_weights(u):
                                if u % UNITS == 0:
                                    n = self.first + 3 * a + u // UNITS
                                    act.wait_ge(slot_in[place_of[n]].sem, pair * 16 + arrivals[n])
                                act.wait_ge(self.w_used.sem, b * BLOCK_UNITS + (u + 1))
                                act.copy(self.WH[:, u % UNITS, :], self.unit(a, u)).then_inc(self.w_high.sem, 1)

                            for u in range(UNITS):
                                round_weights(u)
                            keep_rows(act, 0, act.copy, b)
                            for u in range(UNITS, 2 * UNITS):
                                round_weights(u)
                            act.wait_ge(self.w_used.sem, b * BLOCK_UNITS + 2 * UNITS)
                            act.activation(self.SG[0:CAP], ps[0:CAP, 0, :], ACT.Silu).then_inc(self.gated.sem, 1)
                            for u in range(2 * UNITS, 3 * UNITS - 1):
                                round_weights(u)
                            for c, bank in enumerate((2, 7)):
                                act.wait_ge(self.hidden_turned.sem, b * 2 + (c + 1))
                                act.copy(self.HS[:, 0, 2 * c:2 * c + 2, :].rearrange("p k t -> p (k t)"), ps[:, bank, 0:2 * CAP])\
                                   .then_inc(self.h_high.sem, 1)
                            round_weights(3 * UNITS - 1)
                            act.wait_ge(self.block_turned.sem, b + 2)
                            round_tokens()
                keep_rows(act, 0, act.copy, self.count_of(act))
                L.last = None
                L.wait(self.scattered_all, 1)
                for t in range(NT):
                    if t >= 2:
                        L.wait(self.sum_made, t - 1)
                    act.dma_start(self.PAIRS[t % 2], y_rows[2 * P * t:2 * P * (t + 1), :].rearrange("(p c) d -> p c d", c=2))\
                       .then_inc(self.pairs_in[t % 2].sem, 16)
                end(L, "act")

            def dve(self, L):
                v, NT, NB = L.eng, self.NT, self.NB
                begin(L, "dve")

                def lanes(ap, n):
                    return ap.to_broadcast([P, NT, n])

                def row(ap, n):
                    return ap.unsqueeze(1).to_broadcast([P, NT, n])

                def step(ins, signal=None):
                    L.inc(ins, signal)
                    L.join()

                def first_of_largest(values, n, cand, one_hot):
                    step(v.tensor_reduce(self.M1[:, :, 0], values, X, ALU.max))
                    step(v.tensor_tensor(cand, values, lanes(self.M1, n), ALU.is_ge))
                    step(v.scalar_tensor_tensor(out=cand, in0=cand, scalar=-64.0, in1=row(IOTA[:, 0:n], n),
                                                op0=ALU.mult, op1=ALU.add))
                    step(v.tensor_reduce(self.M1[:, :, 0], cand, X, ALU.min))
                    step(v.tensor_tensor(one_hot, cand, lanes(self.M1, n), ALU.is_equal))

                def softmax(values, out_ap, n, turn):
                    step(v.tensor_reduce(self.M1[:, :, 0], values, X, ALU.max))
                    step(v.tensor_tensor(out_ap, values, lanes(self.M1, n), ALU.subtract), self.less_max)
                    L.wait(self.exps, turn)
                    step(v.tensor_reduce(self.M1[:, :, 0], out_ap, X, ALU.add))
                    step(v.reciprocal(self.M2[:, :, 0], self.M1[:, :, 0]))
                    step(v.tensor_tensor(out_ap, out_ap, lanes(self.M2, n), ALU.mult))

                def pick(out_ap, values, weights, n):
                    t = self.TMP[:, :, 0:n]
                    step(v.tensor_tensor(t, values, weights, ALU.mult))
                    step(v.tensor_reduce(out_ap[:, :, 0], t, X, ALU.add))

                bias = vcol("router_bias", 36, 36 * self.l)
                L.wait(self.logits_made, 1)
                L.inc(v.tensor_copy(self.SUM[0:36, 0:self.T], ps[0:36, 7, 0:self.T]), self.logits_copied)
                L.wait(self.logits, 1)
                step(v.tensor_copy(self.LOG.rearrange("p t n -> p (t n)"), ps[:, 0, 0:36 * NT]), self.logits_kept)
                softmax(self.LOG[:, :, 0:GROUPS], self.GP, GROUPS, 1)
                step(v.tensor_tensor(self.GB, self.GP, row(bias[:, 0:GROUPS], GROUPS), ALU.add))
                first_of_largest(self.GB, GROUPS, self.CG, self.OG)
                pick(self.GW, self.GP, self.OG, GROUPS)
                by_group = self.TMP.rearrange("p t (g j) -> p t g j", g=GROUPS)
                by_expert = self.TMP.rearrange("p t (g j) -> p t j g", g=GROUPS)
                group4 = self.OG.unsqueeze(3).to_broadcast([P, NT, GROUPS, PER_GROUP])
                for o, values in ((self.EL, self.LOG[:, :, GROUPS:36].rearrange("p t (g j) -> p t g j", g=GROUPS)),
                                  (self.EB, bias[:, GROUPS:36].rearrange("p (g j) -> p g j", g=GROUPS).unsqueeze(1)
                                   .to_broadcast([P, NT, GROUPS, PER_GROUP]))):
                    step(v.tensor_tensor(by_group, values, group4, ALU.mult))
                    step(v.tensor_reduce(o, by_expert, X, ALU.add))
                softmax(self.EL, self.ES, PER_GROUP, 2)
                step(v.tensor_tensor(self.EB, self.ES, self.EB, ALU.add))
                for c in range(2):
                    first_of_largest(self.EB, PER_GROUP, self.CE, self.OE[c])
                    pick(self.WT[c], self.ES, self.OE[c], PER_GROUP)
                    step(v.scalar_tensor_tensor(out=self.EB, in0=self.OE[c], scalar=MASKED, in1=self.EB, op0=ALU.mult, op1=ALU.add))
                    step(v.tensor_tensor(self.O32[c].rearrange("p t (g j) -> p t g j", g=GROUPS),
                                         self.OE[c].unsqueeze(2).to_broadcast([P, NT, GROUPS, PER_GROUP]), group4, ALU.mult))
                step(v.tensor_tensor(self.BOTH, self.O32[0], self.O32[1], ALU.add), self.chosen)
                step(v.tensor_tensor(self.WS, self.WT[0], self.WT[1], ALU.add))
                step(v.reciprocal(self.WS, self.WS))
                step(v.tensor_tensor(self.WS, self.WS, self.GW, ALU.mult))
                for c in range(2):
                    step(v.tensor_tensor(self.WT[c], self.WT[c], self.WS, ALU.mult))
                L.wait(self.counts, 1)
                step(v.tensor_copy(self.CNT[0:EXPERTS, :], ps[0:EXPERTS, 6, 0:P]))
                step(v.tensor_scalar(self.NBLK[0:EXPERTS, :], self.CNT[0:EXPERTS, :], float(CAP), 1.0, ALU.is_gt, ALU.add))
                for r in range(2, -(-self.T // CAP)):
                    step(v.scalar_tensor_tensor(out=self.NBLK[0:EXPERTS, :], in0=self.CNT[0:EXPERTS, :], scalar=float(r * CAP),
                                                in1=self.NBLK[0:EXPERTS, :], op0=ALU.is_gt, op1=ALU.add))
                v.sem_inc(self.counts_kept.sem, 1)
                L.wait(self.firsts, 1)
                step(v.tensor_copy(self.FIRST, ps[:, 0, 0:EXPERTS + 1]))
                step(v.tensor_copy(self.FIRSTI, self.FIRST))
                step(v.tensor_scalar(self.UNITS_BEFORE, self.FIRST, float(BLOCK_UNITS), -float(BLOCK_UNITS), ALU.mult, ALU.add))
                step(v.tensor_copy(self.UNITS_BEFOREI, self.UNITS_BEFORE))
                for c in range(2):
                    step(v.tensor_tensor(self.TMP, ps[:, 5, 0:32 * NT].rearrange("p (t e) -> p t e", t=NT), self.O32[c], ALU.mult))
                    step(v.tensor_reduce(self.RANK[c][:, :, 0], self.TMP, X, ALU.add))
                    pick(self.BLK[c], row(self.FIRST[:, 0:EXPERTS], EXPERTS), self.O32[c], EXPERTS)
                    step(v.tensor_scalar(self.QUOT[c], self.RANK[c], float(CAP), None, ALU.is_ge))
                    for r in range(2, -(-self.T // CAP)):
                        step(v.scalar_tensor_tensor(out=self.QUOT[c], in0=self.RANK[c], scalar=float(r * CAP), in1=self.QUOT[c],
                                                    op0=ALU.is_ge, op1=ALU.add))
                    step(v.tensor_tensor(self.BLK[c], self.BLK[c], self.QUOT[c], ALU.add))
                    step(v.scalar_tensor_tensor(out=self.RANK[c], in0=self.QUOT[c], scalar=-float(CAP), in1=self.RANK[c],
                                                op0=ALU.mult, op1=ALU.add))
                for t in range(NT):
                    for c in range(2):
                        L.inc(v.tensor_scalar(self.AT_PLACE[t][c], IOTA[:, 0:CAP], self.RANK[c][:, t, :], None, ALU.is_equal))
                        L.inc(v.tensor_scalar(self.AT_BLOCK[t][c][:, 0, :], IOTA[:, 0:NB], self.BLK[c][:, t, :],
                                              PLACE[:, c, t:t + 1], ALU.is_equal, ALU.mult))
                        L.inc(v.tensor_scalar(self.AT_BLOCK[t][c][:, 1, :], IOTA[:, 0:NB], self.BLK[c][:, t, :],
                                              PLACE[:, 2, t:t + 1], ALU.is_equal, ALU.mult), self.places)
                L.wait(self.table, 1)
                tab = ps[0:CAP, 6, 0:2 * NB].rearrange("p (c b) -> p c b", c=2)
                step(v.tensor_scalar(self.EMPTY[0:CAP], tab, 0.5, OUT_OF_BOUNDS, ALU.is_lt, ALU.mult))
                step(v.scalar_tensor_tensor(out=self.TAB[0:CAP], in0=tab, scalar=-1.0, in1=self.EMPTY[0:CAP], op0=ALU.add, op1=ALU.add))
                step(v.tensor_copy(self.TABI[0:CAP], self.TAB[0:CAP]), self.table_kept)

                keep_rows = self.keep_rows

                def split_tokens(blocks):
                    for c in range(2):
                        v.wait_ge(self.x_high.sem, blocks * 2 + (c + 1))
                        v.tensor_tensor(self.XS[:, 1, 4 * c:4 * c + 4, :].rearrange("p k t -> p (k t)"), ps[:, 3 + c, 0:4 * CAP],
                                        high(self.XS[:, 0, 4 * c:4 * c + 4, :]).rearrange("p k t -> p (k t)"), ALU.subtract)\
                         .then_inc(self.x_split.sem, 1)

                split_tokens(0)
                with v.Fori(0, EXPERTS // 2) as pair:
                    for a in range(2):
                        lo, hi = self.range_of(v, pair, a)
                        with v.Fori(lo, hi) as b:
                            def split_weights(u):
                                v.wait_ge(self.w_high.sem, b * BLOCK_UNITS + (u + 1))
                                v.tensor_tensor(self.WL[:, u % UNITS, :], self.unit(a, u), high(self.WH[:, u % UNITS, :]),
                                                ALU.subtract).then_inc(self.w_split.sem, 1)

                            for u in range(UNITS):
                                split_weights(u)
                            keep_rows(v, 1, v.tensor_copy, b)
                            for u in range(UNITS, 3 * UNITS - 2):
                                split_weights(u)
                            v.wait_ge(self.gated.sem, b + 1)
                            v.wait_ge(self.w_used.sem, b * BLOCK_UNITS + 3 * UNITS)
                            v.tensor_tensor(self.H[0:CAP], self.SG[0:CAP], ps[0:CAP, 1, :], ALU.mult)\
                             .then_inc(self.multiplied.sem, 1)
                            split_weights(3 * UNITS - 2)
                            for c, bank in enumerate((2, 7)):
                                v.wait_ge(self.h_high.sem, b * 2 + (c + 1))
                                v.tensor_tensor(self.HS[:, 1, 2 * c:2 * c + 2, :].rearrange("p k t -> p (k t)"), ps[:, bank, 0:2 * CAP],
                                                high(self.HS[:, 0, 2 * c:2 * c + 2, :]).rearrange("p k t -> p (k t)"), ALU.subtract)\
                                 .then_inc(self.h_split.sem, 1)
                            split_weights(3 * UNITS - 1)
                            split_tokens(b + 1)
                keep_rows(v, 1, v.tensor_copy, self.count_of(v))
                for t in range(NT):
                    L.wait(self.pairs_in[t % 2], 16 * (t // 2 + 1))
                    if t >= 1:
                        L.wait(self.sum_turned, t)
                    step(v.tensor_scalar(self.SUM, self.PAIRS[t % 2][:, 0, :], self.WT[0][:, t, :], None, ALU.mult))
                    step(v.scalar_tensor_tensor(out=self.SUM, in0=self.PAIRS[t % 2][:, 1, :], scalar=self.WT[1][:, t, :],
                                                in1=self.SUM, op0=ALU.mult, op1=ALU.add), self.sum_made)
                    L.wait(self.sum_turned, t + 1)
                    for k in range(KD):
                        xs = XT[:, k, t * P:(t + 1) * P]
                        ins = v.scalar_tensor_tensor(out=xs, in0=ps[:, 5 + k // 4, k % 4 * P:(k % 4 + 1) * P],
                                                     scalar=MOD[self.l][:, 5 * KD + k, t * P // TL:t * P // TL + 1], in1=xs,
                                                     op0=ALU.mult, op1=ALU.add)
                        L.inc(ins, self.sum_added if k == KD - 1 else None)
                end(L, "dve")

            def pool(self, L):
                g, NT = L.eng, self.NT
                g.sem_inc(self.stored.sem, 2)
                g.sem_inc(self.w_used.sem, UNITS)
                L.wait(self.logits_kept, 1)
                g.memset(self.XG[0:CAP], 0.0).then_inc(self.index_g.sem, 1)
                L.wait(self.table_kept, 1)
                for i in range(2):
                    L.wait(self.rows_out[i], 16 * (NT // 2))
                blocks = self.count_of(g)

                def gather(block, indices):
                    g.tensor_copy(self.IDXG[0:CAP], self.TABI[0:CAP, 1, block]).then_inc(self.index_g.sem, 1)
                    g.wait_ge(self.index_g.sem, indices + 1)
                    g.sem_inc(spare.sem, 1)
                    g.indirect_dma_start(out=self.XG[0:CAP], out_offset=None, in_=f_rows[:, :],
                                         in_offset=bass.IndirectOffsetOnAxis(ap=self.IDXG[0:CAP], axis=0),
                                         bounds_check=self.T - 1, oob_is_err=False).then_inc(self.gathered.sem, 16)

                gather(slice(0, 1), 1)
                g.wait_ge(self.gathered.sem, 16)
                g.wait_ge(self.block_turned.sem, 1)
                gather(slice(1, 2), 2)
                with g.Fori(0, blocks) as b:
                    g.wait_ge(self.gathered.sem, b * 16 + 32)
                    g.wait_ge(self.block_turned.sem, b + 2)
                    g.sem_inc(spare.sem, 1)
                    gather(bass.ds(b + 2, 1), b + 3)
                    g.tensor_copy(self.IDXS[0:CAP], self.TABI[0:CAP, 0, bass.ds(b, 1)]).then_inc(self.index_s.sem, 1)
                    g.wait_ge(self.index_s.sem, b + 1)
                    g.wait_ge(self.y_kept.sem, b * 2 + 4)
                    g.sem_inc(spare.sem, 1)
                    g.indirect_dma_start(out=y_rows[:, :], out_offset=bass.IndirectOffsetOnAxis(ap=self.IDXS[0:CAP], axis=0),
                                         in_=self.YS[0:CAP], in_offset=None, bounds_check=2 * self.T - 1,
                                         oob_is_err=False).then_inc(self.scattered.sem, 16)
                    g.wait_ge(self.scattered.sem, b * 16 + 16)
                    g.sem_inc(self.stored.sem, 1)
                g.wait_ge(self.gathered.sem, blocks * 16 + 32)
                g.sem_inc(self.scattered_all.sem, 1)

        take = carver()
        CG = take(4 * TL).rearrange("p (m t) -> p m t", m=4)
        CU = take(4 * (TL + 2)).rearrange("p (m t) -> p m t", m=4)
        CZ = take(4 * TL).rearrange("p (m t) -> p m t", m=4)
        BZ = take(KD * TL).rearrange("p (m t) -> p m t", m=KD)

        class Conv:
            def __init__(self):
                self.tiles = sig("conv_tiles")
                self.kept = sig("conv_kept")
                self.gate_in = sig("conv_gate_in")
                self.y_tiles = sig("conv_y_tiles")
                self.y_added = sig("conv_y_added")
                win = w["conv_w_in"][0]
                self.slots = []
                for half in range(2):
                    for part in (1, 2, 0):
                        c0 = part * D + half * 512
                        self.slots.append(plan(columns(win, c0, c0 + 512), (KD, 512), (self.tiles, 4 * len(self.slots) + 4)))
                self.wo = [plan(columns(w["conv_w_out"][0], 512 * i, 512 * (i + 1)), (KD, 512), (self.y_tiles, 4 * i + 4))
                           for i in range(2)]

            def pe(self, L):
                pe = L.eng
                for s, n in enumerate(self.slots):
                    slot_ready(L, n)
                    wv = slot(n).rearrange("p (k n) -> p k n", k=KD)
                    for t in range(4):
                        i = 4 * s + t
                        if i >= 4:
                            if (s - 1) % 3 == 0:
                                L.wait(self.gate_in, 4 * ((s - 1) // 3) + t + 1)
                            else:
                                L.wait(self.kept, 4 * (2 * ((s - 1) // 3) + (s - 1) % 3 - 1) + t + 1)
                        for k in range(KD):
                            if i == 0:
                                L.wait(norms[2].done, k + 1)
                            mm = pe.matmul(ps[:, t, 0:TL], wv[:, k, t * P:(t + 1) * P], A[:, k, 0:TL], start=k == 0, stop=k == KD - 1)
                        L.inc(mm, self.tiles)
                for m in range(KD):
                    if m % 4 == 0:
                        slot_ready(L, self.wo[m // 4])
                    if m == 0:
                        L.wait(self.kept, 16)
                    if m >= 4:
                        L.wait(self.y_added, m - 3)
                    wv = slot(self.wo[m // 4]).rearrange("p (k n) -> p k n", k=KD)
                    for k in range(KD):
                        mm = pe.matmul(ps[:, m % 4, 0:TL], wv[:, k, m % 4 * P:(m % 4 + 1) * P], BZ[:, k, :],
                                       start=k == 0, stop=k == KD - 1)
                    L.inc(mm, self.y_tiles)
                end(L, "pe")

            def act(self, L):
                begin(L, "act")
                for half in range(2):
                    for t in range(4):
                        L.wait(self.tiles, 12 * half + t + 1)
                        if half:
                            L.wait(self.kept, 8)
                        L.inc(L.eng.copy(CG[:, t, :], ps[:, t, 0:TL]), self.gate_in)
                end(L, "act")

            def dve(self, L):
                v = L.eng
                begin(L, "dve")
                taps = vcol("conv", 3 * KD).rearrange("p (j m) -> p j m", j=3)
                L.inc(v.memset(CU[:, :, 0:1], 0.0))
                L.inc(v.memset(CU[:, :, TL + 1:TL + 2], 0.0))
                L.join()
                for half in range(2):
                    for t in range(4):
                        L.wait(self.gate_in, 4 * half + t + 1)
                        L.wait(self.tiles, 12 * half + 4 + t + 1)
                        L.inc(v.tensor_tensor(CU[:, t, 1:TL + 1], CG[:, t, :], ps[:, t, 0:TL], ALU.mult), self.kept)
                    for t in range(4):
                        m = 4 * half + t
                        L.join()
                        L.inc(v.tensor_scalar(CZ[:, t, :], CU[:, t, 0:TL], taps[:, 0, m:m + 1], None, ALU.mult))
                        for j in (1, 2):
                            L.join()
                            L.inc(v.scalar_tensor_tensor(out=CZ[:, t, :], in0=CU[:, t, j:j + TL], scalar=taps[:, j, m:m + 1],
                                                         in1=CZ[:, t, :], op0=ALU.mult, op1=ALU.add))
                        L.wait(self.tiles, 12 * half + 8 + t + 1)
                        L.join()
                        L.inc(v.tensor_tensor(BZ[:, m, :], CZ[:, t, :], ps[:, t, 0:TL], ALU.mult), self.kept)
                gated_add(L, 1, 0, TL, self.y_tiles, self.y_added)
                end(L, "dve")

        take = carver()
        heads_at = arena_at
        H0 = take((AH + AKV + RH) * TL)

        def inside(at, heads):
            return H0[0:HD, at:at + heads * TL].rearrange("p (h t) -> p h t", h=heads)
        QA, KA, QT = inside(0, AH), inside(AH * TL, AKV), inside((AH + AKV) * TL, RH)
        LN_TILES = arena[:, 0:KD * TA].rearrange("p (k t) -> p k t", k=KD)
        KR = take(RH * TL)[0:HD].rearrange("p (h t) -> p h t", h=RH)
        VA = take(2 * P).rearrange("p (t c) -> p t c", t=2)
        VR = take(2 * 512).rearrange("p (t c) -> p t c", t=2)
        GR = take(4 * TL).rearrange("p (m t) -> p m t", m=4)
        RAW = [take(TL) for _ in range(2)]
        R1, R2 = take(TL), take(TL)
        SC = [take(3 * P) for _ in range(2)]
        PT = [take(3 * P) for _ in range(2)]
        SM = [take(16) for _ in range(2)]
        HS = place("HS", [P, 2, FFT, TL], F32R, heads_at)
        XS = place("XS", [P, 2, KD, TL], F32R, A_at)
        WS = place("WS", [P, 2, UNITS, UNIT], F32R, ring_at + 4 * RING_2 * SLOT)
        SA = [take(TL) for _ in range(2)]
        HF = [take(TL) for _ in range(2)]
        MIXC = take(4 * TL + 3 * P + 3 * P + P + RH * TL)
        Y = A[:, 0:4, :].rearrange("p k t -> p (k t)").rearrange("p (m t) -> p m t", m=KD)
        O4 = A[:, 4:6, :].rearrange("p k t -> p (k t)").rearrange("p (m t) -> p m t", m=4)
        O2 = A[:, 6:8, :].rearrange("p k t -> p (k t)").rearrange("p (m t) -> p m t", m=4)
        COS_A, SIN_A, COS_R, SIN_R = (MIXC[:, i * TL:(i + 1) * TL] for i in range(4))
        TURN_A, TURN_R, HEAD_MEAN = (MIXC[:, 4 * TL + i * P:4 * TL + (i + 1) * P] for i in range(3))
        MASK = MIXC[:, 4 * TL + 3 * P:4 * TL + 6 * P]
        MEAN = MIXC[:, 4 * TL + 6 * P:4 * TL + 7 * P]
        DECAY = MIXC[:, 4 * TL + 7 * P:].rearrange("p (h t) -> p h t", h=RH)
        LNP = sb("LNP", [P, 6 * KD + AH])
        SINK = LNP[:, 6 * KD:]

        class Ffn:

            def __init__(self, ln, use, gu, dn):
                self.ln, self.gu, self.dn = ln, gu, dn
                self.ahead = use == 1
                self.w_high = shared("split_high", FFN_UNITS, 2)
                self.w_split = shared("split_ready", FFN_UNITS, 2)
                self.w_used = shared("split_used", FFN_UNITS, 2)
                self.x_split = stream_split(use, 1)[1]
                self.silu = shared("ffn_silu", FFT, 2)
                self.hidden = shared("ffn_hidden", FFT, 2)
                self.h_high = shared("ffn_h_high", FFT, 2)
                self.h_split = shared("ffn_h_split", FFT, 2)
                self.y_added = shared("ffn_y_added", KD, 2)

            def plan(self, l):
                gu = w[self.gu][l].rearrange("(k p) (a n) -> p k a n", p=P, a=2)
                first = len(loads)
                for s in range(FFT // 2):
                    plan(gu[:, :, :, 2 * P * s:2 * P * (s + 1)], (KD, 2, 2 * P), (self.w_split, 4 * s + 4, l))
                for m in range(KD):
                    plan(columns(w[self.dn][l], P * m, P * (m + 1)), (FFT, P), (self.w_split, 2 * FFT + 3 * m + 3, l))
                if l == 0:
                    self.first = first

            def unit(self, u):
                if u < 2 * FFT:
                    f, a = u // 2, u % 2
                    n = self.first + f // 2
                    wv = slot(n).rearrange("p (k a n) -> p k a n", k=KD, a=2)
                    return n, wv[:, :, a, f % 2 * P:(f % 2 + 1) * P], range(KD)
                m, third = (u - 2 * FFT) // 3, (u - 2 * FFT) % 3
                n = self.first + FFT // 2 + m
                tiles = range(KD * third, min(KD * (third + 1), FFT))
                wv = slot(n)[:, 0:FFT * P].rearrange("p (k n) -> p k n", k=FFT)
                return n, wv[:, tiles.start:tiles.stop, :], tiles

            def parts(self, u):
                count = len(self.unit(u)[2])
                return [WS[:, j, u % UNITS, 0:count * P].rearrange("p (k n) -> p k n", k=count) for j in range(2)]

            def units_used(self, L, count):
                L.wait(self.w_used, count + UNITS)

            def round_weights(self, L, u):
                n, source, _ = self.unit(u)
                slot_ready(L, n)
                self.units_used(L, u + 1 - UNITS)
                L.inc(L.eng.copy(self.parts(u)[0], source), self.w_high)

            def split_weights(self, L, u):
                wh, wl = self.parts(u)
                L.wait(self.w_high, u + 1)
                L.inc(L.eng.tensor_tensor(wl, self.unit(u)[1], high(wh), ALU.subtract), self.w_split)

            def pe(self, L):
                def products(u, out_ap, moving):
                    L.wait(self.w_split, u + 1)
                    wh, wl = self.parts(u)
                    tiles = self.unit(u)[2]
                    total = KD if u < 2 * FFT else FFT
                    for i, k in enumerate(tiles):
                        if u < 2:
                            L.wait(self.x_split, k + 1)
                        elif 2 * FFT <= u < 2 * FFT + 3:
                            L.wait(self.h_split, k + 1)
                        for weights, j in ((wh, 0), (wh, 1), (wl, 0)):
                            mm = L.eng.matmul(out_ap, weights[:, i, :], moving[:, j, k, :], start=k == 0 and weights is wh and j == 0,
                                              stop=k == total - 1 and weights is wl)
                    L.inc(mm, self.w_used)

                for f in range(FFT):
                    if f >= 2:
                        L.wait(self.hidden, f - 1)
                    for a in range(2):
                        products(2 * f + a, ps[:, 2 * (f % 2) + a, 0:TL], XS)
                for m in range(KD):
                    if m >= 2:
                        L.wait(self.y_added, m - 1)
                    for third in range(3):
                        products(2 * FFT + 3 * m + third, ps[:, 4 + m % 2, 0:TL], HS)
                    if m >= 1:
                        self.ln.mean_tile(L, self.y_added, m - 1)
                self.ln.mean_tile(L, self.y_added, KD - 1)
                end(L, "pe")

            def act(self, L):
                act = L.eng

                def round_weights(u):
                    if u < FFN_UNITS:
                        self.round_weights(L, u)

                if not self.ahead:
                    for u in range(UNITS):
                        round_weights(u)
                for f in range(FFT):
                    round_weights(UNITS + 2 * f)
                    self.units_used(L, 2 * f + 1)
                    if f >= 2:
                        L.wait(self.hidden, f - 1)
                    L.inc(act.activation(SA[f % 2], ps[:, 2 * (f % 2), 0:TL], ACT.Silu), self.silu)
                    round_weights(UNITS + 2 * f + 1)
                    L.wait(self.hidden, f + 1)
                    L.inc(act.copy(HS[:, 0, f, :], HF[f % 2]), self.h_high)
                for u in range(UNITS + 2 * FFT, FFN_UNITS):
                    round_weights(u)
                end(L, "act")

            def dve(self, L):
                v = L.eng

                def split_weights(u):
                    if u < FFN_UNITS:
                        self.split_weights(L, u)

                if not self.ahead:
                    for u in range(UNITS):
                        split_weights(u)
                for f in range(FFT):
                    split_weights(UNITS + 2 * f)
                    L.wait(self.silu, f + 1)
                    self.units_used(L, 2 * f + 2)
                    if f >= 2:
                        L.wait(self.h_split, f - 1)
                    L.inc(v.tensor_tensor(HF[f % 2], SA[f % 2], ps[:, 2 * (f % 2) + 1, 0:TL], ALU.mult), self.hidden)
                    split_weights(UNITS + 2 * f + 1)
                    L.wait(self.h_high, f + 1)
                    L.inc(v.tensor_tensor(HS[:, 1, f, :], HF[f % 2], high(HS[:, 0, f, :]), ALU.subtract), self.h_split)
                for m in range(KD):
                    for third in range(3):
                        split_weights(2 * FFT + UNITS + 3 * m + third)
                    self.units_used(L, 2 * FFT + 3 * m + 3)
                    L.inc(v.scalar_tensor_tensor(out=XT[:, m, 0:TL], in0=ps[:, 4 + m % 2, 0:TL], scalar=0.5 / ALPHA,
                                                 in1=XT[:, m, 0:TL], op0=ALU.mult, op1=ALU.add), self.y_added)
                end(L, "dve")

        def residual(L, m, tiles, added, scale):
            L.wait(tiles, m + 1)
            L.inc(L.eng.scalar_tensor_tensor(out=XT[:, m, 0:TL], in0=ps[:, m % 4, 0:TL], scalar=scale,
                                             in1=XT[:, m, 0:TL], op0=ALU.mult, op1=ALU.add), added)

        class Mixer:

            ROTATED = ([("qa", t) for t in range(4)] + [("ka", 0)] + [("qr", t) for t in range(4)] + [("kr", t) for t in range(4)])

            def __init__(self, ln_before, ln, ffn):
                self.ln_before, self.ln, self.ffn = ln_before, ln, ffn
                self.tiles = sig("mix_tiles", 13)
                self.raw = sig("mix_raw", 13)
                self.turned = sig("mix_turned", 13)
                self.rotated = sig("mix_rotated", 13)
                self.values = sig("mix_values", 4)
                self.values_kept = sig("mix_values_kept", 4)
                self.gates = sig("mix_gates", 4)
                self.gates_kept = sig("mix_gates_kept", 4)
                self.scores = sig("mix_scores", AH)
                self.neg = sig("mix_neg", AH)
                self.exps = sig("mix_exps", 3 * AH)
                self.probs = sig("mix_probs", AH)
                self.p_turned = sig("mix_p_turned", AH)
                self.p_kept = sig("mix_p_kept", AH)
                self.outs = sig("mix_outs", AH)
                self.outs_kept = sig("mix_outs_kept", AH)
                self.r_scores = sig("mix_r_scores", RH)
                self.decayed = sig("mix_decayed", RH)
                self.r_outs = sig("mix_r_outs", RH)
                self.r_outs_kept = sig("mix_r_outs_kept", RH)
                self.means = sig("mix_means", 4)
                self.centred = sig("mix_centred", 4)
                self.squares = sig("mix_squares", 4)
                self.vars = sig("mix_vars", 4)
                self.var = sig("mix_var", 4)
                self.std = sig("mix_std", 4)
                self.y_ready = sig("mix_y_ready", 4)
                self.y_tiles = sig("mix_y_tiles", KD)
                self.y_added = sig("mix_y_added", KD)

            def plan(self, l):
                first = len(loads)
                win = w["w_in_2"][l]
                for c0, c1, freed in ((0, 512, (self.tiles, 4, l)), (512, 768, (self.values, 2, l)),
                                      (768, 1280, (self.tiles, 9, l)), (1280, 1792, (self.tiles, 13, l)),
                                      (1792, 2304, (self.values, 4, l)), (2304, 2816, (self.gates, 4, l))):
                    plan(columns(win, c0, c1), (KD, c1 - c0), freed)
                for i in range(4):
                    plan(columns(w["w_out_2"][l], 256 * i, 256 * (i + 1)), (KD, 256), (self.y_tiles, 2 * i + 2, l))
                if l == 0:
                    self.first = first

            def weights(self, j, width):
                return slot(self.first + j)[:, 0:KD * width].rearrange("p (k n) -> p k n", k=KD)

            def pe(self, L):
                pe = L.eng

                def turn(i):
                    L.wait(self.raw, i + 1)
                    if i >= 2:
                        L.wait(self.rotated, i - 1)
                    L.inc(pe.matmul(ps[:, 2 + i % 2, 0:TL], TURN_A if i < 5 else TURN_R, RAW[i % 2], start=True, stop=True), self.turned)

                def values(count, wv, width):
                    for t in range(2):
                        for k in range(KD):
                            mm = pe.matmul(ps[:, 4 + t, 0:width], XT[:, k, t * P:(t + 1) * P], wv[:, k, :], start=k == 0, stop=k == KD - 1)
                        L.inc(mm, self.values)

                for i, (part, t) in enumerate(self.ROTATED):
                    j = {"qa": 0, "ka": 1, "qr": 2, "kr": 3}[part]
                    if t == 0:
                        slot_ready(L, self.first + j)
                    wv = self.weights(j, 256 if j == 1 else 512)
                    if i >= 2:
                        L.wait(self.raw, i - 1)
                    for k in range(KD):
                        if i == 0:
                            L.wait(self.ln_before.done, k + 1)
                        mm = pe.matmul(ps[:, i % 2, 0:TL], wv[:, k, t * P:(t + 1) * P], XT[:, k, 0:TL], start=k == 0, stop=k == KD - 1)
                    L.inc(mm, self.tiles)
                    if i:
                        turn(i - 1)
                    if part == "ka":
                        values(0, wv[:, :, P:2 * P], P)
                turn(12)
                slot_ready(L, self.first + 4)
                L.wait(self.values_kept, 2)
                values(2, self.weights(4, 512), 512)
                slot_ready(L, self.first + 5)
                wv = self.weights(5, 512)
                L.wait(self.raw, 13)
                for t in range(4):
                    if t >= 2:
                        L.wait(self.gates_kept, t - 1)
                    for k in range(KD):
                        mm = pe.matmul(ps[:, t % 2, 0:TL], wv[:, k, t * P:(t + 1) * P], XT[:, k, 0:TL], start=k == 0, stop=k == KD - 1)
                    L.inc(mm, self.gates)

                def scores(h):
                    b = h % 2
                    if h >= 2:
                        L.wait(self.probs, h - 1)
                    pe.matmul(ps[:, b, 0:P], QA[:, h, 0:P], KA[:, h // 4, 0:P], start=True, stop=True)
                    L.inc(pe.matmul(ps[:, b, P:3 * P], QA[:, h, P:TL], KA[:, h // 4, :], start=True, stop=True), self.scores)

                def turn_probs(h):
                    b = h % 2
                    L.wait(self.probs, h + 1)
                    if h >= 2:
                        L.wait(self.p_kept, h - 1)
                    for c in range(3):
                        mm = pe.transpose(ps[:, 2 + b, c * P:(c + 1) * P], SC[b][:, c * P:(c + 1) * P], IDENT)
                    L.inc(mm, self.p_turned)

                def finish(h):
                    b = h % 2
                    L.wait(self.p_kept, h + 1)
                    if h >= 2:
                        L.wait(self.outs_kept, h - 1)
                    kv = slice(h // 4 * HD, (h // 4 + 1) * HD)
                    pe.matmul(ps[0:HD, 4 + b, 0:P], VA[:, 0, kv], PT[b][:, 0:P], start=True, stop=True)
                    for c in range(2):
                        mm = pe.matmul(ps[0:HD, 4 + b, P:TL], VA[:, c, kv], PT[b][:, (1 + c) * P:(2 + c) * P], start=c == 0, stop=c == 1)
                    L.inc(mm, self.outs)

                L.wait(self.rotated, 13)
                L.wait(self.values_kept, 4)
                L.wait(self.gates_kept, 4)
                scores(0)
                scores(1)
                for h in range(AH):
                    turn_probs(h)
                    if h + 2 < AH:
                        scores(h + 2)
                    finish(h)

                def r_scores(h):
                    b = h % 2
                    if h >= 2:
                        L.wait(self.decayed, h - 1)
                    pe.matmul(ps[:, b, 0:TL], KR[:, h, 0:P], QT[:, h, :], start=True, stop=True)
                    L.inc(pe.matmul(ps[:, b, TL:3 * P], KR[:, h, P:TL], QT[:, h, P:TL], start=True, stop=True), self.r_scores)

                def r_finish(h):
                    b = h % 2
                    L.wait(self.decayed, h + 1)
                    if h >= 2:
                        L.wait(self.r_outs_kept, h - 1)
                    e = slice(h * HD, (h + 1) * HD)
                    pe.matmul(ps[0:HD, 2 + b, 0:P], VR[:, 0, e], SC[b][:, 0:P], start=True, stop=True)
                    pe.matmul(ps[0:HD, 2 + b, P:TL], VR[:, 0, e], SC[b][:, P:TL], start=True, stop=False)
                    L.inc(pe.matmul(ps[0:HD, 2 + b, P:TL], VR[:, 1, e], SC[b][:, TL:3 * P], start=False, stop=True), self.r_outs)

                L.wait(self.outs_kept, AH)
                r_scores(0)
                for h in range(1, RH):
                    r_scores(h)
                    r_finish(h - 1)
                r_finish(RH - 1)
                for m in range(4):
                    L.wait(self.r_outs_kept, 2 * m + 2)
                    if m >= 2:
                        L.wait(self.centred, m - 1)
                    L.inc(pe.matmul(ps[:, 4 + m % 2, (m // 2) * TL:(m // 2 + 1) * TL], HEAD_MEAN, O4[:, m, :], start=True, stop=True), self.means)
                L.wait(self.decayed, RH)
                for m in range(4):
                    L.wait(self.squares, m + 1)
                    if m >= 2:
                        L.wait(self.var, m - 1)
                    L.inc(pe.matmul(ps[:, m % 2, (m // 2) * TL:(m // 2 + 1) * TL], HEAD_MEAN, O2[:, m, :], start=True, stop=True), self.vars)
                L.wait(self.y_ready, 4)
                for m in range(KD):
                    if m % 2 == 0:
                        slot_ready(L, self.first + 6 + m // 2)
                    if m >= 4:
                        L.wait(self.y_added, m - 3)
                    wv = self.weights(6 + m // 2, 256)
                    for k in range(KD):
                        mm = pe.matmul(ps[:, m % 4, 0:TL], wv[:, k, m % 2 * P:(m % 2 + 1) * P], Y[:, k, :], start=k == 0, stop=k == KD - 1)
                    L.inc(mm, self.y_tiles)
                    if m >= 1:
                        self.ln.mean_tile(L, self.y_added, m - 1)
                self.ln.mean_tile(L, self.y_added, KD - 1)
                end(L, "pe")

            def act(self, L):
                act = L.eng
                begin(L, "act")
                for i, (part, t) in enumerate(self.ROTATED):
                    L.wait(self.tiles, i + 1)
                    if i >= 2:
                        L.wait(self.rotated, i - 1)
                    scale = HD ** -0.5 if part in ("qa", "kr") else 1.0
                    L.inc(act.activation(RAW[i % 2], ps[:, i % 2, 0:TL], ACT.Copy, scale=scale), self.raw)
                    if part == "qr" and t == 0:
                        for t2 in range(2):
                            L.wait(self.values, t2 + 1)
                            L.inc(act.copy(VA[:, t2, :], ps[:, 4 + t2, 0:P]), self.values_kept)
                for t in range(2):
                    L.wait(self.values, 3 + t)
                    L.inc(act.copy(VR[:, t, :], ps[:, 4 + t, :]), self.values_kept)
                for t in range(4):
                    L.wait(self.gates, t + 1)
                    L.inc(act.activation(GR[:, t, :], ps[:, t % 2, 0:TL], ACT.Silu), self.gates_kept)

                def keep_out(h, source, tile, signal):
                    half = slice(h % 2 * HD, (h % 2 + 1) * HD)
                    L.inc(act.copy(tile[half, h // 2, :], source), signal)

                for h in range(AH):
                    b = h % 2
                    L.wait(self.neg, h + 1)
                    for c, cols in enumerate((slice(0, P), slice(P, 3 * P))):
                        L.inc(act.activation(SC[b][:, cols], SC[b][:, cols], ACT.Exp, bias=SM[b][:, 4 + c:5 + c],
                                             accum_out=SM[b][:, 6 + c:7 + c]), self.exps)
                    L.inc(act.activation(SM[b][:, 8:10], SM[b][:, 4:6], ACT.Exp, bias=SINK[:, h:h + 1]), self.exps)
                    if h:
                        L.wait(self.outs, h)
                        keep_out(h - 1, ps[0:HD, 4 + (h - 1) % 2, 0:TL], Y, self.outs_kept)
                L.wait(self.outs, AH)
                keep_out(AH - 1, ps[0:HD, 4 + (AH - 1) % 2, 0:TL], Y, self.outs_kept)
                for h in range(RH):
                    L.wait(self.r_outs, h + 1)
                    keep_out(h, ps[0:HD, 2 + h % 2, 0:TL], O4, self.r_outs_kept)
                for m in range(4):
                    L.wait(self.centred, m + 1)
                    L.inc(act.activation(O2[:, m, :], O4[:, m, :], ACT.Square), self.squares)
                for m in range(4):
                    L.wait(self.var, m + 1)
                    L.inc(act.activation(O2[:, m, :], O2[:, m, :], ACT.Sqrt), self.std)
                for u in range(UNITS):
                    self.ffn.round_weights(L, u)
                end(L, "act")

            def dve(self, L):
                v = L.eng
                begin(L, "dve")
                v.wait_ge(mix_in.sem, 16)
                for i, (part, t) in enumerate(self.ROTATED):
                    cos, sin = (COS_A, SIN_A) if i < 5 else (COS_R, SIN_R)
                    L.wait(self.raw, i + 1)
                    L.inc(v.tensor_tensor(R1, RAW[i % 2], cos, ALU.mult))
                    L.wait(self.turned, i + 1)
                    L.inc(v.tensor_tensor(R2, ps[:, 2 + i % 2, 0:TL], sin, ALU.mult))
                    L.join()
                    to = {"qa": QA, "ka": KA, "qr": QT, "kr": KR}[part]
                    L.inc(v.tensor_tensor(to[:, 2 * t, :], R1[0:HD], R2[0:HD], ALU.add))
                    L.inc(v.tensor_tensor(to[:, 2 * t + 1, :], R1[HD:P], R2[HD:P], ALU.add), self.rotated)
                    L.join()
                def mask_scores(h):
                    b = h % 2
                    L.wait(self.scores, h + 1)
                    if h >= 2:
                        L.wait(self.p_turned, h - 1)
                    L.inc(v.tensor_tensor(SC[b], ps[:, b, 0:3 * P], MASK, ALU.add))
                    L.join()
                    L.inc(v.tensor_reduce(SM[b][:, 0:1], SC[b][:, 0:P], X, ALU.max))
                    L.inc(v.tensor_reduce(SM[b][:, 1:2], SC[b][:, P:3 * P], X, ALU.max))
                    L.join()
                    L.inc(v.tensor_scalar(SM[b][:, 4:6], SM[b][:, 0:2], SINK[:, h:h + 1], -1.0, ALU.max, ALU.mult), self.neg)

                mask_scores(0)
                for h in range(AH):
                    b = h % 2
                    if h + 1 < AH:
                        mask_scores(h + 1)
                    L.wait(self.exps, 3 * h + 3)
                    L.inc(v.tensor_tensor(SM[b][:, 10:12], SM[b][:, 6:8], SM[b][:, 8:10], ALU.add))
                    L.join()
                    L.inc(v.reciprocal(SM[b][:, 12:14], SM[b][:, 10:12]))
                    L.join()
                    L.inc(v.tensor_scalar(SC[b][:, 0:P], SC[b][:, 0:P], SM[b][:, 12:13], None, ALU.mult))
                    L.inc(v.tensor_scalar(SC[b][:, P:3 * P], SC[b][:, P:3 * P], SM[b][:, 13:14], None, ALU.mult), self.probs)
                    L.wait(self.p_turned, h + 1)
                    L.inc(v.tensor_copy(PT[b], ps[:, 2 + b, 0:3 * P]), self.p_kept)
                for h in range(RH):
                    b = h % 2
                    L.wait(self.r_scores, h + 1)
                    if h >= 2:
                        L.wait(self.r_outs, h - 1)
                    L.inc(v.tensor_tensor(SC[b][:, 0:TL], ps[:, b, 0:TL], DECAY[:, h, :], ALU.mult))
                    L.inc(v.tensor_tensor(SC[b][:, TL:3 * P], ps[:, b, TL:3 * P], DECAY[:, h, 0:P], ALU.mult), self.decayed)

                def half_bank(m, bank):
                    return ps[:, bank + m % 2, (m // 2) * TL:(m // 2 + 1) * TL]
                for m in range(4):
                    L.wait(self.means, m + 1)
                    L.inc(v.tensor_tensor(O4[:, m, :], O4[:, m, :], half_bank(m, 4), ALU.subtract), self.centred)
                for m in range(4):
                    L.wait(self.vars, m + 1)
                    L.inc(v.tensor_scalar(O2[:, m, :], half_bank(m, 0), GN_EPS, None, ALU.add), self.var)
                for m in range(4):
                    L.wait(self.std, m + 1)
                    L.inc(v.reciprocal(O2[:, m, :], O2[:, m, :]))
                    L.inc(v.tensor_tensor(O4[:, m, :], O4[:, m, :], GR[:, m, :], ALU.mult))
                    L.join()
                    L.inc(v.tensor_tensor(Y[:, 4 + m, :], O4[:, m, :], O2[:, m, :], ALU.mult), self.y_ready)
                for m in range(KD):
                    residual(L, m, self.y_tiles, self.y_added, 1.0 / ALPHA)
                    if m >= KD - UNITS:
                        self.ffn.split_weights(L, m - (KD - UNITS))
                end(L, "dve")

        mods = [None, None]
        mods[0] = Mod(0)
        norms = [Norm("norm0", 0, 0, TA), Norm("norm1", 0, 1, TA), Norm("norm2", 1, 0, TL), Norm("norm3", 1, 1, TL),
                 Norm("norm4", 1, 2, TL)]
        mla = Mla()
        moes = [None, None]
        mods[1] = Mod(1)
        moes[0] = Moe(0, TA, norms[1])
        conv = Conv()
        moes[1] = Moe(1, TL, norms[3])
        layer_first = len(loads)
        second_stack.append(layer_first)
        lns = [LayerNorm(i) for i in range(3)]
        ffns = [Ffn(lns[0], 0, "ffn1_w_gu_2", "ffn1_w_down_2"), Ffn(lns[2], 1, "ffn2_w_gu_2", "ffn2_w_down_2")]
        mixer = Mixer(lns[0], lns[1], ffns[1])
        for l in range(LAYERS):
            before_layer = [s.n for s in slot_in]
            ffns[0].plan(l)
            mixer.plan(l)
            ffns[1].plan(l)
            for s, count in zip(slot_in, before_layer):
                s.per_turn = s.n - count
        assert (len(loads) - layer_first) % (RING_2 * LAYERS) == 0
        first_stack = [mods[0], norms[0], mla, mods[1], norms[1], moes[0], norms[2], conv, norms[3], moes[1], norms[4]]
        layer = [ffns[0], lns[0], mixer, lns[1], ffns[1], lns[2]]
        assert len(layer) == PER_LAYER_STAGES

        block = ctx.enter_context(nc.Block())

        @block.sync
        def _(sp):
            sp.dma_start(VECS[:, :], vec).then_inc(const_in.sem, 16)
            sp.dma_start(BASE[:, :], base_c).then_inc(const_in.sem, 16)

            def load(n):
                if before[n] is not None and frees[before[n]][1]:
                    sp.wait_ge(*frees[before[n]])
                for dst, src in loads[n]:
                    sp.dma_start(dst, src).then_inc(slot_in[place_of[n]].sem, 16)

            n = 0
            while n < len(loads):
                moe = next((m for m in moes if m.first == n - RING), None)
                if moe is None:
                    load(n)
                    n += 1
                    if n == RING:
                        sp.dma_start(XT[:, :, :], xT).then_inc(x_in.sem, 16)
                        sp.dma_start(MLAC, mla_c).then_inc(mla_in.sem, 16)
                    continue
                sp.wait_ge(moe.table_kept.sem, moe.table_kept.base + 1)

                def units_before(e):
                    return sp.value_load(moe.UNITS_BEFOREI[0:1, bass.ds(e, 1)], min_val=0, max_val=moe.NB * BLOCK_UNITS)

                with sp.Fori(0, EXPERTS // 2 - 1) as pair:
                    for a in range(2):
                        e = pair * 2 + (2 + a)
                        units = units_before(pair * 2 + (a + 1))
                        for j, name in enumerate(("moe_w_gate", "moe_w_up", "moe_w_down")):
                            sp.wait_ge(moe.w_split.sem, units + (j + 1) * UNITS)
                            dst = loads[n + 3 * a + j][0][0]
                            src = w[name][moe.l][bass.ds(e, 1)].rearrange("o (k p) n -> p (o k) n", p=P)
                            sp.dma_start(dst, src).then_inc(slot_in[place_of[n + 3 * a + j]].sem, 16)
                sp.wait_ge(moe.w_split.sem, units_before(EXPERTS - 1) + BLOCK_UNITS)
                sp.sem_inc(spare.sem, 1)
                n += 3 * EXPERTS - RING
            sp.wait_ge(stages_done.sem, 3 * (len(first_stack) + 1 + LAYERS * len(layer)))
            sp.dma_start(out, XT[:, :, 0:TL]).then_inc(const_in.sem, 16)
            sp.wait_ge(const_in.sem, 48)

        @block.gpsimd
        def _(pool):
            L = Lane(pool, line["pool"], spare)
            for m in moes:
                m.pool(L)

        @block.scalar
        def _(act):
            L = Lane(act, line["act"], spare)
            act.wait_ge(const_in.sem, 32)
            L.inc(act.activation(COND[:, :, :], vcol("cond", 2 * KD).rearrange("p (k a) -> p k a", a=2), ACT.Silu))
            L.join()
            L.inc(act.copy(COND_SPLIT[:, :, 0:2], COND[:, :, :]))
            end(L, "act")
            for s in first_stack:
                s.act(L)
            L.eng.wait_ge(stages_done.sem, 3 * counters["act"])
            act.dma_start(MIXC, mix_c).then_inc(mix_in.sem, 16)
            L.line, L.last = loop_line["act"], None
            with act.Fori(0, LAYERS) as l:
                L.turn = l
                for s in layer:
                    s.act(L)
            assert loop_line["act"].n == ACT_PER_LAYER, loop_line["act"].n

        @block.tensor
        def _(pe):
            L = Lane(pe, line["pe"], spare)
            pe.sem_inc(ffns[0].w_used.sem, UNITS)
            end(L, "pe")
            for s in first_stack:
                s.pe(L)
            with pe.Fori(0, LAYERS) as l:
                L.turn = l
                for s in layer:
                    s.pe(L)

        @block.vector
        def _(dve):
            L = Lane(dve, line["dve"], spare)
            dve.wait_ge(const_in.sem, 32)
            L.inc(dve.tensor_tensor(FOLD[:, :], IDENT[0:4, 0:2], IDENT[0:4, 2:4], ALU.add))
            dve.wait_ge(line["act"].sem, 2)
            L.inc(dve.tensor_tensor(COND_SPLIT[:, :, 2:4], COND[:, :, :], high(COND_SPLIT[:, :, 0:2]), ALU.subtract))
            end(L, "dve")
            for s in first_stack:
                s.dve(L)
            L.line, L.last = loop_line["dve"], None
            with dve.Fori(0, LAYERS) as l:
                L.turn = l
                dve.wait_ge(stages_done.sem, l * (3 * PER_LAYER_STAGES) + 3 * counters["dve"])
                L.settle()
                L.inc(dve.tensor_copy(LNP[:, 0:6 * KD], VECS[:, bass.ds(l * (6 * KD) + VEC["ln"], 6 * KD)]))
                L.inc(dve.tensor_copy(SINK, VECS[:, bass.ds(l * AH + VEC["sinks"], AH)]))
                L.join()
                for s in layer:
                    s.dve(L)
            assert loop_line["dve"].n == DVE_PER_LAYER, loop_line["dve"].n


WEIGHTS = ["w_mod", "mla_w_dq", "mla_w_uq", "mla_w_dkv", "mla_w_ukv", "mla_w_o", "conv_w_in", "conv_w_out",
           "moe_w_gate", "moe_w_up", "moe_w_down", "w_in_2", "w_out_2",
           "ffn1_w_gu_2", "ffn1_w_down_2", "ffn2_w_gu_2", "ffn2_w_down_2"]


def lay_out(inputs):
    def features(a):
        a = np.asarray(a)
        a = a.reshape(-1, a.shape[-1] // P, P)
        return a.transpose(2, 0, 1).reshape(P, -1)

    def everywhere(a):
        return np.broadcast_to(np.asarray(a).reshape(1, -1), (P, np.asarray(a).size))

    a = {k: np.asarray(v) for k, v in inputs.items()}
    tokens = np.concatenate([a["x"][0], a["ctx"][0]], axis=0)
    xT = np.ascontiguousarray(tokens.T.reshape(KD, P, TA).transpose(1, 0, 2))
    cond = np.stack([a["c"][0], a["c_ctx"]], axis=1).reshape(KD, P, 2).transpose(1, 0, 2).reshape(P, -1)
    ln = np.stack([a[f"ln{i}_{s}_2"] for i in (1, 2, 3) for s in "gb"], axis=1)
    router = np.concatenate([a["moe_w_group"], a["moe_w_expert"]], axis=2).reshape(2, KD, P, 36)
    parts = {
        "cond": cond, "b_mod": features(a["b_mod"]), "norm_mix": features(a["norm_mix_g"]),
        "norm_ffn": features(a["norm_ffn_g"]), "final": features(a["final_norm_g"]), "g_q": features(a["mla_g_q"]),
        "g_kv": features(a["mla_g_kv"]), "conv": features(a["conv_w"][0]), "ln": features(ln),
        "router": router.transpose(2, 0, 1, 3).reshape(P, -1),
        "router_bias": everywhere(np.concatenate([a["moe_b_group"], a["moe_b_expert"]], axis=1)),
        "sinks": everywhere(a["attn_sinks_2"]),
    }
    return xT, np.ascontiguousarray(np.concatenate([parts[name] for name in VEC], axis=1))


def kernel(**inputs):
    import concourse.bacc as bacc
    from concourse.bass_utils import run_bass_kernel_spmd as run

    nc = bacc.Bacc("TRN2", target_bir_lowering=False, num_devices=1)
    arrays = {}

    def given(name, a):
        arrays[name] = np.ascontiguousarray(a)
        return nc.dram_tensor(name, arrays[name].shape, mybir.dt.from_np(arrays[name].dtype), kind="ExternalInput").ap()

    xT, vec = lay_out(inputs)
    base_c, mla_c, mix_c = shape_constants()
    args = [given("in_tokens", xT), given("in_vectors", vec), given("in_base", base_c), given("in_mla", mla_c),
            given("in_mix", mix_c)]
    weights = {name: given("in_" + name, inputs[name]) for name in WEIGHTS}
    out = nc.dram_tensor("out_features", (P, KD, TL), F32, kind="ExternalOutput").ap()
    program(nc, *args, weights, out)
    r = run(nc, [arrays], core_ids=[0])
    got = np.asarray(r.results[0]["out_features"])
    return np.ascontiguousarray(got.transpose(2, 1, 0).reshape(1, TL, D))
```

```python
from contextlib import ExitStack

import concourse.bass as bass
import numpy as np
from concourse import mybir

F32 = mybir.dt.float32
F32R = mybir.dt.float32r
I32 = mybir.dt.int32
ACT = mybir.ActivationFunctionType
ALU = mybir.AluOpType
X = mybir.AxisListType.X

P = 128
D = 1024
KD = D // P
TL = 256
TA = 512
NORM_EPS = 1e-6

HEADS = 8
Q_LORA, KV_LORA = 512, 256
NOPE, ROPE, DV = 128, 64, 128
QW = NOPE + ROPE
MLA_SCALE = float(QW) ** -0.5
GRID_W = 64

GROUPS, PER_GROUP = 4, 8
EXPERTS = GROUPS * PER_GROUP
FF = 512
FT = FF // P
CAP = 3 * P // 4
OUT_OF_BOUNDS = 4096.0

LAYERS = 2
D_FF = 2816
FFT = D_FF // P
HD = 64
AH, AKV, RH = 8, 2, 8
ALPHA = (2 * LAYERS) ** 0.25
LN_EPS, GN_EPS = 1e-5, 1e-6
MASKED = -1e30

RING = 6
SLOT = 4096
RING_2 = 4

UNIT = 1024
UNITS = (RING - RING_2) * SLOT // (2 * UNIT)
MIXER_UNITS = 4 * 5 + KD
CONV_AHEAD = 3
FFN_UNITS = 2 * FFT + KD * 3
BLOCK_UNITS = 3 * SLOT // UNIT
FIRST_BYTE = 16640


def blocks_of(tokens):
    return EXPERTS + 2 * tokens // (CAP + 1) + 2


def shape_constants():
    f = np.float32
    ident = np.eye(P, dtype=f)
    ones = np.ones((P, P), f)
    before = np.triu(np.ones((P, P), f), 1)
    iota = np.tile(np.arange(P, dtype=f), (P, 1))
    lane = np.arange(P)[:, None] + P * np.arange(4)[None, :]
    place = np.concatenate([2 * lane + 1, 2 * lane + 2, lane + 1], axis=1).astype(f)
    base = np.concatenate([ident, ones, before, iota, place], axis=1)

    def angles(pos, half, theta):
        freq = theta ** (-np.arange(half, dtype=f) / f(half))
        return (pos.astype(f)[:, None] * freq[None, :].astype(f)).astype(f)

    rows, cols = np.repeat(np.arange(TL // GRID_W), GRID_W), np.tile(np.arange(GRID_W), TL // GRID_W)
    quarter = ROPE // 4
    ang = np.concatenate([angles(p, quarter, f(10000.0)).T for p in (rows, rows, cols, cols)], axis=0)
    cos, sin = np.zeros((P, TA), f), np.zeros((P, TA), f)
    cos[:ROPE, :TL], sin[:ROPE, :TL] = np.cos(ang), np.sin(ang)
    cos[:ROPE, TL:] = 1.0
    turn = np.zeros((P, ROPE), f)
    for b in range(0, ROPE, 2 * quarter):
        for i in range(quarter):
            turn[b + quarter + i, b + i] = -1.0
            turn[b + i, b + quarter + i] = 1.0
    mla = np.concatenate([cos, sin, turn], axis=1)

    pos = np.arange(TL, dtype=f)
    half = HD // 2
    inv = (f(10000.0) ** (-np.arange(0, HD, 2, dtype=f) / f(HD))).astype(f)
    a = (pos[:, None] * inv[None, :]).astype(f).T
    a = np.concatenate([a, a, a, a], axis=0)
    inv = (f(1.0) / (f(10000.0) ** np.linspace(0.0, 1.0, half, dtype=f))).astype(f)
    r = (pos[:, None] * inv[None, :]).astype(f).T
    r = np.repeat(r, 2, axis=0)
    r = np.concatenate([r, r], axis=0)
    turn_a, turn_r = np.zeros((P, P), f), np.zeros((P, P), f)
    for b in range(0, P, HD):
        for i in range(half):
            turn_a[b + half + i, b + i] = -1.0
            turn_a[b + i, b + half + i] = 1.0
            turn_r[b + 2 * i + 1, b + 2 * i] = -1.0
            turn_r[b + 2 * i, b + 2 * i + 1] = 1.0
    head_mean = np.kron(np.eye(2, dtype=f), np.full((HD, HD), 1.0 / HD, f))
    q, k = np.arange(P)[:, None], np.arange(P)[None, :]
    own = np.where(q >= k, 0.0, MASKED).astype(f)
    prev = np.where(q - k + P < P, 0.0, MASKED).astype(f)
    mask = np.concatenate([own, prev, own], axis=1)
    log_gamma = np.log1p(-np.exp2(-5.0 - np.arange(RH, dtype=f))).astype(f)
    diff = np.arange(TL, dtype=f)[None, :] - np.arange(P, dtype=f)[:, None]
    decay = [np.where(diff >= 0, np.exp(np.maximum(diff, 0.0) * g), 0.0).astype(f) for g in log_gamma]
    mix = np.concatenate([np.cos(a), np.sin(a), np.cos(r), np.sin(r), turn_a, turn_r, head_mean, mask,
                          ones / f(D)] + decay, axis=1).astype(f)
    return base, mla, mix


VEC = {}
VEC_WIDTH = 0
for _name, _width in (("cond", 2 * KD), ("b_mod", 2 * 48), ("norm_mix", 2 * KD), ("norm_ffn", 2 * KD),
                      ("final", KD), ("g_q", 4), ("g_kv", 2), ("conv", 3 * KD), ("ln", LAYERS * 6 * KD),
                      ("router", 2 * KD * 36), ("router_bias", 2 * 36), ("sinks", LAYERS * AH)):
    VEC[_name] = VEC_WIDTH
    VEC_WIDTH += _width


ACT_PER_LAYER = 0
DVE_PER_LAYER = 108
SPLITS_PER_LAYER = 2 * FFN_UNITS + MIXER_UNITS
assert SPLITS_PER_LAYER % UNITS == 0


class Signal:

    def __init__(self, sem, base=0, per_turn=0):
        self.sem, self.base, self.n, self.per_turn = sem, base, base, per_turn


class Lane:

    def __init__(self, eng, line, spare):
        self.eng, self.line, self.spare, self.turn, self.last = eng, line, spare, None, None

    def wait(self, signal, value):
        value += signal.base
        if self.turn is not None and signal.per_turn:
            value = self.turn * signal.per_turn + value
        self.eng.wait_ge(signal.sem, value)

    def inc(self, ins, signal=None):
        signal = signal or self.line
        ins.then_inc(signal.sem, 1)
        signal.n += 1
        self.last = (signal, signal.n - signal.base)

    def join(self):
        self.wait(*self.last)

    def settle(self):
        self.eng.sem_inc(self.spare.sem, 1)


def program(nc, xT, vec, base_c, mla_c, mix_c, w, out):
    ctx = ExitStack()
    with ctx:
        used_bytes = [FIRST_BYTE]

        def place(name, shape, dt, at):
            return nc.alloc_sbuf_tensor_at(name, shape, dt, offset=at)

        def sb(name, shape, dt=F32):
            at = used_bytes[0]
            used_bytes[0] += (4 * int(np.prod(shape[1:])) + 31) // 32 * 32
            return place(name, shape, dt, at)

        def sig(name, per_turn=0):
            return Signal(ctx.enter_context(nc.semaphore(name)), 0, per_turn)

        reused = {}

        def shared(name, count, turns=0):
            if name not in reused:
                reused[name] = [ctx.enter_context(nc.semaphore(name)), 0]
            sem, base = reused[name]
            reused[name][1] += count
            return Signal(sem, base, count * turns)

        ring_at = used_bytes[0]
        ring = sb("ring", [P, RING, SLOT])
        XT = sb("XT", [P, KD, TA])
        A_at = used_bytes[0]
        A = sb("A", [P, KD, TA])
        VECS = sb("VECS", [P, VEC_WIDTH])
        BASE = sb("BASE", [P, 4 * P + 12])
        RS = sb("RS", [P, 2, TA])
        COND = sb("COND", [P, KD, 2])
        MOD = [sb(f"MOD{l}", [P, 48, 2]) for l in range(2)]
        GAIN = [sb(f"GAIN{l}", [P, 2, KD, 2]) for l in range(2)]
        ARENA_W = 17496
        arena_at = used_bytes[0]
        arena = sb("arena", [P, ARENA_W])
        ps = ctx.enter_context(nc.psum_tensor("ps", [P, 8, 512], F32))

        IDENT, ONES, BEFORE, IOTA = (BASE[:, i * P:(i + 1) * P] for i in range(4))
        PLACE = BASE[:, 4 * P:4 * P + 12].rearrange("p (c t) -> p c t", c=3)

        def vcol(name, width, shift=0):
            return VECS[:, VEC[name] + shift:VEC[name] + shift + width]

        def carver():
            used = [0]

            def take(width):
                at = used[0]
                used[0] += width
                assert used[0] <= ARENA_W, (used[0], ARENA_W)
                return arena[:, at:at + width]
            return take

        f_rows = nc.dram_tensor("f_rows", [TA, D], F32, kind="Internal").ap()
        y_rows = nc.dram_tensor("y_rows", [2 * TA, D], F32, kind="Internal").ap()

        const_in = sig("const_in")
        x_in = sig("x_in")
        mla_in = sig("mla_in")
        mix_in = sig("mix_in")
        stages_done = sig("stages_done")
        slot_in = [sig(f"slot_in{i}") for i in range(RING)]
        spare = sig("spare")
        line = {e: sig(f"line_{e}") for e in ("pe", "act", "dve", "pool")}
        loop_line = {"act": sig("loop_line_act", ACT_PER_LAYER), "dve": sig("loop_line_dve", DVE_PER_LAYER)}

        loads, frees, arrivals, place_of, before = [], [], [], [], []
        second_stack = []

        def slot(n):
            return ring[:, place_of[n], :]

        def plan(src, shape, freed_by):
            n = len(loads)
            at = (n - second_stack[0]) % RING_2 if second_stack else n % RING
            before.append(max((i for i in range(n) if place_of[i] == at), default=None))
            place_of.append(at)
            width = int(np.prod(shape))
            dst = slot(n)[:, 0:width]
            if len(shape) == 2:
                dst = dst.rearrange("p (k n) -> p k n", k=shape[0])
            elif len(shape) == 3:
                dst = dst.rearrange("p (k a n) -> p k a n", k=shape[0], a=shape[1])
            parts = [(dst, src)] if len(shape) == 2 else [(dst[:, :, a, :], src[:, :, a, :]) for a in range(shape[1])]
            loads.append(parts)
            slot_in[at].n += 16 * len(parts)
            arrivals.append(slot_in[at].n)
            signal, value, turn = (*freed_by, 0)[:3]
            frees.append((signal.sem, signal.base + signal.per_turn * turn + value))
            return n

        def columns(weight, c0, c1):
            return weight[:, c0:c1].rearrange("(k p) n -> p k n", p=P)

        def slot_ready(L, n, later=0):
            L.wait(slot_in[place_of[n]], arrivals[n] + later * slot_in[place_of[n]].per_turn)

        PER_LAYER_STAGES = 6
        counters = {"pe": 0, "act": 0, "dve": 0}

        def begin(L, name):
            s = counters[name]
            if s:
                value = 3 * s
                if L.turn is not None:
                    value = L.turn * (3 * PER_LAYER_STAGES) + value
                L.eng.wait_ge(stages_done.sem, value)
                if L.turn is not None:
                    L.settle()

        def end(L, name):
            if L.last:
                L.join()
            L.eng.sem_inc(stages_done.sem, 1)
            counters[name] += 1

        def high(ap):
            return ap.bitcast(F32)

        FOLD = sb("FOLD", [4, 2])
        COND_SPLIT = place("COND_SPLIT", [P, KD, 4], F32R, used_bytes[0])
        used_bytes[0] += 4 * 4 * KD
        MOD_WS = place("MOD_WS", [P, 2, UNITS, UNIT], F32R, arena_at)

        class Mod:

            def __init__(self, l):
                self.l = l
                self.w_high = shared("split_high", 48)
                self.w_split = shared("split_ready", 48)
                self.w_used = shared("split_used", 48)
                self.rows_kept = sig(f"mod{l}_rows_kept", 6)
                self.turned = sig(f"mod{l}_turned", 6)
                self.kept = sig(f"mod{l}_kept", 1)
                self.first = len(loads)
                for s in range(12):
                    plan(columns(w["w_mod"][l], 512 * s, 512 * (s + 1)), (KD, 512), (self.w_split, 4 * (s + 1)))
                for signal in (self.w_high, self.w_split, self.w_used):
                    signal.per_turn = 24

            def unit(self, u):
                return slot(self.first + u // 4).rearrange("p (k n) -> p k n", k=KD)[:, 2 * (u % 4):2 * (u % 4) + 2, :]

            def parts(self, u):
                return [MOD_WS[:, j, u % UNITS, :].rearrange("p (k n) -> p k n", k=2) for j in range(2)]

            def units_used(self, L, count):
                L.wait(self.w_used, count + UNITS)

            def pe(self, L):
                begin(L, "pe")
                with L.eng.Fori(0, 2) as turn:
                    L.turn = turn

                    def turn_rows(s):
                        if s == 0:
                            L.eng.wait_ge(self.kept.sem, turn + 1)
                        L.wait(self.rows_kept, s + 1)
                        L.settle()
                        for t in range(4):
                            c = 4 * s + t
                            mm = L.eng.matmul(ps[:, 0, 2 * c:2 * c + 2], RS[0:4, s % 2, t * P:(t + 1) * P], FOLD[:, :],
                                              start=True, stop=True)
                        L.inc(mm, self.turned)

                    for s in range(6):
                        for q in range(4):
                            u = 4 * s + q
                            L.wait(self.w_split, u + 1)
                            for j, weights in enumerate(self.parts(u)):
                                for i in range(2):
                                    mm = L.eng.matmul(ps[0:4, 1 + s % 2, :], COND_SPLIT[:, 2 * q + i, :], weights[:, i, :],
                                                      start=q + i + j == 0, stop=q + i + j == 5)
                            L.inc(mm, self.w_used)
                        if s:
                            turn_rows(s - 1)
                    turn_rows(5)
                L.turn, L.last = None, (self.turned, 12)
                end(L, "pe")

            def act(self, L):
                begin(L, "act")
                with L.eng.Fori(0, 2) as turn:
                    L.turn = turn

                    def keep_rows(s):
                        self.units_used(L, 4 * s + 4)
                        if s >= 2:
                            L.wait(self.turned, s - 1)
                        L.inc(L.eng.copy(RS[0:4, s % 2, :], ps[0:4, 1 + s % 2, :]), self.rows_kept)

                    for s in range(6):
                        n = self.first + s
                        L.eng.wait_ge(slot_in[place_of[n]].sem, turn * 16 + arrivals[n])
                        for q in range(4):
                            u = 4 * s + q
                            self.units_used(L, u + 1 - UNITS)
                            L.inc(L.eng.copy(self.parts(u)[0], self.unit(u)), self.w_high)
                        if s:
                            keep_rows(s - 1)
                    keep_rows(5)
                L.turn, L.last = None, (self.rows_kept, 12)
                end(L, "act")

            def dve(self, L):
                begin(L, "dve")
                L.eng.sem_inc(self.kept.sem, 1)
                b = vcol("b_mod", 48, 48 * self.l)
                mod, gain = MOD[self.l], GAIN[self.l]
                with L.eng.Fori(0, 2) as turn:
                    L.turn = turn
                    for u in range(24):
                        wh, wl = self.parts(u)
                        L.wait(self.w_high, u + 1)
                        L.inc(L.eng.tensor_tensor(wl, self.unit(u), high(wh), ALU.subtract), self.w_split)
                    L.wait(self.turned, 6)
                    half = bass.ds(turn * 24, 24)
                    L.eng.tensor_tensor(mod[:, half, :], ps[:, 0, 0:48].rearrange("p (c a) -> p c a", a=2),
                                        b[:, half].unsqueeze(2).to_broadcast([P, 24, 2]),
                                        ALU.add).then_inc(self.kept.sem, 1)
                L.turn = None
                L.last = (self.kept, 3)
                L.join()
                for which, name in enumerate(("norm_mix", "norm_ffn")):
                    g = vcol(name, KD, KD * self.l).unsqueeze(2).to_broadcast([P, KD, 2])
                    at = KD * (3 * which + 1)
                    L.inc(L.eng.scalar_tensor_tensor(out=gain[:, which], in0=mod[:, at:at + KD, :], scalar=1.0,
                                                     in1=g, op0=ALU.add, op1=ALU.mult))
                end(L, "dve")

        x_high, x_split = sig("x_high"), sig("x_split")

        def stream_split(use, per_turn):
            return [Signal(s.sem, KD * use, 3 * KD * per_turn) for s in (x_high, x_split)]

        def stream_high(L, made, k, signals):
            L.wait(made, k + 1)
            L.inc(L.eng.copy(XS[:, 0, k, :], XT[:, k, 0:TL]), signals[0])

        def stream_low(L, k, signals):
            L.wait(signals[0], k + 1)
            L.inc(L.eng.tensor_tensor(XS[:, 1, k, :], XT[:, k, 0:TL], high(XS[:, 0, k, :]), ALU.subtract), signals[1])

        class Norm:
            def __init__(self, name, l, which, tokens):
                self.l, self.which, self.T = l, which, tokens
                plain = which == 2
                self.split = stream_split(0, 0)
                self.sq_act = shared("norm_sq_act", KD // 2)
                self.sq_dve = shared("norm_sq_dve", KD // 2)
                self.sums = shared("norm_sums", 1)
                self.var = shared("norm_var", 1)
                self.std = shared("norm_std", 1)
                self.scaled = shared("norm_scaled", KD)
                self.done = shared("norm_done", 0 if plain else KD * tokens // TL)

            def pe(self, L):
                begin(L, "pe")
                for k in range(KD):
                    L.wait(self.sq_dve if k % 2 else self.sq_act, k // 2 + 1)
                    mm = L.eng.matmul(ps[:, 6, 0:self.T], ONES, A[:, k, 0:self.T], start=k == 0, stop=k == KD - 1)
                L.inc(mm, self.sums)
                end(L, "pe")

            def act(self, L):
                begin(L, "act")
                if self.l == 0 and self.which == 0:
                    L.eng.wait_ge(x_in.sem, 16)
                T = self.T
                for k in range(0, KD, 2):
                    L.inc(L.eng.activation(A[:, k, 0:T], XT[:, k, 0:T], ACT.Square), self.sq_act)
                if self is norms[2]:
                    for i in range(CONV_AHEAD):
                        conv.round_weights(L, i)
                if self is norms[4]:
                    for u in range(2):
                        ffns[0].round_weights(L, u)
                L.wait(self.var, 1)
                L.inc(L.eng.activation(RS[:, 0, 0:T], RS[:, 0, 0:T], ACT.Sqrt), self.std)
                if self is norms[4]:
                    for u in range(2, UNITS):
                        ffns[0].round_weights(L, u)
                if self.which < 2:
                    gain, mod = GAIN[self.l], MOD[self.l]
                    for k in range(KD):
                        L.wait(self.scaled, k + 1)
                        for c in range(T // TL):
                            a = A[:, k, c * TL:(c + 1) * TL]
                            L.inc(L.eng.activation(a, a, ACT.Identity, bias=mod[:, 3 * KD * self.which + k, c:c + 1],
                                                   scale=gain[:, self.which, k, c:c + 1]), self.done)
                        if self is norms[2] and k:
                            conv.round_stream(L, k - 1)
                    if self is norms[2]:
                        conv.round_stream(L, KD - 1)
                else:
                    for k in range(KD):
                        stream_high(L, self.scaled, k, self.split)
                end(L, "act")

            def dve(self, L):
                begin(L, "dve")
                if self.l == 0 and self.which == 0:
                    L.eng.wait_ge(x_in.sem, 16)
                T = self.T
                for k in range(1, KD, 2):
                    L.inc(L.eng.tensor_tensor(A[:, k, 0:T], XT[:, k, 0:T], XT[:, k, 0:T], ALU.mult), self.sq_dve)
                if self is norms[2]:
                    for i in range(CONV_AHEAD):
                        conv.split_weights(L, i)
                L.wait(self.sums, 1)
                L.inc(L.eng.tensor_scalar(RS[:, 0, 0:T], ps[:, 6, 0:T], 1.0 / D, NORM_EPS, ALU.mult, ALU.add), self.var)
                if self is norms[4]:
                    for u in range(2):
                        ffns[0].split_weights(L, u)
                L.wait(self.std, 1)
                L.inc(L.eng.reciprocal(RS[:, 0, 0:T], RS[:, 0, 0:T]))
                L.join()
                for k in range(KD):
                    if self.which < 2:
                        L.inc(L.eng.tensor_tensor(A[:, k, 0:T], XT[:, k, 0:T], RS[:, 0, 0:T], ALU.mult), self.scaled)
                        if self is norms[2] and k >= 2:
                            conv.split_stream(L, k - 2)
                    else:
                        L.inc(L.eng.scalar_tensor_tensor(out=XT[:, k, 0:T], in0=XT[:, k, 0:T],
                                                         scalar=vcol("final", KD)[:, k:k + 1], in1=RS[:, 0, 0:T],
                                                         op0=ALU.mult, op1=ALU.mult), self.scaled)
                        if k >= 2:
                            stream_low(L, k - 2, self.split)
                if self is norms[2]:
                    for k in (KD - 2, KD - 1):
                        conv.split_stream(L, k)
                if self.which == 2:
                    for k in (KD - 2, KD - 1):
                        stream_low(L, k, self.split)
                    for u in range(2, UNITS):
                        ffns[0].split_weights(L, u)
                end(L, "dve")

        class LayerNorm:
            def __init__(self, i):
                self.i = i
                self.split = stream_split(i + 1, 1)
                self.mean = shared("ln_mean", 1, 3)
                self.centred = shared("ln_centred", KD, 3)
                self.squares = shared("norm_sq_act", KD, 3)
                self.sums = shared("norm_sums", 1, 3)
                self.var = shared("norm_var", 1, 3)
                self.std = shared("norm_std", 1, 3)
                self.scaled = shared("norm_scaled", KD, 3)
                self.done = shared("norm_done", KD, 3)

            def mean_tile(self, L, added, k):
                if k == 0:
                    L.eng.wait_ge(mix_in.sem, 16)
                L.wait(added, k + 1)
                mm = L.eng.matmul(ps[:, 6, 0:TL], MEAN, XT[:, k, 0:TL], start=k == 0, stop=k == KD - 1)
                if k == KD - 1:
                    L.inc(mm, self.mean)

            def pe(self, L):
                for k in range(KD):
                    L.wait(self.squares, k + 1)
                    mm = L.eng.matmul(ps[:, 7, 0:TL], MEAN, LN_TILES[:, k, TL:TA], start=k == 0, stop=k == KD - 1)
                L.inc(mm, self.sums)
                end(L, "pe")

            def act(self, L):
                for k in range(KD):
                    L.wait(self.centred, k + 1)
                    L.inc(L.eng.activation(LN_TILES[:, k, TL:TA], LN_TILES[:, k, 0:TL], ACT.Square), self.squares)
                L.wait(self.var, 1)
                L.inc(L.eng.activation(RS[:, 0, 0:TL], RS[:, 0, 0:TL], ACT.Sqrt), self.std)
                for k in range(KD):
                    L.wait(self.scaled, k + 1)
                    L.inc(L.eng.activation(XT[:, k, 0:TL], XT[:, k, 0:TL], ACT.Identity,
                                           bias=LNP[:, (2 * self.i + 1) * KD + k:(2 * self.i + 1) * KD + k + 1]), self.done)
                    if k:
                        stream_high(L, self.done, k - 1, self.split)
                stream_high(L, self.done, KD - 1, self.split)
                end(L, "act")

            def dve(self, L):
                L.wait(self.mean, 1)
                for k in range(KD):
                    L.inc(L.eng.tensor_tensor(LN_TILES[:, k, 0:TL], XT[:, k, 0:TL], ps[:, 6, 0:TL], ALU.subtract), self.centred)
                if self.next:
                    stage, later = self.next
                    stage.split_weights(L, UNITS - 1, later)
                L.wait(self.sums, 1)
                L.inc(L.eng.tensor_scalar(RS[:, 0, 0:TL], ps[:, 7, 0:TL], LN_EPS / ALPHA ** 2, None, ALU.add), self.var)
                L.wait(self.std, 1)
                L.inc(L.eng.reciprocal(RS[:, 0, 0:TL], RS[:, 0, 0:TL]))
                L.join()
                for k in range(KD):
                    L.inc(L.eng.scalar_tensor_tensor(out=XT[:, k, 0:TL], in0=LN_TILES[:, k, 0:TL],
                                                     scalar=LNP[:, 2 * self.i * KD + k:2 * self.i * KD + k + 1],
                                                     in1=RS[:, 0, 0:TL], op0=ALU.mult, op1=ALU.mult), self.scaled)
                    if k >= 2:
                        stream_low(L, k - 2, self.split)
                for k in (KD - 2, KD - 1):
                    stream_low(L, k, self.split)
                end(L, "dve")

        take = carver()
        KT = take(HEADS * TA).rearrange("p (h t) -> p h t", h=HEADS)
        V = take(4 * D).rearrange("p (t c) -> p t c", t=4)
        CKV = take(2 * TA).rearrange("p (c t) -> p c t", c=2)
        CQ = take(4 * TA).rearrange("p (c t) -> p c t", c=4)
        KPE, QN, QR, QRAW, T1 = (take(TA) for _ in range(5))
        PC = take(2 * TL).rearrange("p (q t) -> p q t", q=2)
        PTL = take(4 * TL).rearrange("p (k t) -> p k t", k=4)
        PTC = take(2 * TL).rearrange("p (k t) -> p k t", k=2)
        MLAC = take(2 * TA + ROPE)
        SMALL = take(16)
        PL = CKV
        SQ = [PTL[:, 0:2].rearrange("p a b -> p (a b)"), PTL[:, 2:4].rearrange("p a b -> p (a b)"),
              PTC.rearrange("p a b -> p (a b)"), PC.rearrange("p a b -> p (a b)"), QN, QR]
        OT = A
        COS, SIN, TURN = MLAC[0:ROPE, 0:TA], MLAC[0:ROPE, TA:2 * TA], MLAC[0:ROPE, 2 * TA:2 * TA + ROPE]
        MAXS, NEG, DEN, RDEN = (SMALL[:, 4 * i:4 * i + 4] for i in range(4))

        class Mla:
            def __init__(self):
                self.tiles = sig("mla_tiles")
                self.copied = sig("mla_copied")
                self.squares = sig("mla_squares")
                self.kpe_turned = sig("mla_kpe_turned")
                self.sums = sig("mla_sums")
                self.var = sig("mla_var")
                self.std = sig("mla_std")
                self.latents = sig("mla_latents")
                self.q_tiles = sig("mla_q_tiles")
                self.q_copied = sig("mla_q_copied")
                self.q_turned = sig("mla_q_turned")
                self.q_ready = sig("mla_q_ready")
                self.scores = sig("mla_scores")
                self.neg = sig("mla_neg")
                self.exps = sig("mla_exps")
                self.probs = sig("mla_probs")
                self.turned = sig("mla_turned")
                self.turned_copied = sig("mla_turned_copied")
                self.outs = sig("mla_outs")
                self.outs_copied = sig("mla_outs_copied")
                self.y_tiles = sig("mla_y_tiles")
                self.dkv = plan(columns(w["mla_w_dkv"][0], 0, 320), (KD, 320), (self.tiles, 3))
                self.dq = plan(columns(w["mla_w_dq"][0], 0, Q_LORA), (KD, Q_LORA), (self.tiles, 7))
                self.ukv = plan(columns(w["mla_w_ukv"][0], 0, 2048), (2, 2048), (self.tiles, 23))
                self.uq = [plan(columns(w["mla_w_uq"][0], 0, 5 * QW), (4, 5 * QW), (self.q_tiles, 10)),
                           plan(columns(w["mla_w_uq"][0], 5 * QW, 8 * QW), (4, 3 * QW), (self.q_tiles, 16))]
                self.wo = [plan(columns(w["mla_w_o"][0], 512 * i, 512 * (i + 1)), (HEADS, 512), (self.y_tiles, 4 * i + 4))
                           for i in range(2)]

            def q_weights(self, h, c0, c1):
                n = self.uq[0 if h < 5 else 1]
                heads = 5 if h < 5 else 3
                at = (h if h < 5 else h - 5) * QW
                return slot(n)[:, 0:4 * heads * QW].rearrange("p (k n) -> p k n", k=4)[:, :, at + c0:at + c1]

            def pe(self, L):
                pe = L.eng
                pe.wait_ge(mla_in.sem, 16)

                def squares_sum(first, count, bank):
                    for c in range(count):
                        L.eng.wait_ge(self.squares.sem, first + c + 1)
                        mm = pe.matmul(ps[:, bank, :], ONES, SQ[first + c], start=c == 0, stop=c == count - 1)
                    L.inc(mm, self.sums)

                i = 0
                for n, width, outs in ((self.dkv, 320, ((0, 128), (128, 256), (256, 320))),
                                       (self.dq, 512, tuple((c, c + 128) for c in range(0, 512, 128)))):
                    slot_ready(L, n)
                    wv = slot(n)[:, 0:KD * width].rearrange("p (k n) -> p k n", k=KD)
                    for c0, c1 in outs:
                        if i >= 4:
                            L.eng.wait_ge(self.copied.sem, i - 3)
                        for k in range(KD):
                            if i == 0:
                                L.wait(norms[0].done, (k + 1) * TA // TL)
                            mm = pe.matmul(ps[0:c1 - c0, i % 4, :], wv[:, k, c0:c1], A[:, k, :], start=k == 0, stop=k == KD - 1)
                        L.inc(mm, self.tiles)
                        i += 1
                        if i == 4:
                            squares_sum(0, 2, 5)
                L.eng.wait_ge(self.copied.sem, 3)
                L.inc(pe.matmul(ps[0:ROPE, 4, :], TURN, QRAW[0:ROPE, :], start=True, stop=True), self.kpe_turned)
                squares_sum(2, 4, 6)
                slot_ready(L, self.ukv)
                wv = slot(self.ukv).rearrange("p (k h a n) -> p k h a n", k=2, h=HEADS, a=2)
                L.eng.wait_ge(self.latents.sem, 2)
                for h in range(HEADS):
                    L.eng.wait_ge(self.copied.sem, i - 3)
                    for k in range(2):
                        mm = pe.matmul(ps[:, i % 4, :], wv[:, k, h, 0, :], CKV[:, k, :], start=k == 0, stop=k == 1)
                    L.inc(mm, self.tiles)
                    i += 1
                for t in range(4):
                    for half in range(2):
                        L.eng.wait_ge(self.copied.sem, i - 3)
                        for k in range(2):
                            mm = pe.matmul(ps[:, i % 4, :], CKV[:, k, t * P:(t + 1) * P],
                                           wv[:, k, 4 * half:4 * half + 4, 1, :], start=k == 0, stop=k == 1)
                        L.inc(mm, self.tiles)
                        i += 1
                L.eng.wait_ge(self.latents.sem, 6)

                def queries(h):
                    if h in (0, 5):
                        slot_ready(L, self.uq[0 if h < 5 else 1])
                    for k in range(4):
                        mm = pe.matmul(ps[:, 7, :], self.q_weights(h, 0, NOPE)[:, k, :], CQ[:, k, :], start=k == 0, stop=k == 3)
                    L.inc(mm, self.q_tiles)
                    if h == 0:
                        L.eng.wait_ge(self.var.sem, 2)
                    if h >= 2:
                        L.eng.wait_ge(self.outs_copied.sem, h - 1)
                    for k in range(4):
                        mm = pe.matmul(ps[0:ROPE, 6, :], self.q_weights(h, NOPE, QW)[:, k, :], CQ[:, k, :],
                                       start=k == 0, stop=k == 3)
                    L.inc(mm, self.q_tiles)

                def turn_query(h):
                    L.eng.wait_ge(self.q_copied.sem, 2 * h + 2)
                    L.inc(pe.matmul(ps[0:ROPE, 7, :], TURN, QRAW[0:ROPE, :], start=True, stop=True), self.q_turned)

                def output_tile(m, heads):
                    n = self.wo[m // 4]
                    if m % 4 == 0:
                        slot_ready(L, n)
                    wv = slot(n).rearrange("p (k n) -> p k n", k=HEADS)
                    for h in heads:
                        if h < HEADS - 1:
                            L.eng.wait_ge(self.outs_copied.sem, h + 1)
                        mm = pe.matmul(ps[:, (m + 7) % 8, :], wv[:, h, m % 4 * P:(m % 4 + 1) * P], OT[:, h, :],
                                       start=h == 0, stop=h == HEADS - 1)
                    if HEADS - 1 in heads:
                        L.inc(mm, self.y_tiles)

                queries(0)
                turn_query(0)
                L.eng.wait_ge(self.copied.sem, 23)
                for h in range(HEADS):
                    L.eng.wait_ge(self.q_ready.sem, h + 1)
                    if h:
                        L.eng.wait_ge(self.exps.sem, 4 * h)
                    for q in range(2):
                        rows = slice(q * P, (q + 1) * P)
                        pe.matmul(ps[:, q, :], QN[:, rows], KT[:, h, :], start=True, stop=False)
                        L.inc(pe.matmul(ps[:, q, :], QR[0:ROPE, rows], KPE[0:ROPE, :], start=False, stop=True), self.scores)
                    for q in range(2):
                        rows = slice(TL + q * P, TL + (q + 1) * P)
                        o = ps[:, 2, q * TL:(q + 1) * TL]
                        pe.matmul(o, QN[:, rows], KT[:, h, TL:TA], start=True, stop=False)
                        mm = pe.matmul(o, QR[0:ROPE, rows], KPE[0:ROPE, TL:TA], start=False, stop=True)
                    L.inc(mm, self.scores)
                    if h + 1 < HEADS:
                        queries(h + 1)
                    else:
                        output_tile(0, range(HEADS - 1))
                    L.eng.wait_ge(self.probs.sem, 4 * h + 4)
                    if h:
                        L.eng.wait_ge(self.turned_copied.sem, 3 * h)
                    for bank in range(2):
                        for kk in range(2):
                            for q in range(2):
                                k = 2 * bank + kk
                                mm = pe.transpose(ps[:, 3 + bank, kk * TL + q * P:kk * TL + (q + 1) * P],
                                                  PL[:, q, k * P:(k + 1) * P], IDENT)
                        L.inc(mm, self.turned)
                    for kk in range(2):
                        for q in range(2):
                            mm = pe.transpose(ps[:, 5, kk * TL + q * P:kk * TL + (q + 1) * P],
                                              PC[:, q, kk * P:(kk + 1) * P], IDENT)
                    L.inc(mm, self.turned)
                    if h + 1 < HEADS:
                        turn_query(h + 1)
                    L.eng.wait_ge(self.turned_copied.sem, 3 * h + 3)
                    if h:
                        L.eng.wait_ge(self.outs_copied.sem, h)
                    for k in range(4):
                        pe.matmul(ps[:, 6, 0:TL], V[:, k, h * DV:(h + 1) * DV], PTL[:, k, :], start=k == 0, stop=k == 3)
                    for k in range(2):
                        mm = pe.matmul(ps[:, 6, TL:TA], V[:, 2 + k, h * DV:(h + 1) * DV], PTC[:, k, :], start=k == 0, stop=k == 1)
                    L.inc(mm, self.outs)
                L.eng.wait_ge(self.outs_copied.sem, HEADS)
                for m in range(KD):
                    output_tile(m, range(HEADS) if m else range(HEADS - 1, HEADS))
                end(L, "pe")

            def act(self, L):
                begin(L, "act")
                act = L.eng
                for i in range(7):
                    L.eng.wait_ge(self.tiles.sem, i + 1)
                    o = (CKV[:, 0, :], CKV[:, 1, :], QRAW[0:ROPE, :])[i] if i < 3 else CQ[:, i - 3, :]
                    L.inc(act.copy(o, ps[0:ROPE if i == 2 else P, i % 4, :]), self.copied)
                    if i in (4, 6):
                        j = 0 if i == 4 else 1
                        L.eng.wait_ge(self.var.sem, j + 1)
                        L.inc(act.activation(RS[:, j, :], RS[:, j, :], ACT.Sqrt), self.std)
                for i in range(7, 23):
                    L.eng.wait_ge(self.tiles.sem, i + 1)
                    j = i - 7
                    o = KT[:, j, :] if j < 8 else V[:, (j - 8) // 2, (j - 8) % 2 * 512:((j - 8) % 2 + 1) * 512]
                    L.inc(act.copy(o, ps[:, i % 4, :]), self.copied)

                def copy_query(h):
                    L.eng.wait_ge(self.q_tiles.sem, 2 * h + 1)
                    if h == 0:
                        L.eng.wait_ge(self.latents.sem, 6)
                    L.inc(act.copy(QN, ps[:, 7, :]), self.q_copied)
                    L.eng.wait_ge(self.q_tiles.sem, 2 * h + 2)
                    L.inc(act.copy(QRAW[0:ROPE, :], ps[0:ROPE, 6, :]), self.q_copied)

                L.eng.wait_ge(self.latents.sem, 7)
                copy_query(0)
                for h in range(HEADS):
                    L.eng.wait_ge(self.neg.sem, h + 1)
                    for q in range(2):
                        L.inc(act.activation(PL[:, q, :], ps[:, q, :], ACT.Exp, bias=NEG[:, q:q + 1], scale=MLA_SCALE,
                                             accum_out=DEN[:, q:q + 1]), self.exps)
                    for q in range(2):
                        L.inc(act.activation(PC[:, q, :], ps[:, 2, q * TL:(q + 1) * TL], ACT.Exp, bias=NEG[:, 2 + q:3 + q],
                                             scale=MLA_SCALE, accum_out=DEN[:, 2 + q:3 + q]), self.exps)
                    if h + 1 < HEADS:
                        copy_query(h + 1)
                    L.eng.wait_ge(self.outs.sem, h + 1)
                    L.inc(act.copy(OT[:, h, :], ps[:, 6, :]), self.outs_copied)
                end(L, "act")

            def dve(self, L):
                begin(L, "dve")
                dve = L.eng
                dve.wait_ge(mla_in.sem, 16)
                for i, width in enumerate((KV_LORA, Q_LORA)):
                    for c in range(2, 6) if i else range(2):
                        L.eng.wait_ge(self.copied.sem, c + 1 if c < 2 else c + 2)
                        src = CKV[:, c, :] if c < 2 else CQ[:, c - 2, :]
                        L.inc(dve.tensor_tensor(SQ[c], src, src, ALU.mult), self.squares)
                    L.eng.wait_ge(self.sums.sem, i + 1)
                    L.inc(dve.tensor_scalar(RS[:, i, :], ps[:, 5 + i, :], 1.0 / width, NORM_EPS, ALU.mult, ALU.add), self.var)
                    L.eng.wait_ge(self.std.sem, i + 1)
                    L.inc(dve.reciprocal(RS[:, i, :], RS[:, i, :]))
                    L.join()
                    for c in range(2 + 2 * i):
                        o = CQ[:, c, :] if i else CKV[:, c, :]
                        L.inc(dve.scalar_tensor_tensor(out=o, in0=o, scalar=vcol("g_q" if i else "g_kv", 4 if i else 2)[:, c:c + 1],
                                                       in1=RS[:, i, :], op0=ALU.mult, op1=ALU.mult), self.latents)

                def rotate(out_ap, bank, signal):
                    L.inc(dve.tensor_tensor(T1[0:ROPE, :], QRAW[0:ROPE, :], COS, ALU.mult))
                    L.inc(dve.tensor_tensor(out_ap[0:ROPE, :], ps[0:ROPE, bank, :], SIN, ALU.mult))
                    L.join()
                    L.inc(dve.tensor_tensor(out_ap[0:ROPE, :], out_ap[0:ROPE, :], T1[0:ROPE, :], ALU.add), signal)

                L.eng.wait_ge(self.kpe_turned.sem, 1)
                rotate(KPE, 4, self.latents)

                L.eng.wait_ge(self.q_turned.sem, 1)
                rotate(QR, 7, self.q_ready)
                for h in range(HEADS):
                    for q in range(2):
                        L.eng.wait_ge(self.scores.sem, 3 * h + q + 1)
                        L.inc(dve.tensor_reduce(MAXS[:, q:q + 1], ps[:, q, :], X, ALU.max))
                    L.eng.wait_ge(self.scores.sem, 3 * h + 3)
                    L.inc(dve.tensor_reduce(MAXS[:, 2:4], ps[:, 2, :].rearrange("p (q t) -> p q t", q=2), X, ALU.max))
                    L.join()
                    L.inc(dve.tensor_scalar(NEG, MAXS, -MLA_SCALE, None, ALU.mult), self.neg)
                    L.eng.wait_ge(self.exps.sem, 4 * h + 4)
                    L.inc(dve.reciprocal(RDEN, DEN))
                    L.join()
                    for q in range(4):
                        p = PL[:, q, :] if q < 2 else PC[:, q - 2, :]
                        L.inc(dve.tensor_scalar(p, p, RDEN[:, q:q + 1], None, ALU.mult), self.probs)
                    for bank in range(3):
                        L.eng.wait_ge(self.turned.sem, 3 * h + bank + 1)
                        o = PTL[:, 2 * bank:2 * bank + 2, :] if bank < 2 else PTC
                        L.inc(dve.tensor_copy(o.rearrange("p k t -> p (k t)"), ps[:, 3 + bank, :]), self.turned_copied)
                    if h + 1 < HEADS:
                        L.eng.wait_ge(self.q_turned.sem, h + 2)
                        rotate(QR, 7, self.q_ready)
                for m in range(KD):
                    gated_tile(L, 0, 0, TA, self.y_tiles, m + 1, (m + 7) % 8, m)
                end(L, "dve")

        def gated_tile(L, l, which, tokens, ready, value, bank, m):
            L.wait(ready, value)
            for c in range(tokens // TL):
                xs = XT[:, m, c * TL:(c + 1) * TL]
                L.inc(L.eng.scalar_tensor_tensor(out=xs, in0=ps[:, bank, c * TL:(c + 1) * TL],
                                                 scalar=MOD[l][:, 3 * KD * which + 2 * KD + m, c:c + 1], in1=xs,
                                                 op0=ALU.mult, op1=ALU.add))

        class Moe:

            def __init__(self, l, tokens, norm):
                self.l, self.T, self.NT, self.norm = l, tokens, tokens // P, norm
                self.NB = blocks_of(tokens)
                NT = self.NT
                self.logits_made = shared("moe_logits_made", 1)
                self.logits_copied = shared("moe_logits_copied", 1)
                self.logits = shared("moe_logits", 1)
                self.logits_kept = shared("moe_logits_kept", 1)
                self.rows_turned = shared("moe_rows_turned", NT)
                self.rows_kept = shared("moe_rows_kept", NT)
                self.less_max = shared("moe_less_max", 2)
                self.exps = shared("moe_exps", 2)
                self.chosen = shared("moe_chosen", 1)
                self.ranks = shared("moe_ranks", 1)
                self.counts = shared("moe_counts", 1)
                self.counts_kept = shared("moe_counts_kept", 1)
                self.firsts = shared("moe_firsts", 1)
                self.places = shared("moe_places", 2 * NT)
                self.table = shared("moe_table", 1)
                self.table_kept = shared("moe_table_kept", 1)
                self.sum_turned = shared("moe_sum_turned", NT)
                self.sum_made = shared("moe_sum_made", NT)
                self.sum_added = shared("moe_sum_added", NT)
                self.scattered_all = shared("moe_scattered_all", 1)
                self.rows_out = [shared(f"moe_rows_out{i}", 16 * NT // 2) for i in range(2)]
                self.pairs_in = [shared(f"moe_pairs_in{i}", 16 * NT // 2) for i in range(2)]
                self.block_turned = sig(f"moe{l}_block_turned")
                self.x_high = sig(f"moe{l}_x_high")
                self.x_split = sig(f"moe{l}_x_split")
                self.w_high = sig(f"moe{l}_w_high")
                self.w_split = sig(f"moe{l}_w_split")
                self.w_used = sig(f"moe{l}_w_used")
                self.gated = sig(f"moe{l}_gated")
                self.multiplied = sig(f"moe{l}_multiplied")
                self.hidden_turned = sig(f"moe{l}_hidden_turned")
                self.h_high = sig(f"moe{l}_h_high")
                self.h_split = sig(f"moe{l}_h_split")
                self.y_kept = sig(f"moe{l}_y_kept")
                self.stored = sig(f"moe{l}_stored")
                self.index_g = sig(f"moe{l}_index_g")
                self.index_s = sig(f"moe{l}_index_s")
                self.gathered = sig(f"moe{l}_gathered")
                self.scattered = sig(f"moe{l}_scattered")
                self.first = len(loads)
                for e in range(EXPERTS):
                    done = (self.w_split, 0) if e < EXPERTS - 1 else (self.pairs_in[1], 16 * (NT // 2))
                    plan(columns(w["moe_w_gate"][l][e], 0, FF), (KD, FF), done)
                    plan(columns(w["moe_w_up"][l][e], 0, FF), (KD, FF), done)
                    plan(columns(w["moe_w_down"][l][e], 0, D), (FT, D), done)
                NT, NB = self.NT, self.NB
                take = carver()

                def tiles(n):
                    return take(NT * n).rearrange("p (t n) -> p t n", t=NT)
                self.ROWS = [take(D) for _ in range(2)]
                self.PAIRS = [take(2 * D).rearrange("p (c d) -> p c d", c=2) for _ in range(2)]
                self.SUM = take(D)
                self.LOG = tiles(36)
                self.M1, self.M2 = tiles(1), tiles(1)
                self.GP, self.GB, self.CG, self.OG = (tiles(GROUPS) for _ in range(4))
                self.GW, self.GS = tiles(1), tiles(1)
                self.TMP = tiles(EXPERTS)
                self.EL, self.EB, self.ES, self.CE = (tiles(PER_GROUP) for _ in range(4))
                self.OE = [tiles(PER_GROUP) for _ in range(2)]
                self.WT = [tiles(1) for _ in range(2)]
                self.WS = tiles(1)
                self.O32 = [tiles(EXPERTS) for _ in range(2)]
                self.BOTH = tiles(EXPERTS)
                self.RANK = [tiles(1) for _ in range(2)]
                self.QUOT = [tiles(1) for _ in range(2)]
                self.BLK = [tiles(1) for _ in range(2)]
                self.CNT, self.NBLK = take(P), take(P)
                self.FIRST = take(EXPERTS + 1)
                self.FIRSTI = take(EXPERTS + 1).bitcast(I32)
                self.UNITS_BEFORE = take(EXPERTS + 1)
                self.UNITS_BEFOREI = take(EXPERTS + 1).bitcast(I32)
                self.AT_PLACE = [[take(CAP) for _ in range(2)] for _ in range(NT)]
                self.AT_BLOCK = [[take(2 * NB).rearrange("p (c b) -> p c b", c=2) for _ in range(2)] for _ in range(NT)]
                self.TAB, self.EMPTY = (take(2 * NB).rearrange("p (c b) -> p c b", c=2) for _ in range(2))
                self.TABI = take(2 * NB).bitcast(I32).rearrange("p (c b) -> p c b", c=2)
                self.IDXG, self.IDXS = take(1).bitcast(I32), take(1).bitcast(I32)
                self.XG = take(D)
                self.SUMS = [self.SUM, self.XG]
                self.SG, self.H = take(FF), take(FF)
                self.YS = take(D)
                self.WH = place(f"MOE_WH{l}", [P, UNITS, UNIT], F32R, A_at)
                self.WL = place(f"MOE_WL{l}", [P, UNITS, UNIT], F32R, arena_at + 4 * 2 * D)
                self.XS = place(f"MOE_XS{l}", [P, 2, KD, CAP], F32R, arena_at)
                self.HS = place(f"MOE_HS{l}", [P, 2, FT, CAP], F32R, arena_at + 4 * 6 * D)

            def unit(self, a, u):
                n = self.first + 3 * a + u // UNITS
                return slot(n)[:, u % UNITS * UNIT:(u % UNITS + 1) * UNIT]

            def sum_by_features(self, t, k):
                return ps[:, (5 if t % 2 == 0 else 3) + k // 4, k % 4 * P:(k % 4 + 1) * P]

            def pe(self, L):
                pe, NT, NB = L.eng, self.NT, self.NB
                router = vcol("router", KD * 36, self.l * KD * 36).rearrange("p (k n) -> p k n", k=KD)
                for k in range(KD):
                    L.wait(self.norm.done, (k + 1) * self.T // TL)
                    mm = pe.matmul(ps[0:36, 7, 0:self.T], router[:, k, :], A[:, k, 0:self.T], start=k == 0, stop=k == KD - 1)
                L.inc(mm, self.logits_made)
                L.wait(self.logits_copied, 1)
                for t in range(NT):
                    mm = pe.transpose(ps[:, 0, 36 * t:36 * t + 36], self.SUM[0:36, t * P:(t + 1) * P], IDENT[0:36, 0:36])
                L.inc(mm, self.logits)
                for t in range(NT):
                    if t >= 2:
                        L.wait(self.rows_kept, t - 1)
                    for k in range(KD):
                        mm = pe.transpose(ps[:, 1 + 2 * (t % 2) + k // 4, k % 4 * P:(k % 4 + 1) * P],
                                          A[:, k, t * P:(t + 1) * P], IDENT)
                    L.inc(mm, self.rows_turned)
                L.wait(self.chosen, 1)
                for t in range(NT):
                    for u in range(t + 1):
                        mm = pe.matmul(ps[:, 5, 32 * t:32 * t + 32], BEFORE if u == t else ONES, self.BOTH[:, u, :],
                                       start=u == 0, stop=u == t)
                L.inc(mm, self.ranks)
                for t in range(NT):
                    mm = pe.matmul(ps[0:EXPERTS, 6, 0:P], self.BOTH[:, t, :], ONES, start=t == 0, stop=t == NT - 1)
                L.inc(mm, self.counts)
                L.wait(self.counts_kept, 1)
                L.inc(pe.matmul(ps[:, 0, 0:EXPERTS + 1], self.NBLK[0:EXPERTS, :], BEFORE[0:EXPERTS, 0:EXPERTS + 1],
                                start=True, stop=True), self.firsts)
                for t in range(NT):
                    for c in range(2):
                        L.wait(self.places, 2 * t + c + 1)
                        mm = pe.matmul(ps[0:CAP, 6, 0:2 * NB], self.AT_PLACE[t][c],
                                       self.AT_BLOCK[t][c].rearrange("p c b -> p (c b)"),
                                       start=t + c == 0, stop=2 * t + c == 2 * NT - 1)
                L.inc(mm, self.table)

                def turn_block(half):
                    for k in range(4 * half, 4 * half + 4):
                        mm = pe.transpose(ps[:, 3 + k // 4, k % 4 * CAP:(k % 4 + 1) * CAP], self.XG[0:CAP, k * P:(k + 1) * P],
                                          IDENT[0:CAP, 0:CAP])
                    if half:
                        mm.then_inc(self.block_turned.sem, 1)

                L.wait(self.rows_kept, NT)
                pe.wait_ge(self.gathered.sem, 16)
                turn_block(0)
                turn_block(1)

                def products(b, u, outs, moving, tiles, first, last):
                    pe.wait_ge(self.w_split.sem, b * BLOCK_UNITS + (u + 1))
                    j = u % UNITS
                    for i, k in enumerate(tiles):
                        for c, out_ap in enumerate(outs):
                            at = slice((i + c) * 512, (i + c + 1) * 512)
                            for x, weights in ((0, self.WH), (1, self.WH), (0, self.WL)):
                                mm = pe.matmul(out_ap, moving[:, x, k, :], weights[:, j, at],
                                               start=first and i == 0 and x == 0 and weights is self.WH,
                                               stop=last and i == len(tiles) - 1 and weights is self.WL)
                    mm.then_inc(self.w_used.sem, 1)

                with pe.Fori(0, EXPERTS // 2) as pair:
                    for a in range(2):
                        lo, hi = self.range_of(pe, pair, a)
                        with pe.Fori(lo, hi) as b:
                            pe.wait_ge(self.x_split.sem, b * 2 + 2)
                            for u in range(2 * UNITS):
                                q = u % UNITS
                                products(b, u, [ps[0:CAP, u // UNITS, :]], self.XS, (2 * q, 2 * q + 1), q == 0, q == UNITS - 1)
                            pe.wait_ge(self.gathered.sem, b * 16 + 32)
                            pe.sem_inc(spare.sem, 1)
                            turn_block(0)
                            pe.wait_ge(self.multiplied.sem, b + 1)
                            pe.sem_inc(spare.sem, 1)
                            for k in range(FT):
                                mm = pe.transpose(ps[:, 2 if k < 2 else 7, k % 2 * CAP:(k % 2 + 1) * CAP],
                                                  self.H[0:CAP, k * P:(k + 1) * P], IDENT[0:CAP, 0:CAP])
                                if k % 2:
                                    mm.then_inc(self.hidden_turned.sem, 1)
                            turn_block(1)
                            pe.wait_ge(self.y_kept.sem, b * 2 + 2)
                            for k in range(FT):
                                if k % 2 == 0:
                                    pe.wait_ge(self.h_split.sem, b * 2 + (k // 2 + 1))
                                products(b, 2 * UNITS + k, [ps[0:CAP, 5, :], ps[0:CAP, 6, :]], self.HS, (k,), k == 0, k == FT - 1)
                for t in range(NT):
                    L.wait(self.sum_made, t + 1)
                    if t >= 2:
                        L.wait(self.sum_added, t - 1)
                    for k in range(KD):
                        mm = pe.transpose(self.sum_by_features(t, k), self.SUMS[t % 2][:, k * P:(k + 1) * P], IDENT)
                    L.inc(mm, self.sum_turned)
                end(L, "pe")

            def range_of(self, eng, pair, a):
                return tuple(eng.value_load(self.FIRSTI[0:1, bass.ds(pair * 2 + (a + i), 1)], min_val=i, max_val=self.NB - 2)
                             for i in range(2))

            def count_of(self, eng):
                return eng.value_load(self.FIRSTI[0:1, EXPERTS:EXPERTS + 1], min_val=EXPERTS, max_val=self.NB - 2)

            def keep_rows(self, eng, half, copy, blocks):
                eng.wait_ge(self.w_used.sem, blocks * BLOCK_UNITS + UNITS)
                eng.wait_ge(self.stored.sem, blocks + 1)
                eng.sem_inc(spare.sem, 1)
                copy(self.YS[0:CAP, 512 * half:512 * (half + 1)], ps[0:CAP, 5 + half, :]).then_inc(self.y_kept.sem, 1)

            def act(self, L):
                act, NT = L.eng, self.NT
                begin(L, "act")
                def store_rows(t):
                    L.wait(self.rows_turned, t + 1)
                    if t >= 2:
                        L.wait(self.rows_out[t % 2], 16)
                    L.inc(act.copy(self.ROWS[t % 2], ps[:, 1 + 2 * (t % 2):3 + 2 * (t % 2), :].rearrange("p b n -> p (b n)")),
                          self.rows_kept)
                    L.join()
                    act.dma_start(f_rows[t * P:(t + 1) * P, :], self.ROWS[t % 2]).then_inc(self.rows_out[t % 2].sem, 16)

                L.wait(self.less_max, 1)
                L.inc(act.activation(self.GP, self.GP, ACT.Exp), self.exps)
                for t in range(2):
                    store_rows(t)
                L.wait(self.less_max, 2)
                L.inc(act.activation(self.ES, self.ES, ACT.Exp), self.exps)
                for t in range(2, NT):
                    store_rows(t)
                L.wait(self.table_kept, 1)

                keep_rows = self.keep_rows

                def round_tokens():
                    for c in range(2):
                        act.copy(self.XS[:, 0, 4 * c:4 * c + 4, :].rearrange("p k t -> p (k t)"), ps[:, 3 + c, 0:4 * CAP])\
                           .then_inc(self.x_high.sem, 1)

                act.wait_ge(self.block_turned.sem, 1)
                round_tokens()
                with act.Fori(0, EXPERTS // 2) as pair:
                    for a in range(2):
                        lo, hi = self.range_of(act, pair, a)
                        with act.Fori(lo, hi) as b:
                            def round_weights(u):
                                if u % UNITS == 0:
                                    n = self.first + 3 * a + u // UNITS
                                    act.wait_ge(slot_in[place_of[n]].sem, pair * 16 + arrivals[n])
                                act.wait_ge(self.w_used.sem, b * BLOCK_UNITS + (u + 1))
                                act.copy(self.WH[:, u % UNITS, :], self.unit(a, u)).then_inc(self.w_high.sem, 1)

                            for u in range(UNITS):
                                round_weights(u)
                            keep_rows(act, 0, act.copy, b)
                            for u in range(UNITS, 2 * UNITS):
                                round_weights(u)
                            act.wait_ge(self.w_used.sem, b * BLOCK_UNITS + 2 * UNITS)
                            act.activation(self.SG[0:CAP], ps[0:CAP, 0, :], ACT.Silu).then_inc(self.gated.sem, 1)
                            for u in range(2 * UNITS, 3 * UNITS - 1):
                                round_weights(u)
                            for c, bank in enumerate((2, 7)):
                                act.wait_ge(self.hidden_turned.sem, b * 2 + (c + 1))
                                act.copy(self.HS[:, 0, 2 * c:2 * c + 2, :].rearrange("p k t -> p (k t)"), ps[:, bank, 0:2 * CAP])\
                                   .then_inc(self.h_high.sem, 1)
                            round_weights(3 * UNITS - 1)
                            act.wait_ge(self.block_turned.sem, b + 2)
                            round_tokens()
                keep_rows(act, 0, act.copy, self.count_of(act))
                L.last = None
                L.wait(self.scattered_all, 1)
                for t in range(NT):
                    if t >= 2:
                        L.wait(self.sum_made, t - 1)
                    act.dma_start(self.PAIRS[t % 2], y_rows[2 * P * t:2 * P * (t + 1), :].rearrange("(p c) d -> p c d", c=2))\
                       .then_inc(self.pairs_in[t % 2].sem, 16)
                end(L, "act")

            def dve(self, L):
                v, NT, NB = L.eng, self.NT, self.NB
                begin(L, "dve")

                def lanes(ap, n):
                    return ap.to_broadcast([P, NT, n])

                def row(ap, n):
                    return ap.unsqueeze(1).to_broadcast([P, NT, n])

                def step(ins, signal=None):
                    L.inc(ins, signal)
                    L.join()

                def first_of_largest(values, n, cand, one_hot):
                    step(v.tensor_reduce(self.M1[:, :, 0], values, X, ALU.max))
                    step(v.tensor_tensor(cand, values, lanes(self.M1, n), ALU.is_ge))
                    step(v.scalar_tensor_tensor(out=cand, in0=cand, scalar=-64.0, in1=row(IOTA[:, 0:n], n),
                                                op0=ALU.mult, op1=ALU.add))
                    step(v.tensor_reduce(self.M1[:, :, 0], cand, X, ALU.min))
                    step(v.tensor_tensor(one_hot, cand, lanes(self.M1, n), ALU.is_equal))

                def softmax(values, out_ap, n, turn):
                    step(v.tensor_reduce(self.M1[:, :, 0], values, X, ALU.max))
                    step(v.tensor_tensor(out_ap, values, lanes(self.M1, n), ALU.subtract), self.less_max)
                    L.wait(self.exps, turn)
                    step(v.tensor_reduce(self.M1[:, :, 0], out_ap, X, ALU.add))
                    step(v.reciprocal(self.M2[:, :, 0], self.M1[:, :, 0]))
                    step(v.tensor_tensor(out_ap, out_ap, lanes(self.M2, n), ALU.mult))

                def pick(out_ap, values, weights, n):
                    t = self.TMP[:, :, 0:n]
                    step(v.tensor_tensor(t, values, weights, ALU.mult))
                    step(v.tensor_reduce(out_ap[:, :, 0], t, X, ALU.add))

                bias = vcol("router_bias", 36, 36 * self.l)
                L.wait(self.logits_made, 1)
                L.inc(v.tensor_copy(self.SUM[0:36, 0:self.T], ps[0:36, 7, 0:self.T]), self.logits_copied)
                L.wait(self.logits, 1)
                step(v.tensor_copy(self.LOG.rearrange("p t n -> p (t n)"), ps[:, 0, 0:36 * NT]), self.logits_kept)
                softmax(self.LOG[:, :, 0:GROUPS], self.GP, GROUPS, 1)
                step(v.tensor_tensor(self.GB, self.GP, row(bias[:, 0:GROUPS], GROUPS), ALU.add))
                first_of_largest(self.GB, GROUPS, self.CG, self.OG)
                pick(self.GW, self.GP, self.OG, GROUPS)
                by_group = self.TMP.rearrange("p t (g j) -> p t g j", g=GROUPS)
                by_expert = self.TMP.rearrange("p t (g j) -> p t j g", g=GROUPS)
                group4 = self.OG.unsqueeze(3).to_broadcast([P, NT, GROUPS, PER_GROUP])
                for o, values in ((self.EL, self.LOG[:, :, GROUPS:36].rearrange("p t (g j) -> p t g j", g=GROUPS)),
                                  (self.EB, bias[:, GROUPS:36].rearrange("p (g j) -> p g j", g=GROUPS).unsqueeze(1)
                                   .to_broadcast([P, NT, GROUPS, PER_GROUP]))):
                    step(v.tensor_tensor(by_group, values, group4, ALU.mult))
                    step(v.tensor_reduce(o, by_expert, X, ALU.add))
                softmax(self.EL, self.ES, PER_GROUP, 2)
                step(v.tensor_tensor(self.EB, self.ES, self.EB, ALU.add))
                for c in range(2):
                    first_of_largest(self.EB, PER_GROUP, self.CE, self.OE[c])
                    pick(self.WT[c], self.ES, self.OE[c], PER_GROUP)
                    step(v.scalar_tensor_tensor(out=self.EB, in0=self.OE[c], scalar=MASKED, in1=self.EB, op0=ALU.mult, op1=ALU.add))
                    step(v.tensor_tensor(self.O32[c].rearrange("p t (g j) -> p t g j", g=GROUPS),
                                         self.OE[c].unsqueeze(2).to_broadcast([P, NT, GROUPS, PER_GROUP]), group4, ALU.mult))
                step(v.tensor_tensor(self.BOTH, self.O32[0], self.O32[1], ALU.add), self.chosen)
                step(v.tensor_tensor(self.WS, self.WT[0], self.WT[1], ALU.add))
                step(v.reciprocal(self.WS, self.WS))
                step(v.tensor_tensor(self.WS, self.WS, self.GW, ALU.mult))
                for c in range(2):
                    step(v.tensor_tensor(self.WT[c], self.WT[c], self.WS, ALU.mult))
                L.wait(self.counts, 1)
                step(v.tensor_copy(self.CNT[0:EXPERTS, :], ps[0:EXPERTS, 6, 0:P]))
                step(v.tensor_scalar(self.NBLK[0:EXPERTS, :], self.CNT[0:EXPERTS, :], float(CAP), 1.0, ALU.is_gt, ALU.add))
                for r in range(2, -(-self.T // CAP)):
                    step(v.scalar_tensor_tensor(out=self.NBLK[0:EXPERTS, :], in0=self.CNT[0:EXPERTS, :], scalar=float(r * CAP),
                                                in1=self.NBLK[0:EXPERTS, :], op0=ALU.is_gt, op1=ALU.add))
                v.sem_inc(self.counts_kept.sem, 1)
                L.wait(self.firsts, 1)
                step(v.tensor_copy(self.FIRST, ps[:, 0, 0:EXPERTS + 1]))
                step(v.tensor_copy(self.FIRSTI, self.FIRST))
                step(v.tensor_scalar(self.UNITS_BEFORE, self.FIRST, float(BLOCK_UNITS), -float(BLOCK_UNITS), ALU.mult, ALU.add))
                step(v.tensor_copy(self.UNITS_BEFOREI, self.UNITS_BEFORE))
                for c in range(2):
                    step(v.tensor_tensor(self.TMP, ps[:, 5, 0:32 * NT].rearrange("p (t e) -> p t e", t=NT), self.O32[c], ALU.mult))
                    step(v.tensor_reduce(self.RANK[c][:, :, 0], self.TMP, X, ALU.add))
                    pick(self.BLK[c], row(self.FIRST[:, 0:EXPERTS], EXPERTS), self.O32[c], EXPERTS)
                    step(v.tensor_scalar(self.QUOT[c], self.RANK[c], float(CAP), None, ALU.is_ge))
                    for r in range(2, -(-self.T // CAP)):
                        step(v.scalar_tensor_tensor(out=self.QUOT[c], in0=self.RANK[c], scalar=float(r * CAP), in1=self.QUOT[c],
                                                    op0=ALU.is_ge, op1=ALU.add))
                    step(v.tensor_tensor(self.BLK[c], self.BLK[c], self.QUOT[c], ALU.add))
                    step(v.scalar_tensor_tensor(out=self.RANK[c], in0=self.QUOT[c], scalar=-float(CAP), in1=self.RANK[c],
                                                op0=ALU.mult, op1=ALU.add))
                for t in range(NT):
                    for c in range(2):
                        L.inc(v.tensor_scalar(self.AT_PLACE[t][c], IOTA[:, 0:CAP], self.RANK[c][:, t, :], None, ALU.is_equal))
                        L.inc(v.tensor_scalar(self.AT_BLOCK[t][c][:, 0, :], IOTA[:, 0:NB], self.BLK[c][:, t, :],
                                              PLACE[:, c, t:t + 1], ALU.is_equal, ALU.mult))
                        L.inc(v.tensor_scalar(self.AT_BLOCK[t][c][:, 1, :], IOTA[:, 0:NB], self.BLK[c][:, t, :],
                                              PLACE[:, 2, t:t + 1], ALU.is_equal, ALU.mult), self.places)
                L.wait(self.table, 1)
                tab = ps[0:CAP, 6, 0:2 * NB].rearrange("p (c b) -> p c b", c=2)
                step(v.tensor_scalar(self.EMPTY[0:CAP], tab, 0.5, OUT_OF_BOUNDS, ALU.is_lt, ALU.mult))
                step(v.scalar_tensor_tensor(out=self.TAB[0:CAP], in0=tab, scalar=-1.0, in1=self.EMPTY[0:CAP], op0=ALU.add, op1=ALU.add))
                step(v.tensor_copy(self.TABI[0:CAP], self.TAB[0:CAP]), self.table_kept)

                keep_rows = self.keep_rows

                def split_tokens(blocks):
                    for c in range(2):
                        v.wait_ge(self.x_high.sem, blocks * 2 + (c + 1))
                        v.tensor_tensor(self.XS[:, 1, 4 * c:4 * c + 4, :].rearrange("p k t -> p (k t)"), ps[:, 3 + c, 0:4 * CAP],
                                        high(self.XS[:, 0, 4 * c:4 * c + 4, :]).rearrange("p k t -> p (k t)"), ALU.subtract)\
                         .then_inc(self.x_split.sem, 1)

                split_tokens(0)
                with v.Fori(0, EXPERTS // 2) as pair:
                    for a in range(2):
                        lo, hi = self.range_of(v, pair, a)
                        with v.Fori(lo, hi) as b:
                            def split_weights(u):
                                v.wait_ge(self.w_high.sem, b * BLOCK_UNITS + (u + 1))
                                v.tensor_tensor(self.WL[:, u % UNITS, :], self.unit(a, u), high(self.WH[:, u % UNITS, :]),
                                                ALU.subtract).then_inc(self.w_split.sem, 1)

                            for u in range(UNITS):
                                split_weights(u)
                            keep_rows(v, 1, v.tensor_copy, b)
                            for u in range(UNITS, 3 * UNITS - 2):
                                split_weights(u)
                            v.wait_ge(self.gated.sem, b + 1)
                            v.wait_ge(self.w_used.sem, b * BLOCK_UNITS + 3 * UNITS)
                            v.tensor_tensor(self.H[0:CAP], self.SG[0:CAP], ps[0:CAP, 1, :], ALU.mult)\
                             .then_inc(self.multiplied.sem, 1)
                            split_weights(3 * UNITS - 2)
                            for c, bank in enumerate((2, 7)):
                                v.wait_ge(self.h_high.sem, b * 2 + (c + 1))
                                v.tensor_tensor(self.HS[:, 1, 2 * c:2 * c + 2, :].rearrange("p k t -> p (k t)"), ps[:, bank, 0:2 * CAP],
                                                high(self.HS[:, 0, 2 * c:2 * c + 2, :]).rearrange("p k t -> p (k t)"), ALU.subtract)\
                                 .then_inc(self.h_split.sem, 1)
                            split_weights(3 * UNITS - 1)
                            split_tokens(b + 1)
                keep_rows(v, 1, v.tensor_copy, self.count_of(v))
                def make_sum(t):
                    L.wait(self.pairs_in[t % 2], 16 * (t // 2 + 1))
                    if t >= 2:
                        L.wait(self.sum_turned, t - 1)
                    o = self.SUMS[t % 2]
                    step(v.tensor_scalar(o, self.PAIRS[t % 2][:, 0, :], self.WT[0][:, t, :], None, ALU.mult))
                    L.inc(v.scalar_tensor_tensor(out=o, in0=self.PAIRS[t % 2][:, 1, :], scalar=self.WT[1][:, t, :],
                                                 in1=o, op0=ALU.mult, op1=ALU.add), self.sum_made)

                make_sum(0)
                for t in range(NT):
                    if t + 1 < NT:
                        make_sum(t + 1)
                    L.wait(self.sum_turned, t + 1)
                    for k in range(KD):
                        xs = XT[:, k, t * P:(t + 1) * P]
                        ins = v.scalar_tensor_tensor(out=xs, in0=self.sum_by_features(t, k),
                                                     scalar=MOD[self.l][:, 5 * KD + k, t * P // TL:t * P // TL + 1], in1=xs,
                                                     op0=ALU.mult, op1=ALU.add)
                        L.inc(ins, self.sum_added if k == KD - 1 else None)
                end(L, "dve")

            def pool(self, L):
                g, NT = L.eng, self.NT
                g.sem_inc(self.stored.sem, 2)
                g.sem_inc(self.w_used.sem, UNITS)
                L.wait(self.logits_kept, 1)
                g.memset(self.XG[0:CAP], 0.0).then_inc(self.index_g.sem, 1)
                L.wait(self.table_kept, 1)
                for i in range(2):
                    L.wait(self.rows_out[i], 16 * (NT // 2))
                blocks = self.count_of(g)

                def gather(block, indices):
                    g.tensor_copy(self.IDXG[0:CAP], self.TABI[0:CAP, 1, block]).then_inc(self.index_g.sem, 1)
                    g.wait_ge(self.index_g.sem, indices + 1)
                    g.sem_inc(spare.sem, 1)
                    g.indirect_dma_start(out=self.XG[0:CAP], out_offset=None, in_=f_rows[:, :],
                                         in_offset=bass.IndirectOffsetOnAxis(ap=self.IDXG[0:CAP], axis=0),
                                         bounds_check=self.T - 1, oob_is_err=False).then_inc(self.gathered.sem, 16)

                gather(slice(0, 1), 1)
                g.wait_ge(self.gathered.sem, 16)
                g.wait_ge(self.block_turned.sem, 1)
                gather(slice(1, 2), 2)
                with g.Fori(0, blocks) as b:
                    g.wait_ge(self.gathered.sem, b * 16 + 32)
                    g.wait_ge(self.block_turned.sem, b + 2)
                    g.sem_inc(spare.sem, 1)
                    gather(bass.ds(b + 2, 1), b + 3)
                    g.tensor_copy(self.IDXS[0:CAP], self.TABI[0:CAP, 0, bass.ds(b, 1)]).then_inc(self.index_s.sem, 1)
                    g.wait_ge(self.index_s.sem, b + 1)
                    g.wait_ge(self.y_kept.sem, b * 2 + 4)
                    g.sem_inc(spare.sem, 1)
                    g.indirect_dma_start(out=y_rows[:, :], out_offset=bass.IndirectOffsetOnAxis(ap=self.IDXS[0:CAP], axis=0),
                                         in_=self.YS[0:CAP], in_offset=None, bounds_check=2 * self.T - 1,
                                         oob_is_err=False).then_inc(self.scattered.sem, 16)
                    g.wait_ge(self.scattered.sem, b * 16 + 16)
                    g.sem_inc(self.stored.sem, 1)
                g.wait_ge(self.gathered.sem, blocks * 16 + 32)
                g.sem_inc(self.scattered_all.sem, 1)

        take = carver()
        CG = take(4 * TL).rearrange("p (m t) -> p m t", m=4)
        CU = take(4 * (TL + 2)).rearrange("p (m t) -> p m t", m=4)
        CZ = take(4 * TL).rearrange("p (m t) -> p m t", m=4)
        BZ = take(KD * TL).rearrange("p (m t) -> p m t", m=KD)
        conv_at = arena_at + 4 * (4 * TL + 4 * (TL + 2) + 4 * TL + KD * TL)
        CONV_WS = place("CONV_WS", [P, 2, UNITS, UNIT], F32R, conv_at)
        CONV_XS = place("CONV_XS", [P, 2, KD, TL], F32R, conv_at + 4 * 2 * UNITS * UNIT)
        assert conv_at + 4 * (2 * UNITS * UNIT + 2 * KD * TL) <= arena_at + 4 * ARENA_W
        CONV_BS = place("CONV_BS", [P, 2, KD, TL], F32R, A_at)

        class Conv:

            def __init__(self):
                self.tiles = sig("conv_tiles")
                self.kept = sig("conv_kept")
                self.gate_in = sig("conv_gate_in")
                self.w_high = shared("split_high", 4 * KD)
                self.w_split = shared("split_ready", 4 * KD)
                self.x_high = sig("conv_x_high")
                self.x_split = sig("conv_x_split")
                win = w["conv_w_in"][0]
                pieces = [columns(win, part * D + half * 512, part * D + half * 512 + 512)
                          for half in range(2) for part in (1, 2, 0)]
                pieces += [columns(w["conv_w_out"][0], 512 * i, 512 * (i + 1)) for i in range(2)]
                self.slots = [plan(piece, (KD, 512), (self.w_split, 4 * i + 4)) for i, piece in enumerate(pieces)]
                self.y_first = 3 * KD

            def unit(self, i):
                return slot(self.slots[i // 4]).rearrange("p (k n) -> p k n", k=KD)[:, :, i % 4 * P:(i % 4 + 1) * P]

            def parts(self, i):
                return [CONV_WS[:, j, i % UNITS, :].rearrange("p (k n) -> p k n", k=KD) for j in range(2)]

            def round_stream(self, L, k):
                L.wait(norms[2].done, k + 1)
                L.inc(L.eng.copy(CONV_XS[:, 0, k, :], A[:, k, 0:TL]), self.x_high)

            def split_stream(self, L, k):
                L.eng.wait_ge(self.x_high.sem, k + 1)
                L.inc(L.eng.tensor_tensor(CONV_XS[:, 1, k, :], A[:, k, 0:TL], high(CONV_XS[:, 0, k, :]), ALU.subtract), self.x_split)

            def round_weights(self, L, i):
                if i % 4 == 0:
                    slot_ready(L, self.slots[i // 4])
                if i >= UNITS:
                    L.eng.wait_ge(self.tiles.sem, i - UNITS + 1)
                L.inc(L.eng.copy(self.parts(i)[0], self.unit(i)), self.w_high)

            def split_weights(self, L, i):
                L.wait(self.w_high, i + 1)
                high_part, low_part = self.parts(i)
                L.inc(L.eng.tensor_tensor(low_part, self.unit(i), high(high_part), ALU.subtract), self.w_split)

            def pe(self, L):
                pe = L.eng
                for i in range(4 * KD):
                    L.wait(self.w_split, i + 1)
                    if 8 <= i < self.y_first + 8:
                        part, t = (i - 8) // 4, (i - 8) % 4
                        if part % 3 == 0:
                            L.eng.wait_ge(self.gate_in.sem, 4 * (part // 3) + t + 1)
                        else:
                            L.eng.wait_ge(self.kept.sem, 4 * (2 * (part // 3) + part % 3 - 1) + t + 1)
                    moving = CONV_XS if i < self.y_first else CONV_BS
                    high_part, low_part = self.parts(i)
                    for k in range(KD):
                        if i == 0:
                            L.eng.wait_ge(self.x_split.sem, k + 1)
                        if i == self.y_first:
                            L.eng.wait_ge(self.x_split.sem, KD + k + 1)
                        o = ps[:, i % 8, 0:TL]
                        pe.matmul(o, high_part[:, k, :], moving[:, 0, k, :], start=k == 0, stop=False)
                        pe.matmul(o, high_part[:, k, :], moving[:, 1, k, :], start=False, stop=False)
                        mm = pe.matmul(o, low_part[:, k, :], moving[:, 0, k, :], start=False, stop=k == KD - 1)
                    L.inc(mm, self.tiles)
                end(L, "pe")

            def act(self, L):
                act = L.eng
                begin(L, "act")
                for i in range(CONV_AHEAD, UNITS):
                    self.round_weights(L, i)
                for i in range(4 * KD):
                    part, t = i // 4, i % 4
                    if i < self.y_first and part % 3 == 0:
                        if part:
                            L.eng.wait_ge(self.kept.sem, t + 1)
                        L.eng.wait_ge(self.tiles.sem, i + 1)
                        L.inc(act.copy(CG[:, t, :], ps[:, i % 8, 0:TL]), self.gate_in)
                    if i + UNITS < 4 * KD:
                        self.round_weights(L, i + UNITS)
                    if i < self.y_first and part % 3 == 2:
                        m = 4 * (part // 3) + t
                        L.eng.wait_ge(self.kept.sem, 8 * (part // 3) + 4 + t + 1)
                        L.inc(act.copy(CONV_BS[:, 0, m, :], BZ[:, m, :]), self.x_high)
                end(L, "act")

            def dve(self, L):
                v = L.eng
                begin(L, "dve")
                taps = vcol("conv", 3 * KD).rearrange("p (j m) -> p j m", j=3)
                L.inc(v.memset(CU[:, :, 0:1], 0.0))
                L.inc(v.memset(CU[:, :, TL + 1:TL + 2], 0.0))
                for i in range(CONV_AHEAD, UNITS):
                    self.split_weights(L, i)

                def split_gated(m):
                    L.eng.wait_ge(self.x_high.sem, KD + m + 1)
                    L.inc(v.tensor_tensor(CONV_BS[:, 1, m, :], BZ[:, m, :], high(CONV_BS[:, 0, m, :]), ALU.subtract), self.x_split)

                for i in range(4 * KD):
                    part, t = i // 4, i % 4
                    m, kind = 4 * (part // 3) + t, part % 3 if i < self.y_first else None
                    if kind == 1:
                        L.eng.wait_ge(self.gate_in.sem, m + 1)
                        L.eng.wait_ge(self.tiles.sem, i + 1)
                        L.inc(v.tensor_tensor(CU[:, t, 1:TL + 1], CG[:, t, :], ps[:, i % 8, 0:TL], ALU.mult), self.kept)
                    if kind == 2:
                        L.eng.wait_ge(self.tiles.sem, i + 1)
                        L.inc(v.tensor_tensor(BZ[:, m, :], CZ[:, t, :], ps[:, i % 8, 0:TL], ALU.mult), self.kept)
                    if i >= self.y_first:
                        gated_tile(L, 1, 0, TL, self.tiles, i + 1, i % 8, i - self.y_first)
                    if i + UNITS < 4 * KD:
                        self.split_weights(L, i + UNITS)
                    if kind == 1:
                        L.join()
                        L.inc(v.tensor_scalar(CZ[:, t, :], CU[:, t, 0:TL], taps[:, 0, m:m + 1], None, ALU.mult))
                        for j in (1, 2):
                            L.join()
                            L.inc(v.scalar_tensor_tensor(out=CZ[:, t, :], in0=CU[:, t, j:j + TL], scalar=taps[:, j, m:m + 1],
                                                         in1=CZ[:, t, :], op0=ALU.mult, op1=ALU.add))
                        L.join()
                    if kind == 2 and t:
                        split_gated(m - 1)
                    if kind == 2 and t == 3:
                        split_gated(m)
                end(L, "dve")

        take = carver()
        heads_at = arena_at
        H0 = take((AH + AKV + RH) * TL)

        def inside(at, heads):
            return H0[0:HD, at:at + heads * TL].rearrange("p (h t) -> p h t", h=heads)
        QA, KA, QT = inside(0, AH), inside(AH * TL, AKV), inside((AH + AKV) * TL, RH)
        LN_TILES = arena[:, 0:KD * TA].rearrange("p (k t) -> p k t", k=KD)
        KR = take(RH * TL)[0:HD].rearrange("p (h t) -> p h t", h=RH)
        VA = take(2 * P).rearrange("p (t c) -> p t c", t=2)
        VR = take(2 * 512).rearrange("p (t c) -> p t c", t=2)
        GR = take(4 * TL).rearrange("p (m t) -> p m t", m=4)
        RAW = [take(TL) for _ in range(2)]
        R1, R2 = take(TL), take(TL)
        SC = [take(3 * P) for _ in range(2)]
        PT = [take(3 * P) for _ in range(2)]
        SM = [take(16) for _ in range(2)]
        HS = place("HS", [P, 2, FFT, TL], F32R, heads_at)
        YS = place("YS", [P, KD, 2, TL], F32R, heads_at)
        XS = place("XS", [P, 2, KD, TL], F32R, A_at)
        WS = place("WS", [P, 2, UNITS, UNIT], F32R, ring_at + 4 * RING_2 * SLOT)
        SA = [take(TL) for _ in range(2)]
        HF = [take(TL) for _ in range(2)]
        MIXC = take(4 * TL + 3 * P + 3 * P + P + RH * TL)
        Y = A[:, 0:4, :].rearrange("p k t -> p (k t)").rearrange("p (m t) -> p m t", m=KD)
        O4 = A[:, 4:6, :].rearrange("p k t -> p (k t)").rearrange("p (m t) -> p m t", m=4)
        O2 = A[:, 6:8, :].rearrange("p k t -> p (k t)").rearrange("p (m t) -> p m t", m=4)
        COS_A, SIN_A, COS_R, SIN_R = (MIXC[:, i * TL:(i + 1) * TL] for i in range(4))
        TURN_A, TURN_R, HEAD_MEAN = (MIXC[:, 4 * TL + i * P:4 * TL + (i + 1) * P] for i in range(3))
        MASK = MIXC[:, 4 * TL + 3 * P:4 * TL + 6 * P]
        MEAN = MIXC[:, 4 * TL + 6 * P:4 * TL + 7 * P]
        DECAY = MIXC[:, 4 * TL + 7 * P:].rearrange("p (h t) -> p h t", h=RH)
        LNP = sb("LNP", [P, 6 * KD + AH])
        SINK = LNP[:, 6 * KD:]

        class Ffn:

            def __init__(self, ln, use, gu, dn):
                self.ln, self.gu, self.dn = ln, gu, dn
                self.w_high = shared("split_high", FFN_UNITS)
                self.w_split = shared("split_ready", FFN_UNITS)
                self.w_used = shared("split_used", FFN_UNITS)
                for signal in (self.w_high, self.w_split, self.w_used):
                    signal.per_turn = SPLITS_PER_LAYER
                self.x_split = stream_split(2 * use, 1)[1]
                self.silu = shared("ffn_silu", FFT, 2)
                self.hidden = shared("ffn_hidden", FFT, 2)
                self.h_high = shared("ffn_h_high", FFT, 2)
                self.h_split = shared("ffn_h_split", FFT, 2)
                self.y_added = shared("ffn_y_added", KD, 2)

            def plan(self, l):
                gu = w[self.gu][l].rearrange("(k p) (a n) -> p k a n", p=P, a=2)
                first = len(loads)
                for s in range(FFT // 2):
                    plan(gu[:, :, :, 2 * P * s:2 * P * (s + 1)], (KD, 2, 2 * P), (self.w_split, 4 * s + 4, l))
                for m in range(KD):
                    plan(columns(w[self.dn][l], P * m, P * (m + 1)), (FFT, P), (self.w_split, 2 * FFT + 3 * m + 3, l))
                if l == 0:
                    self.first = first

            def unit(self, u):
                if u < 2 * FFT:
                    f, a = u // 2, u % 2
                    n = self.first + f // 2
                    wv = slot(n).rearrange("p (k a n) -> p k a n", k=KD, a=2)
                    return n, wv[:, :, a, f % 2 * P:(f % 2 + 1) * P], range(KD)
                m, third = (u - 2 * FFT) // 3, (u - 2 * FFT) % 3
                n = self.first + FFT // 2 + m
                tiles = range(KD * third, min(KD * (third + 1), FFT))
                wv = slot(n)[:, 0:FFT * P].rearrange("p (k n) -> p k n", k=FFT)
                return n, wv[:, tiles.start:tiles.stop, :], tiles

            def parts(self, u):
                count = len(self.unit(u)[2])
                return [WS[:, j, u % UNITS, 0:count * P].rearrange("p (k n) -> p k n", k=count) for j in range(2)]

            def units_used(self, L, count):
                L.wait(self.w_used, count + UNITS)

            def round_weights(self, L, u, later=0):
                n, source, _ = self.unit(u)
                slot_ready(L, n, later)
                self.units_used(L, u + 1 - UNITS + later * SPLITS_PER_LAYER)
                L.inc(L.eng.copy(self.parts(u)[0], source), self.w_high)

            def split_weights(self, L, u, later=0):
                wh, wl = self.parts(u)
                L.wait(self.w_high, u + 1 + later * SPLITS_PER_LAYER)
                L.inc(L.eng.tensor_tensor(wl, self.unit(u)[1], high(wh), ALU.subtract), self.w_split)

            def pe(self, L):
                def products(u, out_ap, moving):
                    L.wait(self.w_split, u + 1)
                    wh, wl = self.parts(u)
                    tiles = self.unit(u)[2]
                    total = KD if u < 2 * FFT else FFT
                    for i, k in enumerate(tiles):
                        if u < 2:
                            L.wait(self.x_split, k + 1)
                        elif 2 * FFT <= u < 2 * FFT + 3:
                            L.wait(self.h_split, k + 1)
                        for weights, j in ((wh, 0), (wh, 1), (wl, 0)):
                            mm = L.eng.matmul(out_ap, weights[:, i, :], moving[:, j, k, :], start=k == 0 and weights is wh and j == 0,
                                              stop=k == total - 1 and weights is wl)
                    L.inc(mm, self.w_used)

                for f in range(FFT):
                    if f >= 2:
                        L.wait(self.hidden, f - 1)
                    for a in range(2):
                        products(2 * f + a, ps[:, 2 * (f % 2) + a, 0:TL], XS)
                for m in range(KD):
                    if m >= 2:
                        L.wait(self.y_added, m - 1)
                    for third in range(3):
                        products(2 * FFT + 3 * m + third, ps[:, 4 + m % 2, 0:TL], HS)
                    if m >= 1:
                        self.ln.mean_tile(L, self.y_added, m - 1)
                self.ln.mean_tile(L, self.y_added, KD - 1)
                end(L, "pe")

            def act(self, L):
                act = L.eng

                def round_weights(u):
                    if u < FFN_UNITS:
                        self.round_weights(L, u)

                for f in range(FFT):
                    round_weights(UNITS + 2 * f)
                    self.units_used(L, 2 * f + 1)
                    if f >= 2:
                        L.wait(self.hidden, f - 1)
                    L.inc(act.activation(SA[f % 2], ps[:, 2 * (f % 2), 0:TL], ACT.Silu), self.silu)
                    round_weights(UNITS + 2 * f + 1)
                    L.wait(self.hidden, f + 1)
                    L.inc(act.copy(HS[:, 0, f, :], HF[f % 2]), self.h_high)
                for u in range(UNITS + 2 * FFT, FFN_UNITS):
                    round_weights(u)
                stage, later = self.next
                for u in range(UNITS):
                    stage.round_weights(L, u, later)
                end(L, "act")

            def dve(self, L):
                v = L.eng

                def split_weights(u):
                    if u < FFN_UNITS:
                        self.split_weights(L, u)

                for f in range(FFT):
                    split_weights(UNITS + 2 * f)
                    L.wait(self.silu, f + 1)
                    self.units_used(L, 2 * f + 2)
                    if f >= 2:
                        L.wait(self.h_split, f - 1)
                    L.inc(v.tensor_tensor(HF[f % 2], SA[f % 2], ps[:, 2 * (f % 2) + 1, 0:TL], ALU.mult), self.hidden)
                    split_weights(UNITS + 2 * f + 1)
                    L.wait(self.h_high, f + 1)
                    L.inc(v.tensor_tensor(HS[:, 1, f, :], HF[f % 2], high(HS[:, 0, f, :]), ALU.subtract), self.h_split)
                stage, later = self.next
                for m in range(KD):
                    for third in range(3):
                        split_weights(2 * FFT + UNITS + 3 * m + third)
                    if m >= KD - 2:
                        stage.split_weights(L, m - (KD - 2), later)
                    self.units_used(L, 2 * FFT + 3 * m + 3)
                    L.inc(v.scalar_tensor_tensor(out=XT[:, m, 0:TL], in0=ps[:, 4 + m % 2, 0:TL], scalar=0.5 / ALPHA,
                                                 in1=XT[:, m, 0:TL], op0=ALU.mult, op1=ALU.add), self.y_added)
                for u in range(2, UNITS - 1):
                    stage.split_weights(L, u, later)
                end(L, "dve")

        VALUE_UNIT, GATE_UNIT, Y_UNIT = 12, 16, 20

        class Mixer:

            ROTATED = ([("qa", t) for t in range(4)] + [("ka", 0)] + [("qr", t) for t in range(4)] + [("kr", t) for t in range(4)])

            def __init__(self, ln):
                self.ln = ln
                self.w_high = shared("split_high", MIXER_UNITS)
                self.w_split = shared("split_ready", MIXER_UNITS)
                self.w_used = shared("split_used", MIXER_UNITS)
                for signal in (self.w_high, self.w_split, self.w_used):
                    signal.per_turn = SPLITS_PER_LAYER
                self.x_split = stream_split(1, 1)[1]
                self.key_tile = sig("mix_key_tile", 1)
                self.raw = sig("mix_raw", 13)
                self.turned = sig("mix_turned", 13)
                self.rotated = sig("mix_rotated", 13)
                self.values = sig("mix_values", 3)
                self.values_kept = sig("mix_values_kept", 4)
                self.gates_kept = sig("mix_gates_kept", 4)
                self.scores = sig("mix_scores", AH)
                self.neg = sig("mix_neg", AH)
                self.exps = sig("mix_exps", 3 * AH)
                self.probs = sig("mix_probs", AH)
                self.p_turned = sig("mix_p_turned", AH)
                self.p_kept = sig("mix_p_kept", AH)
                self.outs = sig("mix_outs", AH)
                self.outs_kept = sig("mix_outs_kept", AH)
                self.r_scores = sig("mix_r_scores", RH)
                self.decayed = sig("mix_decayed", RH)
                self.r_outs = sig("mix_r_outs", RH)
                self.r_outs_kept = sig("mix_r_outs_kept", RH)
                self.means = sig("mix_means", 4)
                self.centred = sig("mix_centred", 4)
                self.squares = sig("mix_squares", 4)
                self.vars = sig("mix_vars", 4)
                self.var = sig("mix_var", 4)
                self.std = sig("mix_std", 4)
                self.y_ready = sig("mix_y_ready", 4)
                self.y_high = sig("mix_y_high", KD)
                self.y_split = sig("mix_y_split", KD)
                self.y_added = sig("mix_y_added", KD)

            def plan(self, l):
                first = len(loads)
                win = w["w_in_2"][l]
                for c0, c1, freed in ((0, 512, (self.w_split, 4, l)), (512, 768, (self.values, 2, l)),
                                      (768, 1280, (self.w_split, 8, l)), (1280, 1792, (self.w_split, 12, l)),
                                      (1792, 2304, (self.w_split, 16, l)), (2304, 2816, (self.w_split, 20, l))):
                    plan(columns(win, c0, c1), (KD, c1 - c0), freed)
                for i in range(4):
                    plan(columns(w["w_out_2"][l], 256 * i, 256 * (i + 1)), (KD, 256), (self.w_split, Y_UNIT + 2 * i + 2, l))
                if l == 0:
                    self.first = first

            def unit_of(self, i):
                return None if i == 4 else i if i < 4 else i - 1

            def weights(self, j, width):
                return slot(self.first + j)[:, 0:KD * width].rearrange("p (k n) -> p k n", k=KD)

            def unit(self, u):
                if u >= Y_UNIT:
                    j, t = 6 + (u - Y_UNIT) // 2, (u - Y_UNIT) % 2
                    return self.first + j, self.weights(j, 256)[:, :, t * P:(t + 1) * P]
                j, t = (0, 2, 3, 4, 5)[u // 4], u % 4
                wv = self.weights(j, 512)
                return self.first + j, wv[:, 2 * t:2 * t + 2, :] if j == 4 else wv[:, :, t * P:(t + 1) * P]

            def parts(self, u):
                count = 2 if VALUE_UNIT <= u < GATE_UNIT else KD
                return [WS[:, j, u % UNITS, :].rearrange("p (k n) -> p k n", k=count) for j in range(2)]

            def units_used(self, L, count):
                L.wait(self.w_used, count + UNITS)

            def round_weights(self, L, u, later=0):
                n, source = self.unit(u)
                slot_ready(L, n, later)
                self.units_used(L, u + 1 - UNITS + later * SPLITS_PER_LAYER)
                L.inc(L.eng.copy(self.parts(u)[0], source), self.w_high)

            def split_weights(self, L, u, later=0):
                high_part, low_part = self.parts(u)
                L.wait(self.w_high, u + 1 + later * SPLITS_PER_LAYER)
                L.inc(L.eng.tensor_tensor(low_part, self.unit(u)[1], high(high_part), ALU.subtract), self.w_split)

            def pe(self, L):
                pe = L.eng

                def products(u, out_ap, moving, tiles, ready=None):
                    L.wait(self.w_split, u + 1)
                    high_part, low_part = self.parts(u)
                    for k in tiles:
                        if ready:
                            L.wait(ready, k + 1)
                        for weights, x in ((high_part, 0), (high_part, 1), (low_part, 0)):
                            mm = pe.matmul(out_ap, weights[:, k, :], moving[k][x], start=k == 0 and x == 0 and weights is high_part,
                                           stop=k == KD - 1 and weights is low_part)
                    if tiles[-1] == KD - 1:
                        L.inc(mm, self.w_used)

                stream = [[XS[:, x, k, :] for x in range(2)] for k in range(KD)]

                def turn(i):
                    L.wait(self.raw, i + 1)
                    if i >= 2:
                        L.wait(self.rotated, i - 1)
                    L.inc(pe.matmul(ps[:, 2 + i % 2, 0:TL], TURN_A if i < 5 else TURN_R, RAW[i % 2], start=True, stop=True), self.turned)

                def window_values(wv):
                    for t in range(2):
                        for k in range(KD):
                            mm = pe.matmul(ps[:, 4 + t, 0:P], XT[:, k, t * P:(t + 1) * P], wv[:, k, :], start=k == 0, stop=k == KD - 1)
                        L.inc(mm, self.values)

                def retention_values():
                    for q in range(4):
                        u = VALUE_UNIT + q
                        L.wait(self.w_split, u + 1)
                        high_part, low_part = self.parts(u)
                        for t in range(2):
                            for i in range(2):
                                k = 2 * q + i
                                for weights, x in ((high_part, 0), (high_part, 1), (low_part, 0)):
                                    mm = pe.matmul(ps[:, 4 + t, :], XS[:, x, k, t * P:(t + 1) * P], weights[:, i, :],
                                                   start=k == 0 and x == 0 and weights is high_part,
                                                   stop=k == KD - 1 and weights is low_part)
                            if t == 0 and q == 3:
                                L.inc(mm, self.values)
                        L.inc(mm, self.w_used)

                for i, (part, t) in enumerate(self.ROTATED):
                    j = {"qa": 0, "ka": 1, "qr": 2, "kr": 3}[part]
                    if i >= 2:
                        L.wait(self.raw, i - 1)
                    if part == "ka":
                        slot_ready(L, self.first + j)
                        wv = self.weights(j, 256)
                        for k in range(KD):
                            mm = pe.matmul(ps[:, i % 2, 0:TL], wv[:, k, 0:P], XT[:, k, 0:TL], start=k == 0, stop=k == KD - 1)
                        L.inc(mm, self.key_tile)
                    else:
                        products(self.unit_of(i), ps[:, i % 2, 0:TL], stream, range(KD), self.x_split if i == 0 else None)
                    if i:
                        turn(i - 1)
                    if part == "ka":
                        window_values(wv[:, :, P:2 * P])
                turn(12)
                L.wait(self.values_kept, 2)
                retention_values()
                L.wait(self.raw, 13)
                for t in range(4):
                    if t >= 2:
                        L.wait(self.gates_kept, t - 1)
                    products(GATE_UNIT + t, ps[:, t % 2, 0:TL], stream, range(KD))

                def scores(h):
                    b = h % 2
                    if h >= 2:
                        L.wait(self.neg, h - 1)
                    pe.matmul(ps[:, b, 0:P], QA[:, h, 0:P], KA[:, h // 4, 0:P], start=True, stop=True)
                    L.inc(pe.matmul(ps[:, b, P:3 * P], QA[:, h, P:TL], KA[:, h // 4, :], start=True, stop=True), self.scores)

                def turn_probs(h):
                    b = h % 2
                    L.wait(self.probs, h + 1)
                    if h >= 2:
                        L.wait(self.p_kept, h - 1)
                    for c in range(3):
                        mm = pe.transpose(ps[:, 2 + b, c * P:(c + 1) * P], SC[b][:, c * P:(c + 1) * P], IDENT)
                    L.inc(mm, self.p_turned)

                def finish(h):
                    b = h % 2
                    L.wait(self.p_kept, h + 1)
                    if h >= 2:
                        L.wait(self.outs_kept, h - 1)
                    kv = slice(h // 4 * HD, (h // 4 + 1) * HD)
                    pe.matmul(ps[0:HD, 4 + b, 0:P], VA[:, 0, kv], PT[b][:, 0:P], start=True, stop=True)
                    for c in range(2):
                        mm = pe.matmul(ps[0:HD, 4 + b, P:TL], VA[:, c, kv], PT[b][:, (1 + c) * P:(2 + c) * P], start=c == 0, stop=c == 1)
                    L.inc(mm, self.outs)

                L.wait(self.rotated, 13)
                L.wait(self.values_kept, 4)
                L.wait(self.gates_kept, 4)
                scores(0)
                scores(1)
                for h in range(AH):
                    if h + 2 < AH:
                        scores(h + 2)
                    turn_probs(h)
                    finish(h)

                def r_scores(h):
                    b = h % 2
                    if h >= 2:
                        L.wait(self.decayed, h - 1)
                    pe.matmul(ps[:, b, 0:TL], KR[:, h, 0:P], QT[:, h, :], start=True, stop=True)
                    L.inc(pe.matmul(ps[:, b, TL:3 * P], KR[:, h, P:TL], QT[:, h, P:TL], start=True, stop=True), self.r_scores)

                def r_finish(h):
                    b = h % 2
                    L.wait(self.decayed, h + 1)
                    if h >= 2:
                        L.wait(self.r_outs_kept, h - 1)
                    e = slice(h * HD, (h + 1) * HD)
                    pe.matmul(ps[0:HD, 2 + b, 0:P], VR[:, 0, e], SC[b][:, 0:P], start=True, stop=True)
                    pe.matmul(ps[0:HD, 2 + b, P:TL], VR[:, 0, e], SC[b][:, P:TL], start=True, stop=False)
                    L.inc(pe.matmul(ps[0:HD, 2 + b, P:TL], VR[:, 1, e], SC[b][:, TL:3 * P], start=False, stop=True), self.r_outs)

                L.wait(self.outs_kept, AH)
                r_scores(0)
                for h in range(1, RH):
                    r_scores(h)
                    r_finish(h - 1)
                r_finish(RH - 1)
                for m in range(4):
                    L.wait(self.r_outs_kept, 2 * m + 2)
                    if m >= 2:
                        L.wait(self.centred, m - 1)
                    L.inc(pe.matmul(ps[:, 4 + m % 2, (m // 2) * TL:(m // 2 + 1) * TL], HEAD_MEAN, O4[:, m, :], start=True, stop=True), self.means)
                def y_tile(m, tiles):
                    products(Y_UNIT + m, ps[:, 2 + m % 4, 0:TL], gated, tiles, self.y_split if m < 4 else None)

                gated = [[YS[:, k, x, :] for x in range(2)] for k in range(KD)]
                for m in range(2):
                    y_tile(m, range(4))
                L.wait(self.decayed, RH)
                for m in range(4):
                    L.wait(self.squares, m + 1)
                    if m >= 2:
                        L.wait(self.var, m - 1)
                    L.inc(pe.matmul(ps[:, m % 2, (m // 2) * TL:(m // 2 + 1) * TL], HEAD_MEAN, O2[:, m, :], start=True, stop=True), self.vars)
                for m in range(2, 4):
                    y_tile(m, range(4))
                for k in range(4, KD):
                    for m in range(4):
                        y_tile(m, range(k, k + 1))
                for m, added in zip(range(4, KD), ((0, 1), (2, 3), (4,), (5, 6))):
                    L.wait(self.y_added, m - 3)
                    y_tile(m, range(KD))
                    for k in added:
                        self.ln.mean_tile(L, self.y_added, k)
                self.ln.mean_tile(L, self.y_added, KD - 1)
                end(L, "pe")

            def act(self, L):
                act = L.eng
                begin(L, "act")
                for i, (part, t) in enumerate(self.ROTATED):
                    u = self.unit_of(i)
                    if u is None:
                        L.wait(self.key_tile, 1)
                    else:
                        self.units_used(L, u + 1)
                    if i >= 2:
                        L.wait(self.rotated, i - 1)
                    scale = HD ** -0.5 if part in ("qa", "kr") else 1.0
                    L.inc(act.activation(RAW[i % 2], ps[:, i % 2, 0:TL], ACT.Copy, scale=scale), self.raw)
                    if u is not None:
                        self.round_weights(L, u + UNITS)
                    if part == "qr" and t == 0:
                        for t2 in range(2):
                            L.wait(self.values, t2 + 1)
                            L.inc(act.copy(VA[:, t2, :], ps[:, 4 + t2, 0:P]), self.values_kept)
                for q in range(4):
                    self.round_weights(L, GATE_UNIT + q)
                L.wait(self.values, 3)
                for t in range(2):
                    L.inc(act.copy(VR[:, t, :], ps[:, 4 + t, :]), self.values_kept)
                for t in range(4):
                    self.units_used(L, GATE_UNIT + t + 1)
                    L.inc(act.activation(GR[:, t, :], ps[:, t % 2, 0:TL], ACT.Silu), self.gates_kept)
                    if t < 3:
                        self.round_weights(L, Y_UNIT + t)

                def keep_out(h, source, tile, signal):
                    half = slice(h % 2 * HD, (h % 2 + 1) * HD)
                    L.inc(act.copy(tile[half, h // 2, :], source), signal)

                for h in range(AH):
                    b = h % 2
                    L.wait(self.neg, h + 1)
                    for c, cols in enumerate((slice(0, P), slice(P, 3 * P))):
                        L.inc(act.activation(SC[b][:, cols], SC[b][:, cols], ACT.Exp, bias=SM[b][:, 4 + c:5 + c],
                                             accum_out=SM[b][:, 6 + c:7 + c]), self.exps)
                    L.inc(act.activation(SM[b][:, 8:10], SM[b][:, 4:6], ACT.Exp, bias=SINK[:, h:h + 1]), self.exps)
                    if h:
                        L.wait(self.outs, h)
                        keep_out(h - 1, ps[0:HD, 4 + (h - 1) % 2, 0:TL], Y, self.outs_kept)
                    L.wait(self.p_turned, h + 1)
                    L.inc(act.copy(PT[b], ps[:, 2 + b, 0:3 * P]), self.p_kept)
                L.wait(self.outs, AH)
                keep_out(AH - 1, ps[0:HD, 4 + (AH - 1) % 2, 0:TL], Y, self.outs_kept)

                def round_gated(k):
                    L.inc(act.copy(YS[:, k, 0, :], Y[:, k, :]), self.y_high)

                for h in range(RH):
                    L.wait(self.r_outs, h + 1)
                    keep_out(h, ps[0:HD, 2 + h % 2, 0:TL], O4, self.r_outs_kept)
                    if h == 0:
                        self.round_weights(L, Y_UNIT + 3)
                    if 1 <= h < 5:
                        round_gated(h - 1)
                for m in range(4):
                    L.wait(self.centred, m + 1)
                    L.inc(act.activation(O2[:, m, :], O4[:, m, :], ACT.Square), self.squares)
                for m in range(4):
                    L.wait(self.var, m + 1)
                    L.inc(act.activation(O2[:, m, :], O2[:, m, :], ACT.Sqrt), self.std)
                for m in range(4):
                    L.wait(self.y_ready, m + 1)
                    round_gated(4 + m)
                for m in range(4, KD):
                    self.round_weights(L, Y_UNIT + m)
                for u in range(UNITS):
                    ffns[1].round_weights(L, u)
                end(L, "act")

            def dve(self, L):
                v = L.eng
                begin(L, "dve")
                v.wait_ge(mix_in.sem, 16)
                for i, (part, t) in enumerate(self.ROTATED):
                    cos, sin = (COS_A, SIN_A) if i < 5 else (COS_R, SIN_R)
                    L.wait(self.raw, i + 1)
                    L.inc(v.tensor_tensor(R1, RAW[i % 2], cos, ALU.mult))
                    L.wait(self.turned, i + 1)
                    L.inc(v.tensor_tensor(R2, ps[:, 2 + i % 2, 0:TL], sin, ALU.mult))
                    L.join()
                    to = {"qa": QA, "ka": KA, "qr": QT, "kr": KR}[part]
                    L.inc(v.tensor_tensor(to[:, 2 * t, :], R1[0:HD], R2[0:HD], ALU.add))
                    L.inc(v.tensor_tensor(to[:, 2 * t + 1, :], R1[HD:P], R2[HD:P], ALU.add), self.rotated)
                    L.join()
                    if i != 4:
                        self.split_weights(L, self.unit_of(i) + UNITS)
                for u in range(GATE_UNIT, Y_UNIT + 3):
                    self.split_weights(L, u)

                def mask_scores(h):
                    b = h % 2
                    L.wait(self.scores, h + 1)
                    if h >= 2:
                        L.wait(self.p_turned, h - 1)
                    L.inc(v.tensor_tensor(SC[b], ps[:, b, 0:3 * P], MASK, ALU.add))
                    L.join()
                    L.inc(v.tensor_reduce(SM[b][:, 0:1], SC[b][:, 0:P], X, ALU.max))
                    L.inc(v.tensor_reduce(SM[b][:, 1:2], SC[b][:, P:3 * P], X, ALU.max))
                    L.join()
                    L.inc(v.tensor_scalar(SM[b][:, 4:6], SM[b][:, 0:2], SINK[:, h:h + 1], -1.0, ALU.max, ALU.mult), self.neg)

                mask_scores(0)
                for h in range(AH):
                    b = h % 2
                    if h + 1 < AH:
                        mask_scores(h + 1)
                    L.wait(self.exps, 3 * h + 3)
                    L.inc(v.tensor_tensor(SM[b][:, 10:12], SM[b][:, 6:8], SM[b][:, 8:10], ALU.add))
                    L.join()
                    L.inc(v.reciprocal(SM[b][:, 12:14], SM[b][:, 10:12]))
                    L.join()
                    L.inc(v.tensor_scalar(SC[b][:, 0:P], SC[b][:, 0:P], SM[b][:, 12:13], None, ALU.mult))
                    L.inc(v.tensor_scalar(SC[b][:, P:3 * P], SC[b][:, P:3 * P], SM[b][:, 13:14], None, ALU.mult), self.probs)

                def split_gated(k):
                    L.wait(self.y_high, k + 1)
                    L.inc(v.tensor_tensor(YS[:, k, 1, :], Y[:, k, :], high(YS[:, k, 0, :]), ALU.subtract), self.y_split)

                for h in range(RH):
                    b = h % 2
                    L.wait(self.r_scores, h + 1)
                    if h >= 2:
                        L.wait(self.r_outs, h - 1)
                    L.inc(v.tensor_tensor(SC[b][:, 0:TL], ps[:, b, 0:TL], DECAY[:, h, :], ALU.mult))
                    L.inc(v.tensor_tensor(SC[b][:, TL:3 * P], ps[:, b, TL:3 * P], DECAY[:, h, 0:P], ALU.mult), self.decayed)
                    if h == 2:
                        self.split_weights(L, Y_UNIT + 3)
                    if h >= 4:
                        split_gated(h - 4)

                def half_bank(m, bank):
                    return ps[:, bank + m % 2, (m // 2) * TL:(m // 2 + 1) * TL]
                for m in range(4):
                    L.wait(self.means, m + 1)
                    L.inc(v.tensor_tensor(O4[:, m, :], O4[:, m, :], half_bank(m, 4), ALU.subtract), self.centred)
                for m in range(4):
                    L.wait(self.squares, m + 1)
                    L.inc(v.tensor_tensor(O4[:, m, :], O4[:, m, :], GR[:, m, :], ALU.mult))
                for m in range(4):
                    L.wait(self.vars, m + 1)
                    L.inc(v.tensor_scalar(O2[:, m, :], half_bank(m, 0), GN_EPS, None, ALU.add), self.var)
                for m in range(4):
                    L.wait(self.std, m + 1)
                    L.inc(v.reciprocal(O2[:, m, :], O2[:, m, :]))
                    L.join()
                    L.inc(v.tensor_tensor(Y[:, 4 + m, :], O4[:, m, :], O2[:, m, :], ALU.mult), self.y_ready)
                    if m:
                        split_gated(4 + m - 1)
                split_gated(KD - 1)
                for m in range(KD):
                    self.units_used(L, Y_UNIT + m + 1)
                    L.inc(v.scalar_tensor_tensor(out=XT[:, m, 0:TL], in0=ps[:, 2 + m % 4, 0:TL], scalar=1.0 / ALPHA,
                                                 in1=XT[:, m, 0:TL], op0=ALU.mult, op1=ALU.add), self.y_added)
                    if m < KD - UNITS:
                        self.split_weights(L, Y_UNIT + UNITS + m)
                    else:
                        ffns[1].split_weights(L, m - (KD - UNITS))
                end(L, "dve")

        mods = [None, None]
        mods[0] = Mod(0)
        norms = [Norm("norm0", 0, 0, TA), Norm("norm1", 0, 1, TA), Norm("norm2", 1, 0, TL), Norm("norm3", 1, 1, TL),
                 Norm("norm4", 1, 2, TL)]
        mla = Mla()
        moes = [None, None]
        mods[1] = Mod(1)
        moes[0] = Moe(0, TA, norms[1])
        conv = Conv()
        moes[1] = Moe(1, TL, norms[3])
        layer_first = len(loads)
        second_stack.append(layer_first)
        lns = [LayerNorm(i) for i in range(3)]
        ffns = [Ffn(lns[0], 0, "ffn1_w_gu_2", "ffn1_w_down_2")]
        mixer = Mixer(lns[1])
        ffns.append(Ffn(lns[2], 1, "ffn2_w_gu_2", "ffn2_w_down_2"))
        ffns[0].next = lns[0].next = (mixer, 0)
        lns[1].next = None
        ffns[1].next = lns[2].next = (ffns[0], 1)
        for l in range(LAYERS):
            before_layer = [s.n for s in slot_in]
            ffns[0].plan(l)
            mixer.plan(l)
            ffns[1].plan(l)
            for s, count in zip(slot_in, before_layer):
                s.per_turn = s.n - count
        assert (len(loads) - layer_first) % (RING_2 * LAYERS) == 0
        gu = w["ffn1_w_gu_2"][0].rearrange("(k p) (a n) -> p k a n", p=P, a=2)
        plan(gu[:, :, :, 0:2 * P], (KD, 2, 2 * P), (ffns[0].w_split, 4, LAYERS))
        first_stack = [mods[0], norms[0], mla, mods[1], norms[1], moes[0], norms[2], conv, norms[3], moes[1], norms[4]]
        layer = [ffns[0], lns[0], mixer, lns[1], ffns[1], lns[2]]
        assert len(layer) == PER_LAYER_STAGES

        block = ctx.enter_context(nc.Block())

        @block.sync
        def _(sp):
            sp.dma_start(VECS[:, :], vec).then_inc(const_in.sem, 16)
            sp.dma_start(BASE[:, :], base_c).then_inc(const_in.sem, 16)

            def load(n):
                if before[n] is not None and frees[before[n]][1]:
                    sp.wait_ge(*frees[before[n]])
                for dst, src in loads[n]:
                    sp.dma_start(dst, src).then_inc(slot_in[place_of[n]].sem, 16)

            n = 0
            while n < len(loads):
                moe = next((m for m in moes if m.first == n - RING), None)
                if moe is None:
                    load(n)
                    n += 1
                    if n == RING:
                        sp.dma_start(XT[:, :, :], xT).then_inc(x_in.sem, 16)
                        sp.dma_start(MLAC, mla_c).then_inc(mla_in.sem, 16)
                    continue
                sp.wait_ge(moe.table_kept.sem, moe.table_kept.base + 1)

                def units_before(e):
                    return sp.value_load(moe.UNITS_BEFOREI[0:1, bass.ds(e, 1)], min_val=0, max_val=moe.NB * BLOCK_UNITS)

                with sp.Fori(0, EXPERTS // 2 - 1) as pair:
                    for a in range(2):
                        e = pair * 2 + (2 + a)
                        units = units_before(pair * 2 + (a + 1))
                        for j, name in enumerate(("moe_w_gate", "moe_w_up", "moe_w_down")):
                            sp.wait_ge(moe.w_split.sem, units + (j + 1) * UNITS)
                            dst = loads[n + 3 * a + j][0][0]
                            src = w[name][moe.l][bass.ds(e, 1)].rearrange("o (k p) n -> p (o k) n", p=P)
                            sp.dma_start(dst, src).then_inc(slot_in[place_of[n + 3 * a + j]].sem, 16)
                sp.wait_ge(moe.w_split.sem, units_before(EXPERTS - 1) + BLOCK_UNITS)
                sp.sem_inc(spare.sem, 1)
                n += 3 * EXPERTS - RING
            sp.wait_ge(stages_done.sem, 3 * (len(first_stack) + 1 + LAYERS * len(layer)))
            sp.dma_start(out, XT[:, :, 0:TL]).then_inc(const_in.sem, 16)
            sp.wait_ge(const_in.sem, 48)

        @block.gpsimd
        def _(pool):
            L = Lane(pool, line["pool"], spare)
            for m in moes:
                m.pool(L)

        @block.scalar
        def _(act):
            L = Lane(act, line["act"], spare)
            act.wait_ge(const_in.sem, 32)
            L.inc(act.activation(COND[:, :, :], vcol("cond", 2 * KD).rearrange("p (k a) -> p k a", a=2), ACT.Silu))
            L.join()
            L.inc(act.copy(COND_SPLIT[:, :, 0:2], COND[:, :, :]))
            end(L, "act")
            for s in first_stack:
                s.act(L)
            L.eng.wait_ge(stages_done.sem, 3 * counters["act"])
            act.dma_start(MIXC, mix_c).then_inc(mix_in.sem, 16)
            L.line, L.last = loop_line["act"], None
            with act.Fori(0, LAYERS) as l:
                L.turn = l
                for s in layer:
                    s.act(L)
            assert loop_line["act"].n == ACT_PER_LAYER, loop_line["act"].n

        @block.tensor
        def _(pe):
            L = Lane(pe, line["pe"], spare)
            pe.sem_inc(ffns[0].w_used.sem, UNITS)
            end(L, "pe")
            for s in first_stack:
                s.pe(L)
            with pe.Fori(0, LAYERS) as l:
                L.turn = l
                for s in layer:
                    s.pe(L)

        @block.vector
        def _(dve):
            L = Lane(dve, line["dve"], spare)
            dve.wait_ge(const_in.sem, 32)
            L.inc(dve.tensor_tensor(FOLD[:, :], IDENT[0:4, 0:2], IDENT[0:4, 2:4], ALU.add))
            dve.wait_ge(line["act"].sem, 2)
            L.inc(dve.tensor_tensor(COND_SPLIT[:, :, 2:4], COND[:, :, :], high(COND_SPLIT[:, :, 0:2]), ALU.subtract))
            end(L, "dve")
            for s in first_stack:
                s.dve(L)
            L.line, L.last = loop_line["dve"], None
            with dve.Fori(0, LAYERS) as l:
                L.turn = l
                dve.wait_ge(stages_done.sem, l * (3 * PER_LAYER_STAGES) + 3 * counters["dve"])
                L.settle()
                L.inc(dve.tensor_copy(LNP[:, 0:6 * KD], VECS[:, bass.ds(l * (6 * KD) + VEC["ln"], 6 * KD)]))
                L.inc(dve.tensor_copy(SINK, VECS[:, bass.ds(l * AH + VEC["sinks"], AH)]))
                L.join()
                for s in layer:
                    s.dve(L)
            assert loop_line["dve"].n == DVE_PER_LAYER, loop_line["dve"].n


WEIGHTS = ["w_mod", "mla_w_dq", "mla_w_uq", "mla_w_dkv", "mla_w_ukv", "mla_w_o", "conv_w_in", "conv_w_out",
           "moe_w_gate", "moe_w_up", "moe_w_down", "w_in_2", "w_out_2",
           "ffn1_w_gu_2", "ffn1_w_down_2", "ffn2_w_gu_2", "ffn2_w_down_2"]


def lay_out(inputs):
    def features(a):
        a = np.asarray(a)
        a = a.reshape(-1, a.shape[-1] // P, P)
        return a.transpose(2, 0, 1).reshape(P, -1)

    def everywhere(a):
        return np.broadcast_to(np.asarray(a).reshape(1, -1), (P, np.asarray(a).size))

    a = {k: np.asarray(v) for k, v in inputs.items()}
    tokens = np.concatenate([a["x"][0], a["ctx"][0]], axis=0)
    xT = np.ascontiguousarray(tokens.T.reshape(KD, P, TA).transpose(1, 0, 2))
    cond = np.stack([a["c"][0], a["c_ctx"]], axis=1).reshape(KD, P, 2).transpose(1, 0, 2).reshape(P, -1)
    ln = np.stack([a[f"ln{i}_{s}_2"] for i in (1, 2, 3) for s in "gb"], axis=1)
    router = np.concatenate([a["moe_w_group"], a["moe_w_expert"]], axis=2).reshape(2, KD, P, 36)
    parts = {
        "cond": cond, "b_mod": features(a["b_mod"]), "norm_mix": features(a["norm_mix_g"]),
        "norm_ffn": features(a["norm_ffn_g"]), "final": features(a["final_norm_g"]), "g_q": features(a["mla_g_q"]),
        "g_kv": features(a["mla_g_kv"]), "conv": features(a["conv_w"][0]), "ln": features(ln),
        "router": router.transpose(2, 0, 1, 3).reshape(P, -1),
        "router_bias": everywhere(np.concatenate([a["moe_b_group"], a["moe_b_expert"]], axis=1)),
        "sinks": everywhere(a["attn_sinks_2"]),
    }
    return xT, np.ascontiguousarray(np.concatenate([parts[name] for name in VEC], axis=1))


def kernel(**inputs):
    import concourse.bacc as bacc
    from concourse.bass_utils import run_bass_kernel_spmd as run

    nc = bacc.Bacc("TRN2", target_bir_lowering=False, num_devices=1)
    arrays = {}

    def given(name, a):
        arrays[name] = np.ascontiguousarray(a)
        return nc.dram_tensor(name, arrays[name].shape, mybir.dt.from_np(arrays[name].dtype), kind="ExternalInput").ap()

    xT, vec = lay_out(inputs)
    base_c, mla_c, mix_c = shape_constants()
    args = [given("in_tokens", xT), given("in_vectors", vec), given("in_base", base_c), given("in_mla", mla_c),
            given("in_mix", mix_c)]
    weights = {name: given("in_" + name, inputs[name]) for name in WEIGHTS}
    out = nc.dram_tensor("out_features", (P, KD, TL), F32, kind="ExternalOutput").ap()
    program(nc, *args, weights, out)
    r = run(nc, [arrays], core_ids=[0])
    got = np.asarray(r.results[0]["out_features"])
    return np.ascontiguousarray(got.transpose(2, 1, 0).reshape(1, TL, D))
```
